# Optimizing a Trainium2 kernel written in Bass

```python
import math
import jax
import jax.numpy as jnp
from jax import lax
import numpy as np

D_MODEL = 1024
BATCH = 1
SEQ = 512
DEPTH = 1

GRID_W = 64
CTX_LEN = 256
N_MIXERS = 2
RMS_EPS = 1e-6
HG_HEADS = 8
HG_KDIM = D_MODEL // HG_HEADS
HG_VDIM = D_MODEL // HG_HEADS
HG_CHUNK = 64
N_HG = (DEPTH + N_MIXERS - 1) // N_MIXERS
S5_GROUP = 16
S5_GROUPS = D_MODEL // S5_GROUP
S5_STATE = 64
S5_EIG_MAX = -1e-4
S5_DT_MIN = 1e-3
S5_DT_MAX = 1e-1
N_S5 = DEPTH // N_MIXERS
N_EXPERTS = 32
TOP_K = 4
D_FF = D_MODEL
SWIGLU_ALPHA = 1.702
SWIGLU_LIMIT = 7.0
MOE_BLOCK = 128

kernel_name = "hybrid_hgrn2_s5_moe_prefix_dit"

F32 = jnp.float32

def rmsnorm(x, g):
    xf = x.astype(F32)
    y = xf * lax.rsqrt(jnp.mean(xf * xf, axis=-1, keepdims=True) + RMS_EPS)
    return (y * g.astype(F32)).astype(x.dtype)

def modulate(h, shift, scale):
    return h * (1.0 + scale) + shift

def _ident(t):
    return t

def _flip_seq(t):
    return jnp.flip(t, axis=1)

def _flip0(t):
    return jnp.flip(t, axis=0)

def gla_chunked(q, k, v, log_f, s0):
    bsz, t_len, n_h, _ = q.shape
    vd = v.shape[-1]
    n = t_len // HG_CHUNK

    def chunks(t):
        return t.astype(F32).reshape(bsz, n, HG_CHUNK, n_h, t.shape[-1])

    q, k, v, log_f = chunks(q), chunks(k), chunks(v), chunks(log_f)
    b = jnp.cumsum(log_f, axis=2)
    b_ref = b[:, :, HG_CHUNK // 2 - 1:HG_CHUNK // 2]
    scores = jnp.einsum('bnthk,bnshk->bnhts', q * jnp.exp(b - b_ref), k * jnp.exp(b_ref - b))
    prefix = jnp.tril(jnp.ones((HG_CHUNK, HG_CHUNK), bool))
    o_intra = jnp.einsum('bnhts,bnshv->bnthv', jnp.where(prefix, scores, 0.0), v)
    b_last = b[:, :, -1]
    q_in = q * jnp.exp(b)
    k_out = k * jnp.exp(b_last[:, :, None] - b)

    def step(s, xs):
        qc, kc, vc, dc = xs
        o = jnp.einsum('bthk,bhkv->bthv', qc, s)
        s = s * jnp.exp(dc)[..., None] + jnp.einsum('bthk,bthv->bhkv', kc, vc)
        return s, o

    xs = tuple(jnp.moveaxis(t, 1, 0) for t in (q_in, k_out, v, b_last))
    s_fin, o_inter = lax.scan(step, s0.astype(F32), xs)
    o = o_intra + jnp.moveaxis(o_inter, 0, 1)
    return o.reshape(bsz, t_len, n_h, vd), s_fin

def hgrn2_mixer(a_ctx, a_lat, w_in, lb, norm_g, w_out, need_ctx):
    bsz = a_lat.shape[0]

    def heads(t):
        return t.reshape(t.shape[:-1] + (HG_HEADS, -1))

    def project(a):
        q, i, z_fwd, z_bwd, g = jnp.split(a @ w_in, 5, axis=-1)
        gates = []
        for d, z in enumerate((z_fwd, z_bwd)):
            f = lb[d] + (1.0 - lb[d]) * jax.nn.sigmoid(z.astype(F32))
            gates.append((heads(1.0 - f), heads(jnp.log(f))))
        return heads(jax.nn.silu(q)), heads(i), gates, g

    qc, vc, gates_c, gc = project(a_ctx)
    ql, vl, gates_l, gl = project(a_lat)
    s0 = jnp.zeros((bsz, HG_HEADS, HG_KDIM, HG_VDIM), F32)
    o_ctx = 0.0
    o_lat = 0.0
    for d, rev in enumerate((_ident, _flip_seq)):
        (kc, lfc), (kl, lfl) = gates_c[d], gates_l[d]
        oc, s_ctx = gla_chunked(rev(qc), rev(kc), rev(vc), rev(lfc), s0)
        ol, _ = gla_chunked(rev(ql), rev(kl), rev(vl), rev(lfl), s_ctx)
        o_lat = o_lat + rev(ol)
        if need_ctx:
            o_ctx = o_ctx + rev(oc)

    def readout(o, g):
        o = o * lax.rsqrt(jnp.mean(o * o, axis=-1, keepdims=True) + RMS_EPS)
        o = o * norm_g.astype(F32).reshape(HG_HEADS, HG_VDIM)
        o = o.reshape(o.shape[:2] + (D_MODEL,)).astype(g.dtype) * jax.nn.silu(g)
        return o @ w_out

    y_ctx = readout(o_ctx, gc) if need_ctx else None
    return y_ctx, readout(o_lat, gl)

def s5_discretise(a_re, a_im, log_dt, b_re, b_im):
    lam_re = jnp.minimum(a_re.astype(F32), S5_EIG_MAX)
    lam_im = a_im.astype(F32)
    dt = jnp.exp(log_dt.astype(F32))[:, None]
    mag = jnp.exp(lam_re * dt)
    ab_re = mag * jnp.cos(lam_im * dt)
    ab_im = mag * jnp.sin(lam_im * dt)
    den = lam_re * lam_re + lam_im * lam_im
    coef_re = ((ab_re - 1.0) * lam_re + ab_im * lam_im) / den
    coef_im = (ab_im * lam_re - (ab_re - 1.0) * lam_im) / den
    b_re = b_re.astype(F32)
    b_im = b_im.astype(F32)
    bb_re = coef_re[..., None] * b_re - coef_im[..., None] * b_im
    bb_im = coef_re[..., None] * b_im + coef_im[..., None] * b_re
    return ab_re, ab_im, bb_re, bb_im

def _cmul(ar, ai, br, bi):
    return ar * br - ai * bi, ar * bi + ai * br

def _lin_rec_op(e1, e2):
    a1r, a1i, b1r, b1i = e1
    a2r, a2i, b2r, b2i = e2
    ar, ai = _cmul(a2r, a2i, a1r, a1i)
    br, bi = _cmul(a2r, a2i, b1r, b1i)
    return ar, ai, br + b2r, bi + b2i

def complex_diag_scan(ab_re, ab_im, bu_re, bu_im, s0_re, s0_im):
    i_re, i_im = _cmul(ab_re, ab_im, s0_re, s0_im)
    bu_re = bu_re.at[0].add(i_re)
    bu_im = bu_im.at[0].add(i_im)
    a_re = jnp.broadcast_to(ab_re, bu_re.shape)
    a_im = jnp.broadcast_to(ab_im, bu_im.shape)
    _, _, s_re, s_im = lax.associative_scan(_lin_rec_op, (a_re, a_im, bu_re, bu_im), axis=0)
    return s_re, s_im

def s5_mixer(a_ctx, a_lat, a_re, a_im, log_dt, b_re, b_im, c_re, c_im, d_skip, w_glu, b_glu, need_ctx):
    bsz, t_len, _ = a_lat.shape
    rows = t_len // GRID_W
    to_cols = lambda t: t.reshape(bsz, rows, GRID_W, D_MODEL).transpose(0, 2, 1, 3).reshape(bsz, t_len, D_MODEL)
    to_rows = lambda t: t.reshape(bsz, GRID_W, rows, D_MODEL).transpose(0, 2, 1, 3).reshape(bsz, t_len, D_MODEL)
    u_lat = to_cols(a_lat)
    disc = [s5_discretise(a_re[d], a_im[d], log_dt[d], b_re, b_im) for d in range(2)]
    cr = c_re.astype(F32)
    ci = c_im.astype(F32)

    def per_sample(args):
        uc, ul = args
        ucg = uc.astype(F32).reshape(-1, S5_GROUPS, S5_GROUP)
        ulg = ul.astype(F32).reshape(-1, S5_GROUPS, S5_GROUP)
        zero = jnp.zeros((S5_GROUPS, S5_STATE), F32)
        yc = 0.0
        yl = 0.0
        for d, rev in enumerate((_ident, _flip0)):
            ab_re, ab_im, bb_re, bb_im = disc[d]
            drive = lambda u: (jnp.einsum('tgi,gpi->tgp', u, bb_re), jnp.einsum('tgi,gpi->tgp', u, bb_im))
            read = lambda s: jnp.einsum('tgp,gop->tgo', s[0], cr[d]) - jnp.einsum('tgp,gop->tgo', s[1], ci[d])
            sc = complex_diag_scan(ab_re, ab_im, *drive(rev(ucg)), zero, zero)
            sl = complex_diag_scan(ab_re, ab_im, *drive(rev(ulg)), sc[0][-1], sc[1][-1])
            yl = yl + rev(read(sl))
            if need_ctx:
                yc = yc + rev(read(sc))
        yl = yl.reshape(ul.shape)
        if need_ctx:
            return yc.reshape(uc.shape), yl
        return yl

    out = lax.map(per_sample, (a_ctx, u_lat))
    dsk = d_skip.astype(F32)

    def glu(y, u):
        y = (y + dsk * u.astype(F32)).astype(u.dtype)
        za, zb = jnp.split(jax.nn.gelu(y) @ w_glu + b_glu, 2, axis=-1)
        return za * jax.nn.sigmoid(zb)

    if need_ctx:
        y_ctx_raw, y_lat_raw = out
        return glu(y_ctx_raw, a_ctx), glu(to_rows(y_lat_raw), a_lat)
    return None, glu(to_rows(out), a_lat)

def moe(h, router_w, router_b, w1, b1, w2, b2):
    n_tok, d = h.shape
    logits = (h @ router_w + router_b).astype(F32)
    top_v, top_i = lax.top_k(logits, TOP_K)
    top_w = jax.nn.softmax(top_v, axis=-1)
    n_asg = n_tok * TOP_K
    flat_e = top_i.reshape(-1)
    flat_t = jnp.arange(n_asg, dtype=jnp.int32) // TOP_K
    flat_w = top_w.reshape(-1)
    order = jnp.argsort(flat_e)
    e_sorted = flat_e[order]
    counts = jnp.bincount(flat_e, length=N_EXPERTS)
    padded = (counts + MOE_BLOCK - 1) // MOE_BLOCK * MOE_BLOCK
    pad_end = jnp.cumsum(padded)
    pad_start = pad_end - padded
    start = jnp.cumsum(counts) - counts
    dest = pad_start[e_sorted] + jnp.arange(n_asg, dtype=jnp.int32) - start[e_sorted]
    n_blocks = -(-n_asg // MOE_BLOCK) + N_EXPERTS
    slot_tok = jnp.zeros((n_blocks * MOE_BLOCK,), jnp.int32).at[dest].set(flat_t[order])
    slot_w = jnp.zeros((n_blocks * MOE_BLOCK,), F32).at[dest].set(flat_w[order])
    block_pos = jnp.arange(n_blocks, dtype=jnp.int32) * MOE_BLOCK
    block_e = jnp.minimum(jnp.searchsorted(pad_end, block_pos, side='right'), N_EXPERTS - 1)

    def block_ffn(args):
        tok, e = args
        z = h[tok] @ w1[e] + b1[e]
        z_glu, z_lin = jnp.split(z, 2, axis=-1)
        z_glu = jnp.minimum(z_glu, SWIGLU_LIMIT)
        z_lin = jnp.clip(z_lin, -SWIGLU_LIMIT, SWIGLU_LIMIT)
        act = z_glu * jax.nn.sigmoid(SWIGLU_ALPHA * z_glu) * (z_lin + 1.0)
        return act @ w2[e] + b2[e]

    y = lax.map(block_ffn, (slot_tok.reshape(n_blocks, MOE_BLOCK), block_e))
    y = y.reshape(-1, d) * slot_w[:, None].astype(h.dtype)
    return jnp.zeros_like(h).at[slot_tok].add(y)

def setup_inputs(seed: int = 0) -> dict:
    key = jax.random.key(seed)
    keys = iter(jax.random.split(key, 40))

    def normal(shape, scale):
        return jax.random.normal(next(keys), shape, F32) * scale

    def gain(shape):
        return 1.0 + normal(shape, 0.02)

    d, g, p, gc = D_MODEL, S5_GROUPS, S5_STATE, S5_GROUP
    n_idx = jnp.arange(p, dtype=F32)
    return {
        "x": normal((BATCH, SEQ, d), 1.0),
        "c": normal((BATCH, d), 1.0),
        "ctx": normal((BATCH, CTX_LEN, d), 1.0),
        "c_ctx": normal((d,), 1.0),
        "mod_w": normal((DEPTH, d, 6 * d), d ** -0.5),
        "mod_b": normal((DEPTH, 6 * d), 0.02),
        "norm1_g": gain((DEPTH, d)),
        "norm2_g": gain((DEPTH, d)),
        "hg_w_in": normal((N_HG, d, 5 * d), d ** -0.5),
        "hg_lb_logits": normal((N_HG + 1, 2, d), 0.1),
        "hg_norm_g": gain((N_HG, d)),
        "hg_w_out": normal((N_HG, d, d), d ** -0.5),
        "s5_a_re": -0.5 + normal((N_S5, 2, g, p), 0.01),
        "s5_a_im": math.pi * n_idx + normal((N_S5, 2, g, p), 0.01),
        "s5_log_dt": jax.random.uniform(next(keys), (N_S5, 2, g), F32, math.log(S5_DT_MIN), math.log(S5_DT_MAX)),
        "s5_b_re": normal((N_S5, g, p, gc), (2 * gc) ** -0.5),
        "s5_b_im": normal((N_S5, g, p, gc), (2 * gc) ** -0.5),
        "s5_c_re": normal((N_S5, 2, g, gc, p), p ** -0.5),
        "s5_c_im": normal((N_S5, 2, g, gc, p), p ** -0.5),
        "s5_d": normal((N_S5, d), 1.0),
        "s5_w_glu": normal((N_S5, d, 2 * d), d ** -0.5),
        "s5_b_glu": normal((N_S5, 2 * d), 0.02),
        "router_w": normal((DEPTH, d, N_EXPERTS), d ** -0.5),
        "router_b": normal((DEPTH, N_EXPERTS), 0.01),
        "moe_w1": normal((DEPTH, N_EXPERTS, d, 2 * D_FF), d ** -0.5),
        "moe_b1": normal((DEPTH, N_EXPERTS, 2 * D_FF), 0.02),
        "moe_w2": normal((DEPTH, N_EXPERTS, D_FF, d), D_FF ** -0.5),
        "moe_b2": normal((DEPTH, N_EXPERTS, d), 0.02),
        "final_g": gain((d,)),
    }

def reference(x, c, ctx, c_ctx, mod_w, mod_b, norm1_g, norm2_g, hg_w_in, hg_lb_logits, hg_norm_g,
              hg_w_out, s5_a_re, s5_a_im, s5_log_dt, s5_b_re, s5_b_im, s5_c_re, s5_c_im, s5_d, s5_w_glu,
              s5_b_glu, router_w, router_b, moe_w1, moe_b1, moe_w2, moe_b2, final_g):
    d = x.shape[-1]
    lb_all = jnp.cumsum(jax.nn.softmax(hg_lb_logits.astype(F32), axis=0), axis=0)
    h_lat, h_ctx = x, ctx
    for i in range(DEPTH):
        last = i == DEPTH - 1
        j = i // N_MIXERS
        m_lat = (jax.nn.silu(c) @ mod_w[i] + mod_b[i])[:, None, :]
        m_ctx = jax.nn.silu(c_ctx) @ mod_w[i] + mod_b[i]
        sh1, sc1, g1, sh2, sc2, g2 = jnp.split(m_lat, 6, axis=-1)
        csh1, csc1, cg1, csh2, csc2, cg2 = jnp.split(m_ctx, 6, axis=-1)
        a_lat = modulate(rmsnorm(h_lat, norm1_g[i]), sh1, sc1)
        a_ctx = modulate(rmsnorm(h_ctx, norm1_g[i]), csh1, csc1)
        if i % N_MIXERS == 0:
            y_ctx, y_lat = hgrn2_mixer(a_ctx, a_lat, hg_w_in[j], lb_all[j], hg_norm_g[j], hg_w_out[j], not last)
        else:
            y_ctx, y_lat = s5_mixer(a_ctx, a_lat, s5_a_re[j], s5_a_im[j], s5_log_dt[j], s5_b_re[j], s5_b_im[j],
                                    s5_c_re[j], s5_c_im[j], s5_d[j], s5_w_glu[j], s5_b_glu[j], not last)
        h_lat = h_lat + g1 * y_lat
        f_lat = modulate(rmsnorm(h_lat, norm2_g[i]), sh2, sc2)
        if last:
            y = moe(f_lat.reshape(-1, d), router_w[i], router_b[i], moe_w1[i], moe_b1[i], moe_w2[i], moe_b2[i])
            h_lat = h_lat + g2 * y.reshape(h_lat.shape)
        else:
            h_ctx = h_ctx + cg1 * y_ctx
            f_ctx = modulate(rmsnorm(h_ctx, norm2_g[i]), csh2, csc2)
            tokens = jnp.concatenate([f_ctx.reshape(-1, d), f_lat.reshape(-1, d)], axis=0)
            y = moe(tokens, router_w[i], router_b[i], moe_w1[i], moe_b1[i], moe_w2[i], moe_b2[i])
            n_ctx = h_ctx.shape[0] * h_ctx.shape[1]
            h_ctx = h_ctx + cg2 * y[:n_ctx].reshape(h_ctx.shape)
            h_lat = h_lat + g2 * y[n_ctx:].reshape(h_lat.shape)
    return rmsnorm(h_lat, final_g)


_drawn_inputs = setup_inputs


def setup_inputs(seed=0):
    import zlib

    import numpy as np

    out = dict(_drawn_inputs(seed))
    spreads = {}
    factors = {'ctx': 3.467,
     'hg_lb_logits': 5.943,
     'router_b': 2.955,
     'moe_b1': 6.654,
     'moe_b2': 8.0,
     'final_g': 2.726}
    for name, (base, spread) in spreads.items():
        noise = np.random.default_rng([zlib.crc32(name.encode()), seed]).standard_normal(out[name].shape)
        drawn = base * np.exp(spread * noise) if base else spread * noise
        out[name] = jnp.asarray(drawn.astype(out[name].dtype))
    for name, factor in factors.items():
        out[name] = (out[name] * factor).astype(out[name].dtype)
    return out
```

```python
import numpy as np
import concourse.bass as bass
from concourse import mybir
from contextlib import ExitStack

F32 = mybir.dt.float32
BF16 = mybir.dt.bfloat16
I32 = mybir.dt.int32
U32 = mybir.dt.uint32
ALU = mybir.AluOpType
ACT = mybir.ActivationFunctionType
AX_X = mybir.AxisListType.X

P = 128
D = 1024
DK = D // P
LAT, CTX = 512, 256
TOK = LAT + CTX
LT, CT, TT = LAT // P, CTX // P, TOK // P
CH = 64
NCH = LAT // CH
E, TOPK = 32, 4
FF = 1024
NB_MAX = LAT * TOPK // P + E
NBT = NB_MAX + 2
EPS = 1e-6
H = DK


class Steps:

    def __init__(self, engine, sem):
        self.engine, self.sem, self.count, self.base = engine, sem, 0, 0

    def mark(self, ins):
        ins.then_inc(self.sem, 1)
        self.count += 1
        return self.count

    def wait(self, count=None):
        self.engine.wait_ge(self.sem, self.base + (self.count if count is None else count))

    def link(self, ins):
        self.mark(ins)
        self.wait()


def build(nc, x, c, ctx_in, c_ctx, mod_w, mod_b, norm1_g, norm2_g, hg_w_in, hg_lb_logits, hg_norm_g,
          hg_w_out, router_w, router_b, moe_w1, moe_b1, moe_w2, moe_b2, final_g, out):
    yrows = nc.dram_tensor("yrows", [TOPK * LAT, D], F32, kind="Internal").ap()
    with ExitStack() as stack:
        def sb(name, shape, dt=F32):
            return stack.enter_context(nc.sbuf_tensor(name, shape, dt))

        def sem(name):
            return stack.enter_context(nc.semaphore(name))

        arena = sb("arena", [P, 24576])
        x_sb = sb("x_sb", [P, LT, D])
        aT_t = sb("aT_t", [P, DK * TOK])
        xv_t = sb("xv_t", [P, TT * D])
        ring_t = sb("ring_t", [P, 4096])
        ogT = sb("ogT", [P, DK, LAT])
        rows2 = sb("rows2", [P, 2 * D])
        g2_row, fin_row = rows2[:, 0:D], rows2[:, D:2 * D]

        mwc = arena[:, 0:16384].rearrange("p (k n) -> p k n", k=DK)
        w_sq = arena[:, 16384:24576].rearrange("p (k n) -> p k n", k=DK)
        aT = aT_t[:, :].rearrange("p (k t) -> p k t", k=DK)
        f_sb = aT_t[:, 0:LT * D].rearrange("p (i n) -> p i n", i=LT)
        xv = xv_t[:, :].rearrange("p (i n) -> p i n", i=TT)
        wh = ring_t[:, :].rearrange("p (s k n) -> p s k n", s=4, k=DK)

        at = [0]

        def take(n):
            at[0] += n
            return arena[:, at[0] - n:at[0]]

        sgk = [take(TOK) for _ in range(2)]
        lfq = [take(TOK) for _ in range(2)]
        bc = [take(TOK) for _ in range(2)]
        qe = [take(LAT) for _ in range(2)]
        ke = [take(LAT) for _ in range(2)]
        ko = [take(TOK) for _ in range(2)]
        qs, sgq, sgg, gs = (take(LAT) for _ in range(4))
        pm = [take(LAT).rearrange("p (a t) -> p a t", a=LT) for _ in range(2)]
        st = [take(NCH * P).rearrange("p (c v) -> p c v", c=NCH) for _ in range(2)]
        koT = [take(TOK).rearrange("p (i k) -> p i k", i=TT) for _ in range(2)]
        v_h = take(TOK).rearrange("p (i v) -> p i v", i=TT)
        assert at[0] <= 16384
        osb, sq = rows2[:, 0:LAT], rows2[:, LAT:2 * LAT]

        g1_row, sh2_row, G2_row, n2_row = (arena[:, i * D:(i + 1) * D] for i in range(4))
        mb_rows = arena[:, 4096:8192]
        mwr = [ring_t[:, :], arena[:, 8192:12288], arena[:, 12288:16384]]

        cols = sb("cols", [P, 112])
        csil = sb("csil", [P, DK, 2])
        csb = xv_t[:, 0:D].rearrange("p (k m) -> p k m", k=DK)
        sc16 = sb("sc16", [P, 16])
        modc = sb("modc", [P, 16, 2])
        G1 = sb("G1", [P, DK, 2])
        stat = sb("stat", [P, 16])
        rst = sb("rst", [P, 16])
        eps_t = sb("eps_t", [P, 1])
        hcols = sb("hcols", [P, H, 8])
        hc = sb("hc", [P, 8])
        ed = sb("ed", [P, 2, NCH])
        ident = sb("ident", [P, P])
        ones = sb("ones", [P, P])
        tri = sb("tri", [P, P])
        res = sb("res", [P, 2, TOK], BF16)
        mk = sb("mk", [P, 2, LT, CH], mybir.dt.uint8)
        mkf = xv_t[:, 2048:2048 + 512].rearrange("p (d a t) -> p d a t", d=2, a=LT)

        rw = sb("rw", [P, DK, E])
        rb_row = sb("rb_row", [P, E])
        at2 = [0]

        def rtake(n):
            at2[0] += n
            return ring_t[:, at2[0] - n:at2[0]]

        lg = rtake(LT * E).rearrange("p (i e) -> p i e", i=LT)
        v8 = rtake(LT * 8).rearrange("p (i e) -> p i e", i=LT)
        i8 = rtake(LT * 8).rearrange("p (i e) -> p i e", i=LT).bitcast(U32)
        i8f = rtake(LT * 8).rearrange("p (i e) -> p i e", i=LT)
        oh = rtake(LT * TOPK * E).rearrange("p (i k e) -> p i k e", i=LT, k=TOPK)
        ohd = rtake(LT * TOPK * E).rearrange("p (i k e) -> p i k e", i=LT, k=TOPK)
        msk = rtake(LT * E).rearrange("p (i e) -> p i e", i=LT)
        io_e = rtake(E)
        ew4 = rtake(LT * TOPK).rearrange("p (i k) -> p i k", i=LT)
        es = rtake(LT)
        cnt, nblk, nb1, cum, pst, onesE = (rtake(E) for _ in range(6))
        io_b = rtake(NBT * E).rearrange("p (b e) -> p b e", e=E)
        assert at2[0] <= 4096
        rid = sb("rid", [P, LT, E])
        rid_e = sb("rid_e", [P, LT])
        tokf = sb("tokf", [P, LT * TOPK])
        idx_f = sb("idx_f", [P, 1])
        idx_next, idx_cur, zero_i, zero_j = (sb(n, [P, 1], U32) for n in ("idx_next", "idx_cur", "zero_i", "zero_j"))
        wk = sb("wk", [P, LT, TOPK])
        dm = sb("dm", [P, LT, E])
        bef = sb("bef", [1, NBT])
        tab_e = sb("tab_e", [1, NBT], I32)
        tab_new = sb("tab_new", [1, NBT], I32)
        tab_nf = sb("tab_nf", [1, NBT])
        tab_n = sb("tab_n", [1, 1], I32)
        bias_sb = ogT[0:1, 1:7, :].rearrange("p a n -> p (a n)")
        slot_io = sb("slot_io", [P, P])
        pt = ogT[:, 0, :].rearrange("p (i s) -> p i s", i=LT)

        w1s = arena[:, 0:16384].rearrange("p (k n) -> p k n", k=DK)
        w2s = arena[:, 16384:24576].rearrange("p (k n) -> p k n", k=DK)
        XT = xv_t[:, 0:1024].rearrange("p (k s) -> p k s", k=DK)
        actT = xv_t[:, 1024:2048].rearrange("p (k s) -> p k s", k=DK)
        act_a, y_sb, glu_g, glu_s = (xv_t[:, 2048 + i * 1024:3072 + i * 1024] for i in range(4))
        ygat = arena[:, 0:16384].rearrange("p (i k n) -> p i k n", i=LT, k=TOPK)

        ps = [stack.enter_context(nc.psum_tensor(f"ps{i}", [P, 512], F32)) for i in range(8)]

        names = """lbx_ok lbe_ok dve_gla dve_ew fin_s ld_vec ld_x ld_ctx ld_wv ld_wout ld_rw ld_rows ld_mb consts pool_s dve_s act_s
        vecs_ps cols_ok c_sig csil_ok modc_ps modc_ok sumsq_ok stdev_ok xn_ok xT_ps aT_lat_ok aT_ctx_ok
        v_ps v_ev_a v_ev_d
        zc_ps zf_ps zb_ps q_ps g_ps a_ps b_ps o_ps ss_ps
        zc_sig zf_sig zb_sig q_sig g_sig qs_ok gs_ok koT_ok pm_ok st_ok o_ev sq_ok rs_ok og_ok
        hc_ok lnf_ok b_ok bm_ok bo_ok exp_ok ew_ok
        rows_ok csb_ok mwr_used yo_ps h_ok sumsq2_ok stdev2_ok f_ok fT_ps fT_ok lg_ps lg_ok
        e_v_ok e_w_ok msk_ok pos_ps tab_ok wk_ok
        pt_ok xt_ps xt_ok z_ps gmin_ok sig_ok act_ok at_ps at_ok y_ok y_st y_free w1_used w2_used ld_b z_free
        idx_ok idxc_ok xi_ps arena_free fin_sq fin_std fin_ok out_st""".split()
        S = {n: sem(n) for n in names}
        ld_mw = sem("ld_mw")
        ld_wh = [sem(f"ld_wh{s}") for s in range(4)]
        sec_done = [S["zf_ps"], S["zb_ps"], S["q_ps"], S["g_ps"]]
        ld_mwr = [sem(f"ld_mwr{s}") for s in range(3)]
        gath = [sem(f"gath{i}") for i in range(LT)]
        ld_w1 = [sem(f"ld_w1_{k}") for k in range(DK)]
        ld_w2 = [sem(f"ld_w2_{k}") for k in range(4)]

        block = stack.enter_context(nc.Block())
        vecs = ring_t[0:112, 0:P]
        SEC = [2, 3, 0, 4]

        w_in_s = hg_w_in.rearrange("(k p) n -> p k n", p=P)

        def vrow(v):
            return v.rearrange("(j p) -> j p", p=P)

        @block.sync
        def _(sp):
            row = 0
            for v in (c[0], c_ctx, mod_b, norm1_g, hg_lb_logits[0, 0], hg_lb_logits[0, 1],
                      hg_lb_logits[1, 0], hg_lb_logits[1, 1], hg_norm_g):
                n = v.shape[0] // P
                sp.dma_start(ring_t[row:row + n, 0:P], vrow(v)).then_inc(S["ld_vec"], 16)
                row += n
            assert row == 112
            sp.dma_start(x_sb[:, :, :], x.rearrange("(i p) n -> p i n", p=P)).then_inc(S["ld_x"], 16)
            sp.dma_start(xv[:, 0:CT, :], ctx_in.rearrange("(i p) n -> p i n", p=P)).then_inc(S["ld_ctx"], 16)
            for k in range(DK):
                sp.dma_start(mwc[:, k, :], mod_w[k * P:(k + 1) * P, 0:2 * D]).then_inc(ld_mw, 16)
            for k in range(DK):
                sp.dma_start(w_sq[:, k, :], hg_w_in[k * P:(k + 1) * P, D:2 * D]).then_inc(S["ld_wv"], 16)
            sp.dma_start(rw[:, :, :], router_w.rearrange("(k p) e -> p k e", p=P)).then_inc(S["ld_rw"], 16)
            sp.dma_start(rb_row[:, :], router_b.partition_broadcast(P)).then_inc(S["ld_rw"], 16)

            sp.wait_ge(S["vecs_ps"], 1)
            for s in range(4):
                sp.dma_start(wh[:, s], w_in_s[:, :, SEC[s] * D:SEC[s] * D + P]).then_inc(ld_wh[s], 16)
            sp.wait_ge(S["v_ps"], 2 * TT)
            for k in range(DK):
                sp.dma_start(w_sq[:, k, :], hg_w_out[k * P:(k + 1) * P, :]).then_inc(S["ld_wout"], 16)
            with sp.Fori(1, H) as h:
                for s in range(4):
                    sp.wait_ge(sec_done[s], h)
                    sp.dma_start(wh[:, s], w_in_s[:, :, bass.ds((h - 1) * P + (SEC[s] * D + P), P)]).then_inc(ld_wh[s], 16)
            for k in range(DK):
                if k == 0:
                    for s in range(4):
                        sp.wait_ge(sec_done[s], H)
                if k == 1:
                    sp.wait_ge(S["o_ps"], H)
                    sp.wait_ge(S["og_ok"], H)
                    sp.dma_start(mb_rows, mod_b[2 * D:6 * D].partition_broadcast(P)).then_inc(S["ld_mb"], 16)
                    sp.dma_start(n2_row, norm2_g.partition_broadcast(P)).then_inc(S["ld_mb"], 16)
                if k >= 3:
                    sp.wait_ge(S["mwr_used"], k - 2)
                sp.dma_start(mwr[k % 3], mod_w[k * P:(k + 1) * P, 2 * D:6 * D]).then_inc(ld_mwr[k % 3], 16)
            sp.dma_start(fin_row, final_g.partition_broadcast(P)).then_inc(S["ld_rows"], 16)

            sp.wait_ge(S["arena_free"], 1)
            sp.wait_ge(S["tab_ok"], 1)
            n_blocks = sp.value_load(tab_n[0:1, 0:1], min_val=1, max_val=NB_MAX)

            def load_bias(e):
                sp.dma_start(bias_sb[0:1, 0:2 * FF], moe_b1[bass.ds(e, 1), :]).then_inc(S["ld_b"], 16)
                sp.dma_start(bias_sb[0:1, 2 * FF:3 * FF], moe_b2[bass.ds(e, 1), :]).then_inc(S["ld_b"], 16)

            def load_w1(e, k):
                sp.dma_start(w1s[:, k, :], moe_w1[bass.ds(e * D + k * P, P), :]).then_inc(ld_w1[k], 16)

            def load_w2(e, k):
                sp.dma_start(w2s[:, 2 * k:2 * k + 2, :],
                             moe_w2[bass.ds(e * FF + 2 * k * P, 2 * P), :].rearrange("(a p) n -> p a n", p=P)
                             ).then_inc(ld_w2[k], 16)

            e0 = sp.value_load(tab_e[0:1, 0:1], min_val=0, max_val=E - 1)
            load_bias(e0)
            for k in range(DK):
                load_w1(e0, k)
            for k in range(4):
                load_w2(e0, k)
            with sp.Fori(1, n_blocks) as b:
                e = sp.value_load(tab_e[0:1, bass.ds(b, 1)], min_val=0, max_val=E - 1)
                new = sp.value_load(tab_new[0:1, bass.ds(b, 1)], min_val=0, max_val=1)
                with sp.If(new):
                    for k in range(DK):
                        sp.wait_ge(S["w1_used"], b * DK + (k + 1 - DK))
                        load_w1(e, k)
                    for k in range(4):
                        sp.wait_ge(S["w2_used"], b * 4 + (k + 1 - 4))
                        load_w2(e, k)
                    load_bias(e)
                with sp.Else():
                    for k in range(DK):
                        sp.wait_ge(S["w1_used"], b * DK + (k + 1 - DK))
                        sp.sem_inc(ld_w1[k], 16)
                    for k in range(4):
                        sp.wait_ge(S["w2_used"], b * 4 + (k + 1 - 4))
                        sp.sem_inc(ld_w2[k], 16)
                    sp.sem_inc(S["ld_b"], 32)
            sp.wait_ge(S["y_st"], n_blocks * 16)
            for i in range(LT):
                sp.dma_start(ygat[:, i], yrows.rearrange("(k i p) n -> i p k n", k=TOPK, p=P)[i]
                             ).then_inc(gath[i], 16)
            for i in range(LT):
                sp.wait_ge(S["fin_ok"], i + 1)
                sp.dma_start(out[i * P:(i + 1) * P, :], x_sb[:, i, :]).then_inc(S["out_st"], 16)
            sp.wait_ge(S["out_st"], 16 * LT)

        @block.gpsimd
        def _(pool):
            me = Steps(pool, S["pool_s"])
            me.mark(pool.memset(ones[:, :], 1.0))
            me.mark(pool.memset(ident[:, :], 0.0))
            me.mark(pool.memset(mkf, 1.0))
            me.mark(pool.memset(res[:, :, :], 1.0))
            pool.memset(eps_t[:, :], EPS).then_inc(S["consts"], 1)
            me.wait()
            pool.affine_select(out=ident[:, :], in_=ident[:, :], compare_op=ALU.not_equal, fill=1.0, base=0,
                               pattern=[[-1, P]], channel_multiplier=1).then_inc(S["consts"], 1)
            pool.affine_select(out=tri[:, :], in_=ones[:, :], compare_op=ALU.is_gt, fill=0.0, base=0,
                               pattern=[[1, P]], channel_multiplier=-1).then_inc(S["consts"], 1)
            me.mark(pool.memset(res[:, 0, 0:1], 0.0))
            me.mark(pool.memset(res[:, 0, CTX:TOK:CH], 0.0))
            me.mark(pool.memset(res[:, 1, 0:LAT:CH], 0.0))
            me.mark(pool.memset(res[:, 1, LAT:LAT + 1], 0.0))
            me.wait()
            pool.wait_ge(S["consts"], 3)
            for half in range(2):
                r = slice(half * CH, (half + 1) * CH)
                me.link(pool.affine_select(out=mkf[r, 0], in_=mkf[r, 0], compare_op=ALU.is_ge, fill=0.0, base=0,
                                           pattern=[[0, LT], [1, CH]], channel_multiplier=-1))
                me.link(pool.affine_select(out=mkf[r, 1], in_=mkf[r, 1], compare_op=ALU.is_ge, fill=0.0, base=0,
                                           pattern=[[0, LT], [-1, CH]], channel_multiplier=1))
            me.wait()
            pool.tensor_copy(mk[:, :, :, :], mkf).then_inc(S["consts"], 1)
            pool.wait_ge(S["yo_ps"], 1)
            pool.iota(io_e, pattern=[[1, E]], base=0, channel_multiplier=0,
                      allow_small_or_imprecise_dtypes=True).then_inc(S["consts"], 1)
            pool.iota(io_b, pattern=[[1, NBT], [0, E]], base=0, channel_multiplier=0,
                      allow_small_or_imprecise_dtypes=True).then_inc(S["consts"], 1)
            pool.iota(slot_io[:, :], pattern=[[1, P]], base=0, channel_multiplier=0,
                      allow_small_or_imprecise_dtypes=True).then_inc(S["consts"], 1)
            pool.memset(onesE, 1.0).then_inc(S["consts"], 1)
            pool.iota(tokf[:, :].rearrange("p (i k) -> p i k", i=LT), pattern=[[P, LT], [LAT, TOPK]], base=1,
                      channel_multiplier=1, allow_small_or_imprecise_dtypes=True).then_inc(S["consts"], 1)
            pool.memset(zero_i[:, :], 0).then_inc(S["consts"], 1)
            pool.wait_ge(S["consts"], 10)
            pool.wait_ge(S["tab_ok"], 1)
            n_blocks = pool.value_load(tab_n[0:1, 0:1], min_val=1, max_val=NB_MAX)
            pool.sem_inc(S["y_free"], 1)
            with pool.Fori(0, n_blocks) as b:
                pool.wait_ge(S["idx_ok"], b + 1)
                pool.tensor_tensor(out=idx_cur[:, :], in0=idx_next[:, :], in1=zero_i[:, :],
                                   op=ALU.add).then_inc(S["idxc_ok"], 1)
                pool.wait_ge(S["y_ok"], b + 2)
                pool.wait_ge(S["idxc_ok"], b + 1)
                pool.tensor_tensor(out=zero_j[:, :], in0=zero_i[:, :], in1=zero_i[:, :], op=ALU.add)
                pool.indirect_dma_start(out=yrows, out_offset=bass.IndirectOffsetOnAxis(ap=idx_cur[:, :], axis=0),
                                        in_=y_sb, in_offset=None, bounds_check=TOPK * LAT - 1,
                                        oob_is_err=False).then_inc(S["y_st"], 16)
                pool.wait_ge(S["y_st"], b * 16 + 16)
                pool.sem_inc(S["y_free"], 1)

        @block.scalar
        def _(act):
            me = Steps(act, S["act_s"])
            A = nc.scalar.activation
            act.wait_ge(S["cols_ok"], 1)
            A(sc16[:, :], cols[:, 0:16], ACT.Sigmoid).then_inc(S["c_sig"], 1)
            act.wait_ge(S["lbx_ok"], 1)
            A(hcols[:, :, 2:6], hcols[:, :, 2:6], ACT.Exp).then_inc(S["lbe_ok"], 1)
            act.wait_ge(S["ld_x"], 16)
            act.wait_ge(S["ld_ctx"], 16)
            for i in range(TT):
                src = xv[:, i, :] if i < CT else x_sb[:, i - CT, :]
                if i:
                    me.wait()
                me.mark(A(ogT[:, 0:2, :], src.rearrange("p (a n) -> p a n", a=2), ACT.Square,
                          accum_out=stat[:, i:i + 1]))
            me.wait()
            act.wait_ge(S["consts"], 4)
            A(rst[:, 0:TT], stat[:, 0:TT], ACT.Sqrt, bias=eps_t[:, :], scale=1.0 / D).then_inc(S["stdev_ok"], 1)
            act.wait_ge(S["modc_ok"], 1)
            for j in range(DK):
                act.wait_ge(S["xT_ps"], 2 * j + 2)
                A(aT[:, j, 0:CTX], ps[5 + j % 3][:, 0:CTX], ACT.Identity, bias=modc[:, j, 1:2],
                  scale=G1[:, j, 1:2]).then_inc(S["aT_ctx_ok"], 1)
            for n in range(0, 2 * TT, 2):
                act.wait_ge(S["v_ps"], n + 1)
                A(xv[:, n // 2, 0:512], ps[n % 4][:, :], ACT.Copy).then_inc(S["v_ev_a"], 1)

            base = me.count
            per_head = 8

            def head(h, prev):
                me.base, me.count = base + per_head * h, 0
                act.wait_ge(S["zc_ps"], h + 1)
                if prev is not None:
                    act.wait_ge(S["ew_ok"], h)
                A(sgk[0][:, 0:CTX], ps[2][:, 0:CTX], ACT.Sigmoid)
                A(sgk[1][:, 0:CTX], ps[2][:, CTX:2 * CTX], ACT.Sigmoid).then_inc(S["zc_sig"], 1)
                act.wait_ge(S["zf_ps"], h + 1)
                A(sgk[0][:, CTX:TOK], ps[0][:, :], ACT.Sigmoid).then_inc(S["zf_sig"], 1)
                act.wait_ge(S["zb_ps"], h + 1)
                A(sgk[1][:, CTX:TOK], ps[1][:, :], ACT.Sigmoid).then_inc(S["zb_sig"], 1)
                if prev is not None:
                    evac_koT(h)
                act.wait_ge(S["q_ps"], h + 1)
                if prev is not None:
                    act.wait_ge(S["qs_ok"], h)
                A(sgq, ps[3][:, :], ACT.Sigmoid).then_inc(S["q_sig"], 1)
                act.wait_ge(S["g_ps"], h + 1)
                if prev is not None:
                    act.wait_ge(S["gs_ok"], h)
                A(sgg, ps[0][:, :], ACT.Sigmoid).then_inc(S["g_sig"], 1)
                if prev is not None:
                    readout(h)
                act.wait_ge(S["hc_ok"], h + 1)
                for d in range(2):
                    A(lfq[d], sgk[d], ACT.Ln, bias=hc[:, d:d + 1], scale=hc[:, 2 + d:3 + d]).then_inc(S["lnf_ok"], 1)
                for d in range(2):
                    act.wait_ge(S["b_ok"], 2 * h + (d + 1))
                    m1 = me.mark(A(lfq[d][:, CTX:TOK], bc[d][:, CTX:TOK], ACT.Exp))
                    last = bc[d][:, CTX + (CH - 1 if d == 0 else 0):TOK:CH]
                    me.mark(A(ed[:, d, :], last, ACT.Exp))
                    act.wait_ge(S["bm_ok"], 2 * h + (d + 1))
                    m2 = me.mark(A(ke[d], qe[d], ACT.Exp, scale=-1.0))
                    me.wait(m2)
                    A(qe[d], qe[d], ACT.Exp)
                    act.wait_ge(S["bo_ok"], 2 * h + (d + 1))
                    me.wait(m1)
                    me.mark(A(ko[d], ko[d], ACT.Exp))
                    me.wait()
                    act.sem_inc(S["exp_ok"], 1)
                assert me.count == per_head

            def evac_koT(h1):
                act.wait_ge(S["a_ps"], h1)
                A(koT[0][:, CT:TT, :], ps[5][:, :].rearrange("p (i k) -> p i k", i=LT), ACT.Copy)
                A(koT[0][:, 0:CT, :], ps[6][:, 0:CTX].rearrange("p (i k) -> p i k", i=CT), ACT.Copy)
                A(koT[1][:, CT:TT, :], ps[7][:, :].rearrange("p (i k) -> p i k", i=LT), ACT.Copy)
                A(koT[1][:, 0:CT, :], ps[6][:, CTX:2 * CTX].rearrange("p (i k) -> p i k", i=CT),
                  ACT.Copy).then_inc(S["koT_ok"], 1)

            def readout(h1):
                act.wait_ge(S["o_ps"], h1)
                A(osb, ps[5][:, :], ACT.Copy).then_inc(S["o_ev"], 1)
                A(sq, ps[5][:, :], ACT.Square).then_inc(S["sq_ok"], 1)
                act.wait_ge(S["ss_ps"], h1)
                act.wait_ge(S["sq_ok"], h1)
                A(sq, ps[6][:, :], ACT.Ln, bias=eps_t[:, :], scale=1.0 / P).then_inc(S["rs_ok"], 1)
                act.wait_ge(S["rs_ok"], 2 * h1)
                A(sq, sq, ACT.Exp, scale=-0.5).then_inc(S["rs_ok"], 1)

            act.sem_inc(S["rs_ok"], 1)
            head(0, None)
            with act.Fori(1, H) as h:
                head(h, 1)
            evac_koT(H)
            readout(H)

            me.base, me.count = base + per_head * H, 0
            for i in range(LT):
                act.wait_ge(S["h_ok"], i + 1)
                if i:
                    me.wait()
                me.mark(A(aT_t[:, 5120:6144], x_sb[:, i, :], ACT.Square, accum_out=stat[:, 8 + i:9 + i]))
            me.wait()
            A(rst[:, 8:12], stat[:, 8:12], ACT.Sqrt, bias=eps_t[:, :], scale=1.0 / D).then_inc(S["stdev2_ok"], 1)
            for j in range(1, DK, 2):
                act.wait_ge(S["fT_ps"], j + 1)
                A(ogT[:, j, :], ps[j][:, :], ACT.Copy).then_inc(S["fT_ok"], 1)
            act.wait_ge(S["e_v_ok"], 1)
            A(ew4, ew4, ACT.Exp).then_inc(S["e_w_ok"], 1)

            act.wait_ge(S["tab_ok"], 1)
            n_blocks = act.value_load(tab_n[0:1, 0:1], min_val=1, max_val=NB_MAX)

            def evac_xt(b1):
                act.wait_ge(S["xt_ps"], b1)
                A(XT[:, 0:4, :], ps[0][:, :].rearrange("p (k s) -> p k s", k=4), ACT.Copy)
                A(XT[:, 4:8, :], ps[1][:, :].rearrange("p (k s) -> p k s", k=4), ACT.Copy).then_inc(S["xt_ok"], 1)

            act.sem_inc(S["y_ok"], 1)
            evac_xt(1)
            with act.Fori(0, n_blocks) as b:
                act.wait_ge(S["gmin_ok"], b * 2 + 1)
                A(glu_s[:, 0:512], glu_g[:, 0:512], ACT.Sigmoid, scale=1.702).then_inc(S["sig_ok"], 1)
                act.wait_ge(S["gmin_ok"], b * 2 + 2)
                A(glu_s[:, 512:1024], glu_g[:, 512:1024], ACT.Sigmoid, scale=1.702).then_inc(S["sig_ok"], 1)
                evac_xt(b + 2)
                act.wait_ge(S["at_ps"], b + 1)
                A(actT[:, 0:4, :], ps[6][:, :].rearrange("p (k s) -> p k s", k=4), ACT.Copy)
                A(actT[:, 4:8, :], ps[7][:, :].rearrange("p (k s) -> p k s", k=4), ACT.Copy).then_inc(S["at_ok"], 1)
                act.wait_ge(S["w2_used"], b * 4 + 4)
                act.wait_ge(S["y_free"], b + 1)
                A(y_sb[:, 0:512], ps[6][:, :], ACT.Copy)
                A(y_sb[:, 512:1024], ps[7][:, :], ACT.Copy).then_inc(S["y_ok"], 1)

            me.base, me.count = base + per_head * H + LT, 0
            for i in range(LT):
                act.wait_ge(S["fin_sq"], i + 1)
                if i:
                    me.wait()
                me.mark(A(aT_t[:, 5120:6144], x_sb[:, i, :], ACT.Square, accum_out=stat[:, 12 + i:13 + i]))
                me.wait()
                A(rst[:, 12 + i:13 + i], stat[:, 12 + i:13 + i], ACT.Sqrt, bias=eps_t[:, :],
                  scale=1.0 / D).then_inc(S["fin_std"], 1)

        @block.vector
        def _(dve):
            V = nc.vector
            me = Steps(dve, S["dve_s"])
            dve.wait_ge(S["vecs_ps"], 1)
            V.tensor_copy(cols[:, :], ps[0][:, 0:112]).then_inc(S["cols_ok"], 1)
            dve.wait_ge(S["c_sig"], 1)
            dve.wait_ge(S["cols_ok"], 1)
            V.tensor_tensor(csil[:, :, :].rearrange("p k j -> p j k"),
                            cols[:, 0:16].rearrange("p (j k) -> p j k", j=2),
                            sc16[:, :].rearrange("p (j k) -> p j k", j=2), ALU.mult).then_inc(S["csil_ok"], 1)
            lb0 = cols[:, 72:88].rearrange("p (d h) -> p d h", d=2)
            lb1 = cols[:, 88:104].rearrange("p (d h) -> p d h", d=2)
            hd = hcols[:, :, :].rearrange("p h j -> p j h")
            me.link(V.tensor_tensor(hd[:, 0:2], lb0, lb1, ALU.max))
            me.mark(V.tensor_tensor(hd[:, 2:4], lb0, hd[:, 0:2], ALU.subtract))
            me.mark(V.tensor_tensor(hd[:, 4:6], lb1, hd[:, 0:2], ALU.subtract))
            me.wait()
            dve.sem_inc(S["lbx_ok"], 1)
            dve.wait_ge(S["stdev_ok"], 1)
            me.link(V.reciprocal(rst[:, 0:TT], rst[:, 0:TT]))
            for i in range(TT):
                src = xv[:, i, :] if i < CT else x_sb[:, i - CT, :]
                V.tensor_scalar(xv[:, i, :], src, rst[:, i:i + 1], None, ALU.mult).then_inc(S["xn_ok"], 1)
            dve.wait_ge(S["modc_ps"], 1)
            me.link(V.tensor_tensor(modc[:, :, :], ps[1][:, 0:32].rearrange("p (m j) -> p m j", j=2),
                                    cols[:, 16:32].unsqueeze(2).broadcast_to([P, 16, 2]), ALU.add))
            V.scalar_tensor_tensor(G1[:, :, :], modc[:, 8:16, :], 1.0,
                                   cols[:, 64:72].unsqueeze(2).broadcast_to([P, DK, 2]),
                                   ALU.add, ALU.mult).then_inc(S["modc_ok"], 1)
            dve.wait_ge(S["modc_ok"], 1)
            for j in range(DK):
                dve.wait_ge(S["xT_ps"], 2 * j + 1)
                V.tensor_scalar(aT[:, j, CTX:TOK], ps[2 + j % 3][:, :], G1[:, j, 0:1], modc[:, j, 0:1],
                                ALU.mult, ALU.add).then_inc(S["aT_lat_ok"], 1)
            for n in range(1, 2 * TT, 2):
                dve.wait_ge(S["v_ps"], n + 1)
                V.tensor_copy(xv[:, n // 2, 512:1024], ps[n % 4][:, :]).then_inc(S["v_ev_d"], 1)
            dve.wait_ge(S["lbe_ok"], 1)
            me.link(V.tensor_tensor(hd[:, 6:8], hd[:, 2:4], hd[:, 4:6], ALU.add))
            me.link(V.reciprocal(hd[:, 6:8], hd[:, 6:8]))
            me.link(V.tensor_tensor(hd[:, 0:2], hd[:, 2:4], hd[:, 6:8], ALU.mult))
            me.mark(V.tensor_scalar(hd[:, 2:4], hd[:, 0:2], -1.0, 1.0, ALU.mult, ALU.add))
            me.mark(V.tensor_scalar(hd[:, 4:6], hd[:, 0:2], 1.0, None, ALU.subtract))
            me.mark(V.tensor_copy(hd[:, 6], cols[:, 104:112]))
            for d in range(2):
                me.mark(V.memset(pm[d], 0.0))
            me.wait()

            gla = Steps(dve, S["dve_gla"])
            ew = Steps(dve, S["dve_ew"])

            def consume_scores(h1):
                dve.wait_ge(S["a_ps"], h1)
                V.memset(stat[:, 15:16], 0.0)
                for d in range(2):
                    sc = ps[4][:, d * 256:d * 256 + 256].rearrange("p (a t) -> p a t", a=LT)
                    V.copy_predicated(pm[d][0:CH, :, 0:CH], mk[0:CH, d], sc[0:CH])
                    last = V.copy_predicated(pm[d][CH:P, :, CH:P], mk[CH:P, d], sc[CH:P])
                last.then_inc(S["pm_ok"], 1)

            def states(h1):
                gla.base, gla.count = 17 * (h1 - 1), 0
                dve.wait_ge(S["b_ps"], h1)
                for d in range(2):
                    first = 0 if d == 0 else NCH - 1
                    gla.mark(V.tensor_copy(st[d][:, first, :], ps[4][:, d * P:(d + 1) * P]))
                for n in range(NCH - 1):
                    gla.wait()
                    for d in range(2):
                        ci = n if d == 0 else NCH - 1 - n
                        co = ci + 1 if d == 0 else ci - 1
                        bank = (5, 6)[ci % 2] if d == 0 else (7, 2)[ci % 2]
                        gla.mark(V.scalar_tensor_tensor(st[d][:, co, :], st[d][:, ci, :], ed[:, d, ci:ci + 1],
                                                       ps[bank][:, (ci // 2) * P:(ci // 2 + 1) * P],
                                                       ALU.mult, ALU.add))
                gla.wait()
                dve.sem_inc(S["st_ok"], 1)

            def gate(h1, ho):
                dve.wait_ge(S["o_ev"], h1)
                dve.wait_ge(S["rs_ok"], 2 * h1 + 1)
                gla.link(V.scalar_tensor_tensor(osb, osb, hc[:, 6:7], sq, ALU.mult, ALU.mult))
                V.tensor_tensor(ogT[:, ho, :], osb, gs, ALU.mult).then_inc(S["og_ok"], 1)

            def head(h, prev):
                ew.base, ew.count = 6 * h, 0
                if prev is not None:
                    consume_scores(h)
                dve.wait_ge(S["q_sig"], h + 1)
                V.tensor_tensor(qs, ps[3][:, :], sgq, ALU.mult).then_inc(S["qs_ok"], 1)
                if prev is not None:
                    states(h)
                    dve.wait_ge(S["g_sig"], h + 1)
                    gate(h, prev)
                    dve.wait_ge(S["og_ok"], h)
                else:
                    dve.wait_ge(S["g_sig"], h + 1)
                V.tensor_tensor(gs, ps[0][:, :], sgg, ALU.mult).then_inc(S["gs_ok"], 1)
                V.tensor_copy(v_h, xv[:, :, bass.ds(h * P, P)])
                V.tensor_copy(hc[:, :], hcols[:, bass.ds(h, 1), :].squeeze(1)).then_inc(S["hc_ok"], 1)
                dve.wait_ge(S["hc_ok"], h + 1)
                for d in range(2):
                    dve.wait_ge(S["lnf_ok"], 2 * h + (d + 1))
                    ew.mark(V.tensor_scalar(sgk[d], sgk[d], hc[:, 4 + d:5 + d], hc[:, 2 + d:3 + d],
                                            ALU.mult, ALU.add))
                    rev = slice(None, None, 1 if d == 0 else -1)
                    V.tensor_tensor_scan(bc[d][:, rev], res[:, d, :], lfq[d][:, rev], 0.0, ALU.mult,
                                         ALU.add).then_inc(S["b_ok"], 1)
                    dve.wait_ge(S["b_ok"], 2 * h + (d + 1))
                    bl = bc[d][:, CTX:TOK].rearrange("p (c t) -> p c t", c=NCH)
                    iref, ilast = (CH // 2 - 1, CH - 1) if d == 0 else (CH // 2, 0)
                    V.tensor_tensor(qe[d].rearrange("p (c t) -> p c t", c=NCH), bl,
                                    bl[:, :, iref:iref + 1].broadcast_to([P, NCH, CH]),
                                    ALU.subtract).then_inc(S["bm_ok"], 1)
                    ew.mark(V.tensor_tensor(ko[d][:, CTX:TOK].rearrange("p (c t) -> p c t", c=NCH),
                                            bl[:, :, ilast:ilast + 1].broadcast_to([P, NCH, CH]), bl,
                                            ALU.subtract))
                    il = CTX - 1 if d == 0 else 0
                    V.tensor_scalar(ko[d][:, 0:CTX], bc[d][:, 0:CTX], -1.0, bc[d][:, il:il + 1],
                                    ALU.mult, ALU.add).then_inc(S["bo_ok"], 1)
                for d in range(2):
                    dve.wait_ge(S["exp_ok"], 2 * h + (d + 1))
                    ew.wait()
                    V.tensor_tensor(qe[d], qe[d], qs, ALU.mult)
                    V.tensor_tensor(ke[d], ke[d], sgk[d][:, CTX:TOK], ALU.mult)
                    V.tensor_tensor(lfq[d][:, CTX:TOK], lfq[d][:, CTX:TOK], qs, ALU.mult)
                    ew.mark(V.tensor_tensor(ko[d], ko[d], sgk[d], ALU.mult))
                ew.wait()
                dve.sem_inc(S["ew_ok"], 1)
                assert ew.count == 6

            head(0, None)
            with dve.Fori(1, H) as h:
                head(h, h - 1)
            consume_scores(H)
            states(H)
            gate(H, H - 1)

            dve.wait_ge(S["o_ps"], H)
            V.tensor_copy(csb, csil[:, :, 0:1].broadcast_to([P, DK, P])).then_inc(S["csb_ok"], 1)
            dve.wait_ge(S["mwr_used"], DK)
            dve.wait_ge(S["ld_mb"], 32)
            dve.wait_ge(S["og_ok"], H)
            for n in range(8):
                dst = (g1_row, sh2_row, G2_row, g2_row)[n // 2]
                me.mark(V.tensor_tensor(dst[:, (n % 2) * 512:(n % 2) * 512 + 512], ps[n][:, :],
                                        mb_rows[:, n * 512:(n + 1) * 512], ALU.add))
            me.wait()
            V.scalar_tensor_tensor(G2_row, G2_row, 1.0, n2_row, ALU.add, ALU.mult).then_inc(S["rows_ok"], 1)
            dve.wait_ge(S["rows_ok"], 1)
            for i in range(LT):
                for n in range(2):
                    j = 2 * i + n
                    dve.wait_ge(S["yo_ps"], j + 1)
                    c0 = slice(n * 512, n * 512 + 512)
                    tmp = xv_t[:, 1024 + j * 512:1536 + j * 512]
                    me.link(V.tensor_tensor(tmp, ps[j][:, :], g1_row[:, c0], ALU.mult))
                    ins = V.tensor_tensor(x_sb[:, i, c0], x_sb[:, i, c0], tmp, ALU.add)
                    if n:
                        ins.then_inc(S["h_ok"], 1)
                    else:
                        me.mark(ins)
            dve.wait_ge(S["h_ok"], LT)
            dve.wait_ge(S["stdev2_ok"], 1)
            me.link(V.reciprocal(rst[:, 8:12], rst[:, 8:12]))
            for i in range(LT):
                me.link(V.scalar_tensor_tensor(f_sb[:, i, :], x_sb[:, i, :], rst[:, 8 + i:9 + i], G2_row,
                                               ALU.mult, ALU.mult))
                V.tensor_tensor(f_sb[:, i, :], f_sb[:, i, :], sh2_row, ALU.add).then_inc(S["f_ok"], 1)
            dve.wait_ge(S["f_ok"], LT)
            dve.sem_inc(S["arena_free"], 1)
            for j in range(0, DK, 2):
                dve.wait_ge(S["fT_ps"], j + 1)
                V.tensor_copy(ogT[:, j, :], ps[j][:, :]).then_inc(S["fT_ok"], 1)

            dve.wait_ge(S["lg_ps"], 1)
            dve.wait_ge(S["ld_rw"], 32)
            dve.wait_ge(S["consts"], 10)
            me.link(V.tensor_tensor(lg, ps[0][:, 0:LT * E].rearrange("p (i e) -> p i e", i=LT),
                                    rb_row[:, :].unsqueeze(1).broadcast_to([P, LT, E]), ALU.add))
            for i in range(LT):
                me.mark(V.max(v8[:, i, :], lg[:, i, :]))
            me.wait()
            for i in range(LT):
                me.mark(V.max_index(i8[:, i, :], v8[:, i, :], lg[:, i, :]))
            me.wait()
            me.mark(V.tensor_copy(i8f, i8))
            V.tensor_tensor(ew4, v8[:, :, 0:TOPK], v8[:, :, 0:1].broadcast_to([P, LT, TOPK]),
                            ALU.subtract).then_inc(S["e_v_ok"], 1)
            me.wait()
            for k in range(TOPK):
                me.mark(V.tensor_tensor(oh[:, :, k, :], io_e.unsqueeze(1).broadcast_to([P, LT, E]),
                                        i8f[:, :, k:k + 1].broadcast_to([P, LT, E]), ALU.is_equal))
            me.wait()
            V.tensor_reduce(msk, oh.rearrange("p i k e -> p i e k"), AX_X, ALU.add).then_inc(S["msk_ok"], 1)
            dve.wait_ge(S["e_w_ok"], 1)
            me.link(V.tensor_reduce(es, ew4, AX_X, ALU.add))
            me.link(V.reciprocal(es, es))
            me.mark(V.tensor_tensor(wk[:, :, :], ew4, es.unsqueeze(2).broadcast_to([P, LT, TOPK]), ALU.mult))
            dve.wait_ge(S["pos_ps"], 1)
            me.link(V.tensor_copy(cnt, ps[1][:, LT * E:(LT + 1) * E]))
            me.link(V.tensor_scalar(nblk, cnt, 0.5, None, ALU.is_gt))
            for n in range(1, LT):
                me.link(V.scalar_tensor_tensor(nblk, cnt, n * P + 0.5, nblk, ALU.is_gt, ALU.add))
            me.link(V.tensor_tensor_scan(cum, onesE, nblk, 0.0, ALU.mult, ALU.add))
            me.link(V.tensor_tensor(pst, cum, nblk, ALU.subtract))
            me.link(V.tensor_scalar(pst, pst, float(P), None, ALU.mult))
            me.link(V.tensor_tensor(dm[:, :, :], ps[1][:, 0:LT * E].rearrange("p (i e) -> p i e", i=LT),
                                    pst.unsqueeze(1).broadcast_to([P, LT, E]), ALU.add))
            me.link(V.scalar_tensor_tensor(dm[:, :, :], dm[:, :, :], 1.0, msk, ALU.add, ALU.mult))
            me.link(V.tensor_scalar(dm[:, :, :], dm[:, :, :], -1.0, None, ALU.add))
            for k in range(TOPK):
                me.mark(V.tensor_tensor(ohd[:, :, k, :], oh[:, :, k, :],
                                        tokf[:, :].rearrange("p (i k) -> p i k", i=LT)[:, :, k:k + 1]
                                        .broadcast_to([P, LT, E]), ALU.mult))
            me.wait()
            me.mark(V.tensor_reduce(rid[:, :, :], ohd.rearrange("p i k e -> p i e k"), AX_X, ALU.add))
            me.link(V.tensor_tensor(io_b[0:1], io_b[0:1], cum[0:1].unsqueeze(1).broadcast_to([1, NBT, E]),
                                    ALU.is_ge))
            me.link(V.tensor_reduce(bef[:, :], io_b[0:1], AX_X, ALU.add))
            me.link(V.tensor_scalar(bef[:, :], bef[:, :], float(E - 1), None, ALU.min))
            me.mark(V.tensor_copy(tab_e[:, :], bef[:, :]))
            me.mark(V.memset(tab_nf[:, :], 1.0))
            me.wait()
            me.mark(V.tensor_tensor(tab_nf[:, 1:NBT], bef[:, 1:NBT], bef[:, 0:NBT - 1], ALU.not_equal))
            me.mark(V.tensor_copy(tab_n[:, :], cum[0:1, E - 1:E]))
            me.wait()
            me.link(V.tensor_copy(tab_new[:, :], tab_nf[:, :]))
            dve.sem_inc(S["tab_ok"], 1)
            n_blocks = dve.value_load(tab_n[0:1, 0:1], min_val=1, max_val=NB_MAX)

            def one_hot(b):
                e = dve.value_load(tab_e[0:1, bass.ds(b, 1)] if not isinstance(b, int) else tab_e[0:1, b:b + 1],
                                   min_val=0, max_val=E - 1)
                for i in range(LT):
                    V.tensor_scalar(pt[:, i, :], slot_io[:, :], dm[:, i, bass.ds(e, 1)], None, ALU.is_equal)
                V.tensor_copy(rid_e[:, :], rid[:, :, bass.ds(e, 1)].squeeze(2)).then_inc(S["pt_ok"], 1)

            def index():
                me.link(V.tensor_scalar(idx_f[:, :], ps[6][:, 0:1], 0.0, 4096.0, ALU.is_equal, ALU.mult))
                me.link(V.scalar_tensor_tensor(idx_f[:, :], ps[6][:, 0:1], 1.0, idx_f[:, :], ALU.subtract, ALU.add))
                V.tensor_copy(idx_next[:, :], idx_f[:, :]).then_inc(S["idx_ok"], 1)

            dve.sem_inc(S["z_free"], 1)
            one_hot(0)
            dve.wait_ge(S["xi_ps"], 1)
            index()
            base2 = me.base + me.count
            n_in = 7
            with dve.Fori(0, n_blocks) as b:
                me.base, me.count = base2 + n_in * b, 0
                dve.wait_ge(S["xi_ps"], b + 1)
                dve.wait_ge(S["pt_ok"], b + 1)
                me.link(V.tensor_scalar(slot_io[:, :], slot_io[:, :], float(P), None, ALU.add))
                one_hot(b + 1)
                dve.wait_ge(S["z_ps"], b + 1)
                for n in range(2):
                    c0 = slice(n * 512, n * 512 + 512)
                    V.tensor_scalar(glu_g[:, c0], ps[2 + n][:, :], 7.0, None, ALU.min).then_inc(S["gmin_ok"], 1)
                me.mark(V.tensor_scalar(act_a[:, 0:512], ps[4][:, :], 7.0, -7.0, ALU.min, ALU.max))
                me.mark(V.tensor_scalar(act_a[:, 512:1024], ps[5][:, :], 7.0, -7.0, ALU.min, ALU.max))
                me.wait()
                dve.sem_inc(S["z_free"], 1)
                dve.wait_ge(S["xi_ps"], b + 2)
                dve.wait_ge(S["idxc_ok"], b + 1)
                index()
                dve.wait_ge(S["gmin_ok"], b * 2 + 2)
                for n in range(2):
                    c0 = slice(n * 512, n * 512 + 512)
                    me.mark(V.scalar_tensor_tensor(act_a[:, c0], act_a[:, c0], 1.0, glu_g[:, c0],
                                                   ALU.add, ALU.mult))
                me.wait()
                for n in range(2):
                    c0 = slice(n * 512, n * 512 + 512)
                    dve.wait_ge(S["sig_ok"], b * 2 + (n + 1))
                    V.tensor_tensor(act_a[:, c0], act_a[:, c0], glu_s[:, c0], ALU.mult).then_inc(S["act_ok"], 1)
                assert me.count == n_in, me.count

            me = Steps(dve, S["fin_s"])

            def finish(i):
                dve.wait_ge(S["fin_std"], i + 1)
                me.link(V.reciprocal(rst[:, 12 + i:13 + i], rst[:, 12 + i:13 + i]))
                V.scalar_tensor_tensor(x_sb[:, i, :], x_sb[:, i, :], rst[:, 12 + i:13 + i], fin_row,
                                       ALU.mult, ALU.mult).then_inc(S["fin_ok"], 1)

            dve.wait_ge(S["ld_rows"], 16)
            for i in range(LT):
                dve.wait_ge(gath[i], 16)
                y0 = ygat[:, i, 0, :]
                me.link(V.tensor_scalar(y0, y0, wk[:, i, 0:1], None, ALU.mult))
                for k in range(1, TOPK):
                    me.link(V.scalar_tensor_tensor(y0, ygat[:, i, k, :], wk[:, i, k:k + 1], y0,
                                                   ALU.mult, ALU.add))
                me.link(V.tensor_tensor(y0, y0, g2_row, ALU.mult))
                V.tensor_tensor(x_sb[:, i, :], x_sb[:, i, :], y0, ALU.add).then_inc(S["fin_sq"], 1)
                if i:
                    finish(i - 1)
            finish(LT - 1)

        @block.tensor
        def _(pe):
            mm, tr = nc.tensor.matmul, nc.tensor.transpose
            pe.wait_ge(S["ld_vec"], 16 * 9)
            pe.wait_ge(S["consts"], 4)
            tr(ps[0][:, 0:112], vecs, ident[0:112, 0:112]).then_inc(S["vecs_ps"], 1)
            pe.wait_ge(S["csil_ok"], 1)
            pe.wait_ge(ld_mw, 16 * DK)
            for m in range(16):
                for k in range(DK):
                    last = mm(ps[1][:, 2 * m:2 * m + 2], mwc[:, k, m * P:(m + 1) * P], csil[:, k, :],
                              start=(k == 0), stop=(k == DK - 1))
            last.then_inc(S["modc_ps"], 1)
            pe.wait_ge(S["xn_ok"], TT)
            for j in range(DK):
                for lat in (True, False):
                    if j >= 3:
                        pe.wait_ge(S["aT_lat_ok" if lat else "aT_ctx_ok"], j - 2)
                    bank = ps[(2 if lat else 5) + j % 3]
                    tiles = range(CT, TT) if lat else range(CT)
                    for n, i in enumerate(tiles):
                        last = tr(bank[:, n * P:(n + 1) * P], xv[:, i, j * P:(j + 1) * P], ident[:, :])
                    last.then_inc(S["xT_ps"], 1)
            pe.wait_ge(S["ld_wv"], 16 * DK)
            pe.wait_ge(S["aT_lat_ok"], DK)
            pe.wait_ge(S["aT_ctx_ok"], DK)
            for n in range(2 * TT):
                if n >= 4:
                    pe.wait_ge(S["v_ev_a" if n % 2 == 0 else "v_ev_d"], (n - 4) // 2 + 1)
                i = n // 2
                for k in range(DK):
                    last = mm(ps[n % 4][:, :], aT[:, k, i * P:(i + 1) * P],
                              w_sq[:, k, (n % 2) * 512:(n % 2) * 512 + 512], start=(k == 0), stop=(k == DK - 1))
                last.then_inc(S["v_ps"], 1)
            pe.wait_ge(S["v_ev_a"], TT)
            pe.wait_ge(S["v_ev_d"], TT)

            def section(s, bank, done):
                for k in range(DK):
                    last = mm(bank[:, :], wh[:, s, k, :], aT[:, k, CTX:TOK], start=(k == 0), stop=(k == DK - 1))
                last.then_inc(done, 1)

            def scores(h1):
                pe.wait_ge(S["ew_ok"], h1)
                pe.wait_ge(S["rs_ok"], 2 * h1 - 1)
                for d in range(2):
                    for ch in range(NCH):
                        r = slice((ch % 2) * CH, (ch % 2) * CH + CH)
                        cs = slice(ch * CH, (ch + 1) * CH)
                        col = d * 256 + (ch // 2) * CH
                        mm(ps[4][r, col:col + CH], ke[d][:, cs], qe[d][:, cs], start=True, stop=True)
                for d in range(2):
                    for n in range(LT):
                        tr(ps[5 if d == 0 else 7][:, n * P:(n + 1) * P], ko[d][:, CTX + n * P:CTX + (n + 1) * P],
                           ident[:, :])
                    for n in range(CT):
                        last = tr(ps[6][:, (d * CT + n) * P:(d * CT + n + 1) * P], ko[d][:, n * P:(n + 1) * P],
                                  ident[:, :])
                last.then_inc(S["a_ps"], 1)

            def outer(h1, zc_seen):
                pe.wait_ge(S["koT_ok"], h1)
                pe.wait_ge(S["pm_ok"], h1)
                pe.wait_ge(S["zc_sig"], zc_seen)
                for d in range(2):
                    for i in range(CT):
                        mm(ps[4][:, d * P:(d + 1) * P], koT[d][:, i, :], v_h[:, i, :], start=(i == 0),
                           stop=(i == CT - 1))
                    for ch in range(NCH):
                        if ch == (NCH - 1 if d == 0 else 0):
                            continue
                        r = slice((ch % 2) * CH, (ch % 2) * CH + CH)
                        bank = ps[(5, 6)[ch % 2] if d == 0 else (7, 2)[ch % 2]]
                        last = mm(bank[:, (ch // 2) * P:(ch // 2 + 1) * P], koT[d][r, CT + ch // 2, :],
                                  v_h[r, CT + ch // 2, :], start=True, stop=True)
                last.then_inc(S["b_ps"], 1)

            def outputs(h1):
                pe.wait_ge(S["st_ok"], h1)
                for d in range(2):
                    for n in range(LT):
                        mm(ps[5][:, n * P:(n + 1) * P], v_h[:, CT + n, :], pm[d][:, n, :],
                           start=(d == 0 and n == 0), stop=False, skip_group_check=True)
                for d in range(2):
                    for ch in range(NCH):
                        last = mm(ps[5][:, ch * CH:(ch + 1) * CH], st[d][:, ch, :],
                                  lfq[d][:, CTX + ch * CH:CTX + (ch + 1) * CH], start=False,
                                  stop=(d == 1 and ch == NCH - 1), skip_group_check=True)
                last.then_inc(S["o_ps"], 1)
                pe.wait_ge(S["sq_ok"], h1)
                mm(ps[6][:, :], ones[:, :], sq, start=True, stop=True).then_inc(S["ss_ps"], 1)

            def head(h, prev):
                for s in range(2):
                    pe.wait_ge(ld_wh[s], 16 * h + 16)
                if prev is not None:
                    pe.wait_ge(S["zc_sig"], h)
                for s in range(2):
                    for k in range(DK):
                        last = mm(ps[2][:, s * CTX:(s + 1) * CTX], wh[:, s, k, :], aT[:, k, 0:CTX],
                                  start=(k == 0), stop=(k == DK - 1))
                last.then_inc(S["zc_ps"], 1)
                if prev is not None:
                    pe.wait_ge(S["gs_ok"], h)
                section(0, ps[0], S["zf_ps"])
                if prev is not None:
                    pe.wait_ge(S["zb_sig"], h)
                section(1, ps[1], S["zb_ps"])
                if prev is not None:
                    scores(h)
                pe.wait_ge(ld_wh[2], 16 * h + 16)
                if prev is not None:
                    pe.wait_ge(S["qs_ok"], h)
                section(2, ps[3], S["q_ps"])
                if prev is not None:
                    outer(h, h + 1)
                pe.wait_ge(ld_wh[3], 16 * h + 16)
                pe.wait_ge(S["zf_sig"], h + 1)
                section(3, ps[0], S["g_ps"])
                if prev is not None:
                    outputs(h)

            head(0, None)
            with pe.Fori(1, H) as h:
                head(h, 1)
            scores(H)
            outer(H, H)
            outputs(H)

            pe.wait_ge(S["csb_ok"], 1)
            pe.wait_ge(S["rs_ok"], 2 * H)
            pe.wait_ge(S["gs_ok"], H)
            for k in range(DK):
                pe.wait_ge(ld_mwr[k % 3], 16 * (k // 3 + 1))
                for n in range(8):
                    last = mm(ps[n][:, :], csb[:, k, :], mwr[k % 3][:, n * 512:(n + 1) * 512],
                              start=(k == 0), stop=(k == DK - 1))
                last.then_inc(S["mwr_used"], 1)
            pe.wait_ge(S["rows_ok"], 1)
            pe.wait_ge(S["og_ok"], H)
            pe.wait_ge(S["ld_wout"], 16 * DK)
            for j in range(2 * LT):
                i, n = j // 2, j % 2
                for k in range(DK):
                    last = mm(ps[j][:, :], ogT[:, k, i * P:(i + 1) * P], w_sq[:, k, n * 512:(n + 1) * 512],
                              start=(k == 0), stop=(k == DK - 1))
                last.then_inc(S["yo_ps"], 1)
            pe.wait_ge(S["f_ok"], LT)
            for j in range(DK):
                for i in range(LT):
                    last = tr(ps[j][:, i * P:(i + 1) * P], f_sb[:, i, j * P:(j + 1) * P], ident[:, :])
                last.then_inc(S["fT_ps"], 1)
            pe.wait_ge(S["fT_ok"], DK)
            pe.wait_ge(S["ld_rw"], 32)
            for i in range(LT):
                for k in range(DK):
                    last = mm(ps[0][:, i * E:(i + 1) * E], ogT[:, k, i * P:(i + 1) * P], rw[:, k, :],
                              start=(k == 0), stop=(k == DK - 1))
            last.then_inc(S["lg_ps"], 1)
            pe.wait_ge(S["msk_ok"], 1)
            for i in range(LT):
                for i0 in range(i + 1):
                    mm(ps[1][:, i * E:(i + 1) * E], (tri if i0 == i else ones)[:, :], msk[:, i0, :],
                       start=(i0 == 0), stop=(i0 == i))
            for i in range(LT):
                last = mm(ps[1][:, LT * E:(LT + 1) * E], ones[:, :], msk[:, i, :], start=(i == 0),
                          stop=(i == LT - 1))
            last.then_inc(S["pos_ps"], 1)

            pe.wait_ge(S["tab_ok"], 1)
            n_blocks = pe.value_load(tab_n[0:1, 0:1], min_val=1, max_val=NB_MAX)

            def gather(b1):
                pe.wait_ge(S["pt_ok"], b1)
                for k in range(DK):
                    for i in range(LT):
                        last = mm(ps[k // 4][:, (k % 4) * P:(k % 4 + 1) * P], f_sb[:, i, k * P:(k + 1) * P],
                                  pt[:, i, :], start=(i == 0), stop=(i == LT - 1))
                last.then_inc(S["xt_ps"], 1)
                if not isinstance(b1, int):
                    pe.wait_ge(S["y_ok"], b1 - 1)
                for i in range(LT):
                    last = mm(ps[6][:, 0:1], pt[:, i, :], rid_e[:, i:i + 1], start=(i == 0), stop=(i == LT - 1))
                last.then_inc(S["xi_ps"], 1)

            gather(1)
            with pe.Fori(0, n_blocks) as b:
                pe.wait_ge(S["xt_ok"], b + 1)
                pe.wait_ge(S["z_free"], b + 1)
                for k in range(DK):
                    pe.wait_ge(ld_w1[k], b * 16 + 16)
                    for n in range(4):
                        last = mm(ps[2 + n][:, :], XT[:, k, :], w1s[:, k, n * 512:(n + 1) * 512],
                                  start=(k == 0), stop=False)
                    last.then_inc(S["w1_used"], 1)
                pe.wait_ge(S["ld_b"], b * 32 + 32)
                for n in range(4):
                    last = mm(ps[2 + n][:, :], ones[0:1, :], bias_sb[0:1, n * 512:(n + 1) * 512],
                              start=False, stop=True)
                last.then_inc(S["z_ps"], 1)
                gather(b + 2)
                pe.wait_ge(S["act_ok"], b * 2 + 2)
                pe.wait_ge(S["idx_ok"], b + 2)
                for k in range(DK):
                    last = tr(ps[6 + k // 4][:, (k % 4) * P:(k % 4 + 1) * P], act_a[:, k * P:(k + 1) * P],
                              ident[:, :])
                last.then_inc(S["at_ps"], 1)
                pe.wait_ge(S["at_ok"], b + 1)
                for n in range(2):
                    mm(ps[6 + n][:, :], ones[0:1, :], bias_sb[0:1, 2 * FF + n * 512:2 * FF + (n + 1) * 512],
                       start=True, stop=False)
                for k in range(DK):
                    if k % 2 == 0:
                        pe.wait_ge(ld_w2[k // 2], b * 16 + 16)
                    for n in range(2):
                        last = mm(ps[6 + n][:, :], actT[:, k, :], w2s[:, k, n * 512:(n + 1) * 512],
                                  start=False, stop=(k == DK - 1))
                    if k % 2 == 1:
                        last.then_inc(S["w2_used"], 1)


INPUTS = ["x", "c", "ctx", "c_ctx", "mod_w", "mod_b", "norm1_g", "norm2_g", "hg_w_in", "hg_lb_logits",
          "hg_norm_g", "hg_w_out", "router_w", "router_b", "moe_w1", "moe_b1", "moe_w2", "moe_b2", "final_g"]
SHAPES = {"x": [LAT, D], "c": [1, D], "ctx": [CTX, D], "mod_w": [D, 6 * D], "mod_b": [6 * D],
          "norm1_g": [D], "norm2_g": [D], "hg_w_in": [D, 5 * D], "hg_norm_g": [D], "hg_w_out": [D, D],
          "router_w": [D, E], "router_b": [E], "moe_w1": [E * D, 2 * FF], "moe_b1": [E, 2 * FF],
          "moe_w2": [E * FF, D], "moe_b2": [E, D]}


def kernel(**inputs):
    import concourse.bacc as bacc
    from concourse.bass_utils import run_bass_kernel_spmd

    nc = bacc.Bacc("TRN2", target_bir_lowering=False, num_devices=1, dynamic_dma_scratch_size=8192)
    arrays, args = {}, []
    for name in INPUTS:
        a = np.ascontiguousarray(inputs[name])
        a = a.reshape(SHAPES.get(name, a.shape))
        arrays[f"in_{name}"] = a
        args.append(nc.dram_tensor(f"in_{name}", a.shape, mybir.dt.from_np(a.dtype), kind="ExternalInput").ap())
    args.append(nc.dram_tensor("out", [LAT, D], F32, kind="ExternalOutput").ap())
    build(nc, *args)
    r = run_bass_kernel_spmd(nc, [arrays], core_ids=[0])
    return r.results[0]["out"].reshape(1, LAT, D)
```

```python
import numpy as np
import concourse.bass as bass
from concourse import mybir
from contextlib import ExitStack

F32 = mybir.dt.float32
BF16 = mybir.dt.bfloat16
I32 = mybir.dt.int32
U32 = mybir.dt.uint32
F32R = mybir.dt.float32r
ALU = mybir.AluOpType
ACT = mybir.ActivationFunctionType
AX_X = mybir.AxisListType.X

P = 128
D = 1024
DK = D // P
LAT, CTX = 512, 256
TOK = LAT + CTX
LT, CT, TT = LAT // P, CTX // P, TOK // P
CH = 64
NCH = LAT // CH
E, TOPK = 32, 4
FF = 1024
NB_MAX = LAT * TOPK // P + E
NBT = NB_MAX + 3
EPS = 1e-6
N_CONST = 15
LIMIT = 7.0
ALPHA = 1.702
SIG_MAX = float(1.0 / (1.0 + np.exp(-ALPHA * LIMIT)))
W1C, W2C = DK, DK // 2
NC = W1C + W2C
AHEAD = 3
SLOTS = 3
WHOLE = (1, 6, 7)
NS = NC - len(WHOLE)
H = DK


class Steps:

    def __init__(self, engine, sem):
        self.engine, self.sem, self.count, self.base = engine, sem, 0, 0

    def mark(self, ins):
        ins.then_inc(self.sem, 1)
        self.count += 1
        return self.count

    def wait(self, count=None):
        self.engine.wait_ge(self.sem, self.base + (self.count if count is None else count))

    def link(self, ins):
        self.mark(ins)
        self.wait()


def build(nc, x, c, ctx_in, c_ctx, mod_w, mod_b, norm1_g, norm2_g, hg_w_in, hg_lb_logits, hg_norm_g,
          hg_w_out, router_w, router_b, moe_w1, moe_b1, moe_w2, moe_b2, final_g, out):
    frows = nc.dram_tensor("frows", [LAT, D], F32, kind="Internal").ap()
    yrows = nc.dram_tensor("yrows", [TOPK * LAT, D], F32, kind="Internal").ap()
    with ExitStack() as stack:
        place = {}

        def sb(name, shape, dt=F32):
            place[name] = nc.sbuf_base
            return stack.enter_context(nc.sbuf_tensor(name, shape, dt))

        def sem(name):
            return stack.enter_context(nc.semaphore(name))

        arena = sb("arena", [P, 24576])
        x_sb = sb("x_sb", [P, LT, D])
        aT_t = sb("aT_t", [P, DK * TOK])
        xv_t = sb("xv_t", [P, TT * D])
        ring_t = sb("ring_t", [P, 4096])
        ogT = sb("ogT", [P, DK, LAT])
        rows2 = sb("rows2", [P, 2 * D])
        g2_row, fin_row = rows2[:, 0:D], rows2[:, D:2 * D]

        mwc = arena[:, 0:16384].rearrange("p (k n) -> p k n", k=DK)
        w_sq = arena[:, 16384:24576].rearrange("p (k n) -> p k n", k=DK)
        aT = aT_t[:, :].rearrange("p (k t) -> p k t", k=DK)
        f_sb = aT_t[:, 0:LT * D].rearrange("p (i n) -> p i n", i=LT)
        xv = xv_t[:, :].rearrange("p (i n) -> p i n", i=TT)
        wh = ring_t[:, :].rearrange("p (s k n) -> p s k n", s=4, k=DK)

        at = [0]

        def take(n):
            at[0] += n
            return arena[:, at[0] - n:at[0]]

        sgk = [take(TOK) for _ in range(2)]
        lfq = [take(TOK) for _ in range(2)]
        bc = [take(TOK) for _ in range(2)]
        qe = [take(LAT) for _ in range(2)]
        ke = [take(LAT) for _ in range(2)]
        ko = [take(TOK) for _ in range(2)]
        qs, sgq, sgg, gs = (take(LAT) for _ in range(4))
        pm = [take(LAT).rearrange("p (a t) -> p a t", a=LT) for _ in range(2)]
        st = [take(NCH * P).rearrange("p (c v) -> p c v", c=NCH) for _ in range(2)]
        koT = [take(TOK).rearrange("p (i k) -> p i k", i=TT) for _ in range(2)]
        v_h = take(TOK).rearrange("p (i v) -> p i v", i=TT)
        assert at[0] <= 16384
        osb, sq = rows2[:, 0:LAT], rows2[:, LAT:2 * LAT]

        g1_row, sh2_row, G2_row, n2_row = (arena[:, i * D:(i + 1) * D] for i in range(4))
        mb_rows = arena[:, 4096:8192]
        mwr = [ring_t[:, :], arena[:, 8192:12288], arena[:, 12288:16384]]

        cols = sb("cols", [P, 112])
        csil = sb("csil", [P, DK, 2])
        csb = xv_t[:, 0:D].rearrange("p (k m) -> p k m", k=DK)
        sc16 = sb("sc16", [P, 16])
        modc = sb("modc", [P, 16, 2])
        G1 = sb("G1", [P, DK, 2])
        stat = sb("stat", [P, 16])
        rst = sb("rst", [P, 16])
        eps_t = sb("eps_t", [P, 1])
        junk = sb("junk", [P, 1])
        hcols = sb("hcols", [P, H, 8])
        hc = sb("hc", [P, 8])
        ed = sb("ed", [P, 2, NCH])
        ident = sb("ident", [P, P])
        ones = sb("ones", [P, P])
        tri = sb("tri", [P, P])
        res = sb("res", [P, 2, TOK], BF16)
        mk = sb("mk", [P, 2, LT, CH], mybir.dt.uint8)
        mkf = xv_t[:, 2048:2048 + 512].rearrange("p (d a t) -> p d a t", d=2, a=LT)

        rw = sb("rw", [P, DK, E])
        rb_row = sb("rb_row", [P, E])
        at2 = [0]

        def rtake(n):
            at2[0] += n
            return ring_t[:, at2[0] - n:at2[0]]

        lg = rtake(LT * E).rearrange("p (i e) -> p i e", i=LT)
        v8 = rtake(LT * 8).rearrange("p (i e) -> p i e", i=LT)
        i8 = rtake(LT * 8).rearrange("p (i e) -> p i e", i=LT).bitcast(U32)
        i8f = rtake(LT * 8).rearrange("p (i e) -> p i e", i=LT)
        oh = rtake(LT * TOPK * E).rearrange("p (i k e) -> p i k e", i=LT, k=TOPK)
        ohd = rtake(LT * TOPK * E).rearrange("p (i k e) -> p i k e", i=LT, k=TOPK)
        msk = rtake(LT * E).rearrange("p (i e) -> p i e", i=LT)
        io_e = rtake(E)
        ew4 = rtake(LT * TOPK).rearrange("p (i k) -> p i k", i=LT)
        es = rtake(LT)
        cnt, nblk, nb1, cum, pst, onesE = (rtake(E) for _ in range(6))
        io_b = rtake(NBT * E).rearrange("p (b e) -> p b e", e=E)
        assert at2[0] <= 4096
        kk = sb("kk", [P, LT, E])
        kf = sb("kf", [P, LT * TOPK])
        idx_f = sb("idx_f", [P, 8])
        row_next, row_3, row_2, row_1, tok_next, zero_i, zero_j, zero_k = (
            sb(n, [P, 1], U32) for n in ("row_next", "row_3", "row_2", "row_1", "tok_next", "zero_i", "zero_j", "zero_k"))
        wk = sb("wk", [P, LT, TOPK])
        dm = sb("dm", [P, LT, E])
        bef = sb("bef", [P, NBT])
        tab_e = sb("tab_e", [1, NBT], I32)
        tab_new = sb("tab_new", [1, NBT], I32)
        tab_nf = sb("tab_nf", [1, NBT])
        tab_n = sb("tab_n", [1, 1], I32)
        slot_io = sb("slot_io", [P, P])
        pt = sb("pt", [P, LT, P], BF16)
        ids = sb("ids", [P, LT, P], BF16)
        pmod = sb("pmod", [P, 1])
        sel = sb("sel", [96, P], BF16)
        bias3 = sb("bias3", [96, 3 * FF], BF16)
        b_raw = aT_t[0:96, 0:3 * FF]

        w1s = arena[:, 0:16384].rearrange("p (k n) -> p k n", k=DK)
        w2s = arena[:, 16384:24576].rearrange("p (k n) -> p k n", k=DK)

        def at_place(name, base, offset, n):
            return nc.alloc_sbuf_tensor_at(name, [P, n], F32R, offset=place[base] + 4 * offset)

        w_hi = [at_place("w_hi0", "aT_t", 0, 2048), at_place("w_hi1", "aT_t", 4096, 2048),
                at_place("w_hi2", "ogT", 2048, 2048)]
        w_lo = [at_place("w_lo0", "aT_t", 2048, 2048), at_place("w_lo1", "ogT", 0, 2048),
                at_place("w_lo2", "ring_t", 0, 2048)]
        XTh, XTl, aTh, aTl = (at_place(n, "xv_t", i * 1024, 1024) for i, n in
                              enumerate(("XTh", "XTl", "aTh", "aTl")))
        XT = xv_t[:, 1024:2048]
        xg, act_a = (xv_t[:, 4096 + i * 1024:5120 + i * 1024] for i in range(2))
        y_sb, lin = (ring_t[:, 2048 + i * 1024:3072 + i * 1024] for i in range(2))
        sig = rows2[:, D:2 * D]
        ygat = arena[:, 0:16384].rearrange("p (i k n) -> p i k n", i=LT, k=TOPK)

        ps = [stack.enter_context(nc.psum_tensor(f"ps{i}", [P, 512], F32)) for i in range(8)]

        MID = W1C - AHEAD
        order = [("w1", 0, k) for k in range(AHEAD, W1C)] + [("w1", 1, k) for k in range(AHEAD)] \
            + [("w2", 0, m) for m in range(W2C)]
        assert all(order[j][0] == "w1" for j in WHOLE) and NS % SLOTS == 0
        whole_k = sorted(order[j][2] for j in WHOLE)
        split_no = {j: n for n, j in enumerate(j for j in range(NC) if j not in WHOLE)}
        slot_of = {j: n % SLOTS for j, n in split_no.items()}
        place_of = {(kind, k): (j, ahead) for j, (kind, ahead, k) in enumerate(order)}
        EARLY = [j for j in range(4) if j not in WHOLE][:2]

        def slot_free(j):
            n = split_no[j] - SLOTS
            before = next(i for i, m in split_no.items() if m == n % NS)
            return before + 1 - (NC if n < 0 else 0)

        names = """lbx_ok lbe_ok dve_gla dve_ew fin_s ld_vec ld_x ld_ctx ld_wv ld_wout ld_rw ld_rows ld_mb consts pool_s dve_s act_s
        vecs_ps cols_ok c_sig csil_ok modc_ps modc_ok sumsq_ok stdev_ok xn_ok xT_ps aT_lat_ok aT_ctx_ok
        v_ps v_ev_a v_ev_d
        zc_ps zf_ps zb_ps q_ps g_ps a_ps b_ps o_ps ss_ps
        zc_sig zf_sig zb_sig q_sig g_sig qs_ok gs_ok koT_ok pm_ok st_ok o_ev sq_ok rs_ok og_ok
        hc_ok lnf_ok b_ok bm_ok bo_ok exp_ok ew_ok
        rows_ok csb_ok mwr_used yo_ps h_ok sumsq2_ok stdev2_ok f_ok fT_ps fT_ok lg_ps lg_ok
        e_v_ok e_w_ok msk_ok pos_ps tab_ok wk_ok
        frow_st pt_ok xi_ps idx_ok mid_ok xg_ld xt_ps xth_ok xtl_ok z_ps lin_ok sig_ok glu_ok act_ok at_ps
        ath_ok atl_ok y_ok y_st y_free rot hi_ok lo_ok w_used sel_ok ld_br arena_free fin_sq fin_std fin_ok out_st""".split()
        S = {n: sem(n) for n in names}
        ld_mw = sem("ld_mw")
        ld_wh = [sem(f"ld_wh{s}") for s in range(4)]
        sec_done = [S["zf_ps"], S["zb_ps"], S["q_ps"], S["g_ps"]]
        ld_mwr = [sem(f"ld_mwr{s}") for s in range(3)]
        gath = [sem(f"gath{i}") for i in range(LT)]
        ld_w1 = [sem(f"ld_w1_{k}") for k in range(DK)]
        ld_w2 = [sem(f"ld_w2_{k}") for k in range(4)]

        block = stack.enter_context(nc.Block())
        vecs = ring_t[0:112, 0:P]
        SEC = [2, 3, 0, 4]

        w_in_s = hg_w_in.rearrange("(k p) n -> p k n", p=P)

        def vrow(v):
            return v.rearrange("(j p) -> j p", p=P)

        @block.sync
        def _(sp):
            row = 0
            for v in (c[0], c_ctx, mod_b, norm1_g, hg_lb_logits[0, 0], hg_lb_logits[0, 1],
                      hg_lb_logits[1, 0], hg_lb_logits[1, 1], hg_norm_g):
                n = v.shape[0] // P
                sp.dma_start(ring_t[row:row + n, 0:P], vrow(v)).then_inc(S["ld_vec"], 16)
                row += n
            assert row == 112
            sp.dma_start(x_sb[:, :, :], x.rearrange("(i p) n -> p i n", p=P)).then_inc(S["ld_x"], 16)
            sp.dma_start(xv[:, 0:CT, :], ctx_in.rearrange("(i p) n -> p i n", p=P)).then_inc(S["ld_ctx"], 16)
            for k in range(DK):
                sp.dma_start(mwc[:, k, :], mod_w[k * P:(k + 1) * P, 0:2 * D]).then_inc(ld_mw, 16)
            for k in range(DK):
                sp.dma_start(w_sq[:, k, :], hg_w_in[k * P:(k + 1) * P, D:2 * D]).then_inc(S["ld_wv"], 16)
            sp.dma_start(rw[:, :, :], router_w.rearrange("(k p) e -> p k e", p=P)).then_inc(S["ld_rw"], 16)
            sp.dma_start(rb_row[:, :], router_b.partition_broadcast(P)).then_inc(S["ld_rw"], 16)

            sp.wait_ge(S["vecs_ps"], 1)
            for s in range(4):
                sp.dma_start(wh[:, s], w_in_s[:, :, SEC[s] * D:SEC[s] * D + P]).then_inc(ld_wh[s], 16)
            sp.wait_ge(S["v_ps"], 2 * TT)
            for k in range(DK):
                sp.dma_start(w_sq[:, k, :], hg_w_out[k * P:(k + 1) * P, :]).then_inc(S["ld_wout"], 16)
            with sp.Fori(1, H) as h:
                for s in range(4):
                    sp.wait_ge(sec_done[s], h)
                    sp.dma_start(wh[:, s], w_in_s[:, :, bass.ds((h - 1) * P + (SEC[s] * D + P), P)]).then_inc(ld_wh[s], 16)
            for k in range(DK):
                if k == 0:
                    for s in range(4):
                        sp.wait_ge(sec_done[s], H)
                if k == 1:
                    sp.wait_ge(S["o_ps"], H)
                    sp.wait_ge(S["og_ok"], H)
                    sp.dma_start(mb_rows, mod_b[2 * D:6 * D].partition_broadcast(P)).then_inc(S["ld_mb"], 16)
                    sp.dma_start(n2_row, norm2_g.partition_broadcast(P)).then_inc(S["ld_mb"], 16)
                if k >= 3:
                    sp.wait_ge(S["mwr_used"], k - 2)
                sp.dma_start(mwr[k % 3], mod_w[k * P:(k + 1) * P, 2 * D:6 * D]).then_inc(ld_mwr[k % 3], 16)
            for part in range(3):
                sp.dma_start(aT_t[part * E:(part + 1) * E, 0:2 * FF], moe_b1).then_inc(S["ld_br"], 16)
                sp.dma_start(aT_t[part * E:(part + 1) * E, 2 * FF:3 * FF], moe_b2).then_inc(S["ld_br"], 16)
            for i in range(LT):
                sp.wait_ge(S["f_ok"], i + 1)
                sp.dma_start(frows[i * P:(i + 1) * P, :], f_sb[:, i, :]).then_inc(S["frow_st"], 16)

            sp.wait_ge(S["arena_free"], 1)
            sp.wait_ge(S["tab_ok"], 1)
            n_blocks = sp.value_load(tab_n[0:1, 0:1], min_val=1, max_val=NB_MAX)

            def load_w1(e, k):
                sp.dma_start(w1s[:, k, :], moe_w1[bass.ds(e * D + k * P, P), :]).then_inc(ld_w1[k], 16)

            def load_w2(e, k):
                sp.dma_start(w2s[:, 2 * k:2 * k + 2, :],
                             moe_w2[bass.ds(e * FF + 2 * k * P, 2 * P), :].rearrange("(a p) n -> p a n", p=P)
                             ).then_inc(ld_w2[k], 16)

            e0 = sp.value_load(tab_e[0:1, 0:1], min_val=0, max_val=E - 1)
            for k in range(W1C):
                load_w1(e0, k)
            for k in range(W2C):
                load_w2(e0, k)

            def chunk_read(b, kind, k):
                j, ahead = place_of[kind, k]
                if j in WHOLE:
                    sp.wait_ge(S["w_used"], b * NC + (j + 1 - ahead * NC))
                else:
                    sp.wait_ge(S["lo_ok"], b * NS + (split_no[j] + 1 - ahead * NS))

            chunks = [("w1", k) for k in range(W1C)] + [("w2", k) for k in range(W2C)]
            with sp.Fori(1, n_blocks) as b:
                e = sp.value_load(tab_e[0:1, bass.ds(b, 1)], min_val=0, max_val=E - 1)
                new = sp.value_load(tab_new[0:1, bass.ds(b, 1)], min_val=0, max_val=1)
                with sp.If(new):
                    for kind, k in chunks:
                        chunk_read(b, kind, k)
                        load_w1(e, k) if kind == "w1" else load_w2(e, k)
                with sp.Else():
                    for kind, k in chunks:
                        chunk_read(b, kind, k)
                        sp.sem_inc(ld_w1[k] if kind == "w1" else ld_w2[k], 16)
            sp.wait_ge(S["lo_ok"], n_blocks * NS + (split_no[EARLY[-1]] + 1))
            for k in list(range(AHEAD)) + [order[j][2] for j in EARLY]:
                sp.sem_inc(ld_w1[k], 16)
            sp.wait_ge(S["y_st"], n_blocks * 16)
            sp.dma_start(fin_row, final_g.partition_broadcast(P)).then_inc(S["ld_rows"], 16)
            for i in range(LT):
                sp.dma_start(ygat[:, i], yrows.rearrange("(k i p) n -> i p k n", k=TOPK, p=P)[i]
                             ).then_inc(gath[i], 16)
            for i in range(LT):
                sp.wait_ge(S["fin_ok"], i + 1)
                sp.dma_start(out[i * P:(i + 1) * P, :], x_sb[:, i, :]).then_inc(S["out_st"], 16)
            sp.wait_ge(S["out_st"], 16 * LT)

        @block.gpsimd
        def _(pool):
            me = Steps(pool, S["pool_s"])
            me.mark(pool.memset(ones[:, :], 1.0))
            me.mark(pool.memset(ident[:, :], 0.0))
            me.mark(pool.memset(mkf, 1.0))
            me.mark(pool.memset(res[:, :, :], 1.0))
            pool.memset(eps_t[:, :], EPS).then_inc(S["consts"], 1)
            me.wait()
            pool.affine_select(out=ident[:, :], in_=ident[:, :], compare_op=ALU.not_equal, fill=1.0, base=0,
                               pattern=[[-1, P]], channel_multiplier=1).then_inc(S["consts"], 1)
            pool.affine_select(out=tri[:, :], in_=ones[:, :], compare_op=ALU.is_gt, fill=0.0, base=0,
                               pattern=[[1, P]], channel_multiplier=-1).then_inc(S["consts"], 1)
            me.mark(pool.memset(res[:, 0, 0:1], 0.0))
            me.mark(pool.memset(res[:, 0, CTX:TOK:CH], 0.0))
            me.mark(pool.memset(res[:, 1, 0:LAT:CH], 0.0))
            me.mark(pool.memset(res[:, 1, LAT:LAT + 1], 0.0))
            me.wait()
            pool.wait_ge(S["consts"], 3)
            for half in range(2):
                r = slice(half * CH, (half + 1) * CH)
                me.link(pool.affine_select(out=mkf[r, 0], in_=mkf[r, 0], compare_op=ALU.is_ge, fill=0.0, base=0,
                                           pattern=[[0, LT], [1, CH]], channel_multiplier=-1))
                me.link(pool.affine_select(out=mkf[r, 1], in_=mkf[r, 1], compare_op=ALU.is_ge, fill=0.0, base=0,
                                           pattern=[[0, LT], [-1, CH]], channel_multiplier=1))
            me.wait()
            pool.tensor_copy(mk[:, :, :, :], mkf).then_inc(S["consts"], 1)
            pool.wait_ge(S["yo_ps"], 1)
            pool.iota(io_e, pattern=[[1, E]], base=0, channel_multiplier=0,
                      allow_small_or_imprecise_dtypes=True).then_inc(S["consts"], 1)
            pool.iota(io_b, pattern=[[1, NBT], [0, E]], base=0, channel_multiplier=0,
                      allow_small_or_imprecise_dtypes=True).then_inc(S["consts"], 1)
            pool.iota(slot_io[:, :], pattern=[[1, P]], base=0, channel_multiplier=0,
                      allow_small_or_imprecise_dtypes=True).then_inc(S["consts"], 1)
            pool.memset(onesE, 1.0).then_inc(S["consts"], 1)
            pool.iota(kf[:, :].rearrange("p (i k) -> p i k", i=LT), pattern=[[0, LT], [1, TOPK]], base=1,
                      channel_multiplier=0, allow_small_or_imprecise_dtypes=True).then_inc(S["consts"], 1)
            for part in range(3):
                pool.wait_ge(S["consts"], 9 + part)
                pool.iota(pmod[part * E:(part + 1) * E, :], pattern=[[0, 1]], base=0, channel_multiplier=1,
                          allow_small_or_imprecise_dtypes=True).then_inc(S["consts"], 1)
            pool.wait_ge(S["consts"], 12)
            me.mark(pool.memset(ids[:, :, :], 0.0))
            me.wait()
            pool.iota(ids[:, :, 0:1], pattern=[[0, LT], [0, 1]], base=0, channel_multiplier=1,
                      allow_small_or_imprecise_dtypes=True).then_inc(S["consts"], 1)
            pool.iota(ids[:, :, 1:2], pattern=[[1, LT], [0, 1]], base=0, channel_multiplier=0,
                      allow_small_or_imprecise_dtypes=True).then_inc(S["consts"], 1)
            pool.memset(zero_i[:, :], 0).then_inc(S["consts"], 1)
            pool.wait_ge(S["consts"], N_CONST)
            pool.wait_ge(S["tab_ok"], 1)
            n_blocks = pool.value_load(tab_n[0:1, 0:1], min_val=1, max_val=NB_MAX)
            pool.sem_inc(S["y_free"], 1)
            me.link(pool.memset(xg, 0.0))

            def move(out, in_):
                return pool.tensor_tensor(out=out[:, :], in0=in_[:, :], in1=zero_i[:, :], op=ALU.add)

            def gather():
                pool.indirect_dma_start(out=xg, out_offset=None, in_=frows,
                                        in_offset=bass.IndirectOffsetOnAxis(ap=tok_next[:, :], axis=0),
                                        bounds_check=LAT - 1, oob_is_err=False).then_inc(S["xg_ld"], 16)

            pool.wait_ge(S["frow_st"], 16 * LT)
            for n, row in enumerate((row_1, row_2)):
                pool.wait_ge(S["idx_ok"], n + 1)
                if n:
                    pool.wait_ge(S["xt_ps"], n)
                move(row, row_next)
                gather()
                pool.wait_ge(S["xg_ld"], 16 * n + 16)
                move(zero_j, zero_i).then_inc(S["mid_ok"], 1)
                pool.wait_ge(S["mid_ok"], n + 1)

            def round_(b, first):
                pool.wait_ge(S["idx_ok"], b + 3)
                pool.wait_ge(S["xt_ps"], b + 2)
                move(zero_j, zero_i)
                gather()
                if not first:
                    pool.wait_ge(S["y_st"], b * 16)
                    move(row_1, row_2).then_inc(S["rot"], 1)
                    pool.wait_ge(S["rot"], b * 2 - 1)
                    move(row_2, row_3).then_inc(S["rot"], 1)
                    pool.wait_ge(S["rot"], b * 2)
                    pool.sem_inc(S["y_free"], 1)
                pool.wait_ge(S["xg_ld"], b * 16 + 48)
                move(row_3, row_next).then_inc(S["mid_ok"], 1)
                pool.wait_ge(S["y_ok"], b + 2)
                pool.wait_ge(S["mid_ok"], b + 3)
                move(zero_k, zero_i)
                pool.indirect_dma_start(out=yrows, out_offset=bass.IndirectOffsetOnAxis(ap=row_1[:, :], axis=0),
                                        in_=y_sb, in_offset=None, bounds_check=TOPK * LAT - 1,
                                        oob_is_err=False).then_inc(S["y_st"], 16)

            round_(0, True)
            with pool.Fori(1, n_blocks) as b:
                round_(b, False)

        @block.scalar
        def _(act):
            me = Steps(act, S["act_s"])
            A = nc.scalar.activation
            act.wait_ge(S["cols_ok"], 1)
            A(sc16[:, :], cols[:, 0:16], ACT.Sigmoid).then_inc(S["c_sig"], 1)
            act.wait_ge(S["lbx_ok"], 1)
            A(hcols[:, :, 2:6], hcols[:, :, 2:6], ACT.Exp).then_inc(S["lbe_ok"], 1)
            act.wait_ge(S["ld_x"], 16)
            act.wait_ge(S["ld_ctx"], 16)
            for i in range(TT):
                src = xv[:, i, :] if i < CT else x_sb[:, i - CT, :]
                if i:
                    me.wait()
                me.mark(A(ogT[:, 0:2, :], src.rearrange("p (a n) -> p a n", a=2), ACT.Square,
                          accum_out=stat[:, i:i + 1]))
            me.wait()
            act.wait_ge(S["consts"], 4)
            A(rst[:, 0:TT], stat[:, 0:TT], ACT.Sqrt, bias=eps_t[:, :], scale=1.0 / D).then_inc(S["stdev_ok"], 1)
            act.wait_ge(S["modc_ok"], 1)
            for j in range(DK):
                act.wait_ge(S["xT_ps"], 2 * j + 2)
                A(aT[:, j, 0:CTX], ps[5 + j % 3][:, 0:CTX], ACT.Identity, bias=modc[:, j, 1:2],
                  scale=G1[:, j, 1:2]).then_inc(S["aT_ctx_ok"], 1)
            for n in range(0, 2 * TT, 2):
                act.wait_ge(S["v_ps"], n + 1)
                A(xv[:, n // 2, 0:512], ps[n % 4][:, :], ACT.Copy).then_inc(S["v_ev_a"], 1)

            base = me.count
            per_head = 8

            def head(h, prev):
                me.base, me.count = base + per_head * h, 0
                act.wait_ge(S["zc_ps"], h + 1)
                if prev is not None:
                    act.wait_ge(S["ew_ok"], h)
                A(sgk[0][:, 0:CTX], ps[2][:, 0:CTX], ACT.Sigmoid)
                A(sgk[1][:, 0:CTX], ps[2][:, CTX:2 * CTX], ACT.Sigmoid).then_inc(S["zc_sig"], 1)
                act.wait_ge(S["zf_ps"], h + 1)
                A(sgk[0][:, CTX:TOK], ps[0][:, :], ACT.Sigmoid).then_inc(S["zf_sig"], 1)
                act.wait_ge(S["zb_ps"], h + 1)
                A(sgk[1][:, CTX:TOK], ps[1][:, :], ACT.Sigmoid).then_inc(S["zb_sig"], 1)
                if prev is not None:
                    evac_koT(h)
                act.wait_ge(S["q_ps"], h + 1)
                if prev is not None:
                    act.wait_ge(S["qs_ok"], h)
                A(sgq, ps[3][:, :], ACT.Sigmoid).then_inc(S["q_sig"], 1)
                act.wait_ge(S["g_ps"], h + 1)
                if prev is not None:
                    act.wait_ge(S["gs_ok"], h)
                A(sgg, ps[0][:, :], ACT.Sigmoid).then_inc(S["g_sig"], 1)
                if prev is not None:
                    readout(h)
                act.wait_ge(S["hc_ok"], h + 1)
                for d in range(2):
                    A(lfq[d], sgk[d], ACT.Ln, bias=hc[:, d:d + 1], scale=hc[:, 2 + d:3 + d]).then_inc(S["lnf_ok"], 1)
                for d in range(2):
                    act.wait_ge(S["b_ok"], 2 * h + (d + 1))
                    m1 = me.mark(A(lfq[d][:, CTX:TOK], bc[d][:, CTX:TOK], ACT.Exp))
                    last = bc[d][:, CTX + (CH - 1 if d == 0 else 0):TOK:CH]
                    me.mark(A(ed[:, d, :], last, ACT.Exp))
                    act.wait_ge(S["bm_ok"], 2 * h + (d + 1))
                    m2 = me.mark(A(ke[d], qe[d], ACT.Exp, scale=-1.0))
                    me.wait(m2)
                    A(qe[d], qe[d], ACT.Exp)
                    act.wait_ge(S["bo_ok"], 2 * h + (d + 1))
                    me.wait(m1)
                    me.mark(A(ko[d], ko[d], ACT.Exp))
                    me.wait()
                    act.sem_inc(S["exp_ok"], 1)
                assert me.count == per_head

            def evac_koT(h1):
                act.wait_ge(S["a_ps"], h1)
                A(koT[0][:, CT:TT, :], ps[5][:, :].rearrange("p (i k) -> p i k", i=LT), ACT.Copy)
                A(koT[0][:, 0:CT, :], ps[6][:, 0:CTX].rearrange("p (i k) -> p i k", i=CT), ACT.Copy)
                A(koT[1][:, CT:TT, :], ps[7][:, :].rearrange("p (i k) -> p i k", i=LT), ACT.Copy)
                A(koT[1][:, 0:CT, :], ps[6][:, CTX:2 * CTX].rearrange("p (i k) -> p i k", i=CT),
                  ACT.Copy).then_inc(S["koT_ok"], 1)

            def readout(h1):
                act.wait_ge(S["o_ps"], h1)
                A(osb, ps[5][:, :], ACT.Copy).then_inc(S["o_ev"], 1)
                A(sq, ps[5][:, :], ACT.Square).then_inc(S["sq_ok"], 1)
                act.wait_ge(S["ss_ps"], h1)
                act.wait_ge(S["sq_ok"], h1)
                A(sq, ps[6][:, :], ACT.Ln, bias=eps_t[:, :], scale=1.0 / P).then_inc(S["rs_ok"], 1)
                act.wait_ge(S["rs_ok"], 2 * h1)
                A(sq, sq, ACT.Exp, scale=-0.5).then_inc(S["rs_ok"], 1)

            act.sem_inc(S["rs_ok"], 1)
            head(0, None)
            with act.Fori(1, H) as h:
                head(h, 1)
            evac_koT(H)
            readout(H)

            me.base, me.count = base + per_head * H, 0
            for i in range(LT):
                act.wait_ge(S["h_ok"], i + 1)
                if i:
                    me.wait()
                me.mark(A(aT_t[:, 5120:6144], x_sb[:, i, :], ACT.Square, accum_out=stat[:, 8 + i:9 + i]))
            me.wait()
            A(rst[:, 8:12], stat[:, 8:12], ACT.Sqrt, bias=eps_t[:, :], scale=1.0 / D).then_inc(S["stdev2_ok"], 1)
            for j in range(1, DK, 2):
                act.wait_ge(S["fT_ps"], j + 1)
                A(ogT[:, j, :], ps[j][:, :], ACT.Copy).then_inc(S["fT_ok"], 1)
            act.wait_ge(S["e_v_ok"], 1)
            A(ew4, ew4, ACT.Exp).then_inc(S["e_w_ok"], 1)

            act.wait_ge(S["tab_ok"], 1)
            n_blocks = act.value_load(tab_n[0:1, 0:1], min_val=1, max_val=NB_MAX)


            def hi_part(b, j):
                kind, ahead, k = order[j]
                act.wait_ge(ld_w1[k] if kind == "w1" else ld_w2[k], b * 16 + 16 * (1 + ahead))
                act.wait_ge(S["w_used"], b * NC + (NC + slot_free(j)))
                src = w1s[:, k, :] if kind == "w1" else w2s[:, 2 * k:2 * k + 2, :].rearrange("p a n -> p (a n)")
                A(w_hi[slot_of[j]][:, :], src, ACT.Copy).then_inc(S["hi_ok"], 1)

            def xth(half, bank):
                for k in whole_k:
                    if k // 4 == half:
                        A(XT[:, k * P:(k + 1) * P], bank[:, (k % 4) * P:(k % 4 + 1) * P], ACT.Copy)
                A(XTh[:, half * 512:half * 512 + 512], bank[:, :], ACT.Copy).then_inc(S["xth_ok"], 1)

            act.sem_inc(S["y_ok"], 1)
            act.sem_inc(S["hi_ok"], split_no[MID])
            act.wait_ge(S["xt_ps"], 1)
            xth(0, ps[0])
            xth(1, ps[1])
            act.wait_ge(ld_w1[0], 16)
            A(w_hi[slot_of[MID]][:, :], w1s[:, 0, :], ACT.Copy).then_inc(S["hi_ok"], 1)
            act.wait_ge(S["hi_ok"], split_no[MID] + 1)
            act.sem_inc(S["hi_ok"], NS - split_no[MID] - 1)
            for j in EARLY:
                hi_part(0, j)
            with act.Fori(0, n_blocks) as b:
                A(junk[:, :], eps_t[:, :], ACT.Sigmoid)
                for j in range(EARLY[-1] + 1, MID + 1):
                    hi_part(b, j)
                act.wait_ge(S["xt_ps"], b + 2)
                act.wait_ge(S["w_used"], b * NC + (NC + 1))
                xth(0, ps[0])
                hi_part(b, W1C)
                act.wait_ge(S["z_ps"], b + 1)
                for n in range(2):
                    A(lin[:, n * 512:n * 512 + 512], ps[4 + n][:, :], ACT.Identity,
                      bias=ones[:, 0:1]).then_inc(S["lin_ok"], 1)
                    A(sig[:, n * 512:n * 512 + 512], ps[2 + n][:, :], ACT.Sigmoid,
                      scale=ALPHA).then_inc(S["sig_ok"], 1)
                xth(1, ps[1])
                hi_part(b, W1C + 1)
                hi_part(b, W1C + 2)
                act.wait_ge(S["at_ps"], b + 1)
                for n in range(2):
                    A(aTh[:, n * 512:n * 512 + 512], ps[6 + n][:, :], ACT.Copy).then_inc(S["ath_ok"], 1)
                hi_part(b, W1C + 3)
                for j in EARLY:
                    hi_part(b + 1, j)
                act.wait_ge(S["w_used"], b * NC + 2 * NC)
                act.wait_ge(S["y_free"], b + 1)
                A(y_sb[:, 0:512], ps[6][:, :], ACT.Copy)
                A(y_sb[:, 512:1024], ps[7][:, :], ACT.Copy).then_inc(S["y_ok"], 1)

            me.base, me.count = base + per_head * H + LT, 0
            for i in range(LT):
                act.wait_ge(S["fin_sq"], i + 1)
                if i:
                    me.wait()
                me.mark(A(aT_t[:, 5120:6144], x_sb[:, i, :], ACT.Square, accum_out=stat[:, 12 + i:13 + i]))
                me.wait()
                A(rst[:, 12 + i:13 + i], stat[:, 12 + i:13 + i], ACT.Sqrt, bias=eps_t[:, :],
                  scale=1.0 / D).then_inc(S["fin_std"], 1)

        @block.vector
        def _(dve):
            V = nc.vector
            me = Steps(dve, S["dve_s"])
            dve.wait_ge(S["vecs_ps"], 1)
            V.tensor_copy(cols[:, :], ps[0][:, 0:112]).then_inc(S["cols_ok"], 1)
            dve.wait_ge(S["c_sig"], 1)
            dve.wait_ge(S["cols_ok"], 1)
            V.tensor_tensor(csil[:, :, :].rearrange("p k j -> p j k"),
                            cols[:, 0:16].rearrange("p (j k) -> p j k", j=2),
                            sc16[:, :].rearrange("p (j k) -> p j k", j=2), ALU.mult).then_inc(S["csil_ok"], 1)
            lb0 = cols[:, 72:88].rearrange("p (d h) -> p d h", d=2)
            lb1 = cols[:, 88:104].rearrange("p (d h) -> p d h", d=2)
            hd = hcols[:, :, :].rearrange("p h j -> p j h")
            me.link(V.tensor_tensor(hd[:, 0:2], lb0, lb1, ALU.max))
            me.mark(V.tensor_tensor(hd[:, 2:4], lb0, hd[:, 0:2], ALU.subtract))
            me.mark(V.tensor_tensor(hd[:, 4:6], lb1, hd[:, 0:2], ALU.subtract))
            me.wait()
            dve.sem_inc(S["lbx_ok"], 1)
            dve.wait_ge(S["stdev_ok"], 1)
            me.link(V.reciprocal(rst[:, 0:TT], rst[:, 0:TT]))
            for i in range(TT):
                src = xv[:, i, :] if i < CT else x_sb[:, i - CT, :]
                V.tensor_scalar(xv[:, i, :], src, rst[:, i:i + 1], None, ALU.mult).then_inc(S["xn_ok"], 1)
            dve.wait_ge(S["modc_ps"], 1)
            me.link(V.tensor_tensor(modc[:, :, :], ps[1][:, 0:32].rearrange("p (m j) -> p m j", j=2),
                                    cols[:, 16:32].unsqueeze(2).broadcast_to([P, 16, 2]), ALU.add))
            V.scalar_tensor_tensor(G1[:, :, :], modc[:, 8:16, :], 1.0,
                                   cols[:, 64:72].unsqueeze(2).broadcast_to([P, DK, 2]),
                                   ALU.add, ALU.mult).then_inc(S["modc_ok"], 1)
            dve.wait_ge(S["modc_ok"], 1)
            for j in range(DK):
                dve.wait_ge(S["xT_ps"], 2 * j + 1)
                V.tensor_scalar(aT[:, j, CTX:TOK], ps[2 + j % 3][:, :], G1[:, j, 0:1], modc[:, j, 0:1],
                                ALU.mult, ALU.add).then_inc(S["aT_lat_ok"], 1)
            for n in range(1, 2 * TT, 2):
                dve.wait_ge(S["v_ps"], n + 1)
                V.tensor_copy(xv[:, n // 2, 512:1024], ps[n % 4][:, :]).then_inc(S["v_ev_d"], 1)
            dve.wait_ge(S["lbe_ok"], 1)
            me.link(V.tensor_tensor(hd[:, 6:8], hd[:, 2:4], hd[:, 4:6], ALU.add))
            me.link(V.reciprocal(hd[:, 6:8], hd[:, 6:8]))
            me.link(V.tensor_tensor(hd[:, 0:2], hd[:, 2:4], hd[:, 6:8], ALU.mult))
            me.mark(V.tensor_scalar(hd[:, 2:4], hd[:, 0:2], -1.0, 1.0, ALU.mult, ALU.add))
            me.mark(V.tensor_scalar(hd[:, 4:6], hd[:, 0:2], 1.0, None, ALU.subtract))
            me.mark(V.tensor_copy(hd[:, 6], cols[:, 104:112]))
            for d in range(2):
                me.mark(V.memset(pm[d], 0.0))
            me.wait()

            gla = Steps(dve, S["dve_gla"])
            ew = Steps(dve, S["dve_ew"])

            def consume_scores(h1):
                dve.wait_ge(S["a_ps"], h1)
                V.memset(stat[:, 15:16], 0.0)
                for d in range(2):
                    sc = ps[4][:, d * 256:d * 256 + 256].rearrange("p (a t) -> p a t", a=LT)
                    V.copy_predicated(pm[d][0:CH, :, 0:CH], mk[0:CH, d], sc[0:CH])
                    last = V.copy_predicated(pm[d][CH:P, :, CH:P], mk[CH:P, d], sc[CH:P])
                last.then_inc(S["pm_ok"], 1)

            def states(h1):
                gla.base, gla.count = 17 * (h1 - 1), 0
                dve.wait_ge(S["b_ps"], h1)
                for d in range(2):
                    first = 0 if d == 0 else NCH - 1
                    gla.mark(V.tensor_copy(st[d][:, first, :], ps[4][:, d * P:(d + 1) * P]))
                for n in range(NCH - 1):
                    gla.wait()
                    for d in range(2):
                        ci = n if d == 0 else NCH - 1 - n
                        co = ci + 1 if d == 0 else ci - 1
                        bank = (5, 6)[ci % 2] if d == 0 else (7, 2)[ci % 2]
                        gla.mark(V.scalar_tensor_tensor(st[d][:, co, :], st[d][:, ci, :], ed[:, d, ci:ci + 1],
                                                       ps[bank][:, (ci // 2) * P:(ci // 2 + 1) * P],
                                                       ALU.mult, ALU.add))
                gla.wait()
                dve.sem_inc(S["st_ok"], 1)

            def gate(h1, ho):
                dve.wait_ge(S["o_ev"], h1)
                dve.wait_ge(S["rs_ok"], 2 * h1 + 1)
                gla.link(V.scalar_tensor_tensor(osb, osb, hc[:, 6:7], sq, ALU.mult, ALU.mult))
                V.tensor_tensor(ogT[:, ho, :], osb, gs, ALU.mult).then_inc(S["og_ok"], 1)

            def head(h, prev):
                ew.base, ew.count = 6 * h, 0
                if prev is not None:
                    consume_scores(h)
                dve.wait_ge(S["q_sig"], h + 1)
                V.tensor_tensor(qs, ps[3][:, :], sgq, ALU.mult).then_inc(S["qs_ok"], 1)
                if prev is not None:
                    states(h)
                    dve.wait_ge(S["g_sig"], h + 1)
                    gate(h, prev)
                    dve.wait_ge(S["og_ok"], h)
                else:
                    dve.wait_ge(S["g_sig"], h + 1)
                V.tensor_tensor(gs, ps[0][:, :], sgg, ALU.mult).then_inc(S["gs_ok"], 1)
                V.tensor_copy(v_h, xv[:, :, bass.ds(h * P, P)])
                V.tensor_copy(hc[:, :], hcols[:, bass.ds(h, 1), :].squeeze(1)).then_inc(S["hc_ok"], 1)
                dve.wait_ge(S["hc_ok"], h + 1)
                for d in range(2):
                    dve.wait_ge(S["lnf_ok"], 2 * h + (d + 1))
                    ew.mark(V.tensor_scalar(sgk[d], sgk[d], hc[:, 4 + d:5 + d], hc[:, 2 + d:3 + d],
                                            ALU.mult, ALU.add))
                    rev = slice(None, None, 1 if d == 0 else -1)
                    V.tensor_tensor_scan(bc[d][:, rev], res[:, d, :], lfq[d][:, rev], 0.0, ALU.mult,
                                         ALU.add).then_inc(S["b_ok"], 1)
                    dve.wait_ge(S["b_ok"], 2 * h + (d + 1))
                    bl = bc[d][:, CTX:TOK].rearrange("p (c t) -> p c t", c=NCH)
                    iref, ilast = (CH // 2 - 1, CH - 1) if d == 0 else (CH // 2, 0)
                    V.tensor_tensor(qe[d].rearrange("p (c t) -> p c t", c=NCH), bl,
                                    bl[:, :, iref:iref + 1].broadcast_to([P, NCH, CH]),
                                    ALU.subtract).then_inc(S["bm_ok"], 1)
                    ew.mark(V.tensor_tensor(ko[d][:, CTX:TOK].rearrange("p (c t) -> p c t", c=NCH),
                                            bl[:, :, ilast:ilast + 1].broadcast_to([P, NCH, CH]), bl,
                                            ALU.subtract))
                    il = CTX - 1 if d == 0 else 0
                    V.tensor_scalar(ko[d][:, 0:CTX], bc[d][:, 0:CTX], -1.0, bc[d][:, il:il + 1],
                                    ALU.mult, ALU.add).then_inc(S["bo_ok"], 1)
                for d in range(2):
                    dve.wait_ge(S["exp_ok"], 2 * h + (d + 1))
                    ew.wait()
                    V.tensor_tensor(qe[d], qe[d], qs, ALU.mult)
                    V.tensor_tensor(ke[d], ke[d], sgk[d][:, CTX:TOK], ALU.mult)
                    V.tensor_tensor(lfq[d][:, CTX:TOK], lfq[d][:, CTX:TOK], qs, ALU.mult)
                    ew.mark(V.tensor_tensor(ko[d], ko[d], sgk[d], ALU.mult))
                ew.wait()
                dve.sem_inc(S["ew_ok"], 1)
                assert ew.count == 6

            head(0, None)
            with dve.Fori(1, H) as h:
                head(h, h - 1)
            consume_scores(H)
            states(H)
            gate(H, H - 1)

            dve.wait_ge(S["o_ps"], H)
            V.tensor_copy(csb, csil[:, :, 0:1].broadcast_to([P, DK, P])).then_inc(S["csb_ok"], 1)
            dve.wait_ge(S["ld_br"], 16 * 6)
            me.link(V.tensor_copy(bias3[:, :], b_raw))
            for part in range(1, 3):
                r = slice(part * E, (part + 1) * E)
                for _ in range(part):
                    me.link(V.tensor_tensor(b_raw[r], b_raw[r], bias3[r, :], ALU.subtract))
                    me.link(V.tensor_copy(bias3[r, :], b_raw[r]))
            dve.wait_ge(S["mwr_used"], DK)
            dve.wait_ge(S["ld_mb"], 32)
            dve.wait_ge(S["og_ok"], H)
            for n in range(8):
                dst = (g1_row, sh2_row, G2_row, g2_row)[n // 2]
                me.mark(V.tensor_tensor(dst[:, (n % 2) * 512:(n % 2) * 512 + 512], ps[n][:, :],
                                        mb_rows[:, n * 512:(n + 1) * 512], ALU.add))
            me.wait()
            V.scalar_tensor_tensor(G2_row, G2_row, 1.0, n2_row, ALU.add, ALU.mult).then_inc(S["rows_ok"], 1)
            dve.wait_ge(S["rows_ok"], 1)
            for i in range(LT):
                for n in range(2):
                    j = 2 * i + n
                    dve.wait_ge(S["yo_ps"], j + 1)
                    c0 = slice(n * 512, n * 512 + 512)
                    tmp = xv_t[:, 1024 + j * 512:1536 + j * 512]
                    me.link(V.tensor_tensor(tmp, ps[j][:, :], g1_row[:, c0], ALU.mult))
                    ins = V.tensor_tensor(x_sb[:, i, c0], x_sb[:, i, c0], tmp, ALU.add)
                    if n:
                        ins.then_inc(S["h_ok"], 1)
                    else:
                        me.mark(ins)
            dve.wait_ge(S["h_ok"], LT)
            dve.wait_ge(S["stdev2_ok"], 1)
            me.link(V.reciprocal(rst[:, 8:12], rst[:, 8:12]))
            for i in range(LT):
                me.link(V.scalar_tensor_tensor(f_sb[:, i, :], x_sb[:, i, :], rst[:, 8 + i:9 + i], G2_row,
                                               ALU.mult, ALU.mult))
                V.tensor_tensor(f_sb[:, i, :], f_sb[:, i, :], sh2_row, ALU.add).then_inc(S["f_ok"], 1)
            dve.wait_ge(S["f_ok"], LT)
            dve.sem_inc(S["arena_free"], 1)
            for j in range(0, DK, 2):
                dve.wait_ge(S["fT_ps"], j + 1)
                V.tensor_copy(ogT[:, j, :], ps[j][:, :]).then_inc(S["fT_ok"], 1)

            dve.wait_ge(S["lg_ps"], 1)
            dve.wait_ge(S["ld_rw"], 32)
            dve.wait_ge(S["consts"], N_CONST)
            me.link(V.tensor_tensor(lg, ps[0][:, 0:LT * E].rearrange("p (i e) -> p i e", i=LT),
                                    rb_row[:, :].unsqueeze(1).broadcast_to([P, LT, E]), ALU.add))
            for i in range(LT):
                me.mark(V.max(v8[:, i, :], lg[:, i, :]))
            me.wait()
            for i in range(LT):
                me.mark(V.max_index(i8[:, i, :], v8[:, i, :], lg[:, i, :]))
            me.wait()
            me.mark(V.tensor_copy(i8f, i8))
            V.tensor_tensor(ew4, v8[:, :, 0:TOPK], v8[:, :, 0:1].broadcast_to([P, LT, TOPK]),
                            ALU.subtract).then_inc(S["e_v_ok"], 1)
            me.wait()
            for k in range(TOPK):
                me.mark(V.tensor_tensor(oh[:, :, k, :], io_e.unsqueeze(1).broadcast_to([P, LT, E]),
                                        i8f[:, :, k:k + 1].broadcast_to([P, LT, E]), ALU.is_equal))
            me.wait()
            V.tensor_reduce(msk, oh.rearrange("p i k e -> p i e k"), AX_X, ALU.add).then_inc(S["msk_ok"], 1)
            dve.wait_ge(S["e_w_ok"], 1)
            me.link(V.tensor_reduce(es, ew4, AX_X, ALU.add))
            me.link(V.reciprocal(es, es))
            me.mark(V.tensor_tensor(wk[:, :, :], ew4, es.unsqueeze(2).broadcast_to([P, LT, TOPK]), ALU.mult))
            dve.wait_ge(S["pos_ps"], 1)
            me.link(V.tensor_copy(cnt, ps[1][:, LT * E:(LT + 1) * E]))
            me.link(V.tensor_scalar(nblk, cnt, 0.5, None, ALU.is_gt))
            for n in range(1, LT):
                me.link(V.scalar_tensor_tensor(nblk, cnt, n * P + 0.5, nblk, ALU.is_gt, ALU.add))
            me.link(V.tensor_tensor_scan(cum, onesE, nblk, 0.0, ALU.mult, ALU.add))
            me.link(V.tensor_tensor(pst, cum, nblk, ALU.subtract))
            me.link(V.tensor_scalar(pst, pst, float(P), None, ALU.mult))
            me.link(V.tensor_tensor(dm[:, :, :], ps[1][:, 0:LT * E].rearrange("p (i e) -> p i e", i=LT),
                                    pst.unsqueeze(1).broadcast_to([P, LT, E]), ALU.add))
            me.link(V.scalar_tensor_tensor(dm[:, :, :], dm[:, :, :], 1.0, msk, ALU.add, ALU.mult))
            me.link(V.tensor_scalar(dm[:, :, :], dm[:, :, :], -1.0, None, ALU.add))
            for k in range(TOPK):
                me.mark(V.tensor_tensor(ohd[:, :, k, :], oh[:, :, k, :],
                                        kf[:, :].rearrange("p (i k) -> p i k", i=LT)[:, :, k:k + 1]
                                        .broadcast_to([P, LT, E]), ALU.mult))
            me.wait()
            me.mark(V.tensor_reduce(kk[:, :, :], ohd.rearrange("p i k e -> p i e k"), AX_X, ALU.add))
            me.link(V.tensor_tensor(io_b, io_b, cum.unsqueeze(1).broadcast_to([P, NBT, E]), ALU.is_ge))
            me.link(V.tensor_reduce(bef[:, :], io_b, AX_X, ALU.add))
            me.link(V.tensor_scalar(bef[:, :], bef[:, :], float(E - 1), None, ALU.min))
            me.mark(V.tensor_copy(tab_e[:, :], bef[0:1, :]))
            me.mark(V.memset(tab_nf[:, :], 1.0))
            me.wait()
            me.mark(V.tensor_tensor(tab_nf[:, 1:NBT], bef[0:1, 1:NBT], bef[0:1, 0:NBT - 1], ALU.not_equal))
            me.mark(V.tensor_copy(tab_n[:, :], cum[0:1, E - 1:E]))
            me.wait()
            me.link(V.tensor_copy(tab_new[:, :], tab_nf[:, :]))
            dve.sem_inc(S["tab_ok"], 1)
            n_blocks = dve.value_load(tab_n[0:1, 0:1], min_val=1, max_val=NB_MAX)

            def one_hot(b):
                e = dve.value_load(tab_e[0:1, bass.ds(b, 1)] if not isinstance(b, int) else tab_e[0:1, b:b + 1],
                                   min_val=0, max_val=E - 1)
                for i in range(LT):
                    V.tensor_scalar(pt[:, i, :], slot_io[:, :], dm[:, i, bass.ds(e, 1)], None, ALU.is_equal)
                V.tensor_copy(ids[:, :, 2:3], kk[:, :, bass.ds(e, 1)]).then_inc(S["pt_ok"], 1)
                me.mark(V.tensor_scalar(slot_io[:, :], slot_io[:, :], float(P), None, ALU.add))

            def index():
                col = lambda n: idx_f[:, n:n + 1]
                me.link(V.tensor_copy(idx_f[:, 0:3], ps[0][:, 0:3]))
                me.mark(V.scalar_tensor_tensor(col(3), col(1), float(P), col(0), ALU.mult, ALU.add))
                me.link(V.tensor_scalar(col(4), col(2), 0.0, 8192.0, ALU.is_equal, ALU.mult))
                me.link(V.tensor_tensor(col(3), col(3), col(4), ALU.add))
                me.mark(V.tensor_copy(tok_next[:, :], col(3)))
                me.link(V.tensor_scalar(col(5), col(2), float(LAT), float(-LAT), ALU.mult, ALU.add))
                V.tensor_tensor(row_next[:, :], col(5), col(3), ALU.add).then_inc(S["idx_ok"], 1)

            def lo_part(b, j):
                kind, _, k = order[j]
                dve.wait_ge(S["hi_ok"], b * NS + (NS + split_no[j] + 1))
                src = w1s[:, k, :] if kind == "w1" else w2s[:, 2 * k:2 * k + 2, :].rearrange("p a n -> p (a n)")
                V.tensor_tensor(w_lo[slot_of[j]][:, :], src, w_hi[slot_of[j]][:, :].bitcast(F32),
                                ALU.subtract).then_inc(S["lo_ok"], 1)

            def less(out, bank, hi, half, done, skip=()):
                ks = [k for k in range(4 * half, 4 * half + 4) if k not in skip]
                step = ks[1] - ks[0]
                assert ks == list(range(ks[0], ks[-1] + 1, step))

                def cols_of(t, k0):
                    return t.rearrange("p (k n) -> p k n", n=P)[:, ks[0] - k0:ks[-1] - k0 + 1:step, :]

                V.tensor_tensor(cols_of(out[:, :], 0), cols_of(bank[:, :], 4 * half),
                                cols_of(hi[:, :].bitcast(F32), 0), ALU.subtract).then_inc(done, 1)

            one_hot(0)
            dve.wait_ge(S["xi_ps"], 1)
            index()
            me.wait()
            one_hot(1)
            dve.wait_ge(S["xi_ps"], 2)
            dve.wait_ge(S["mid_ok"], 1)
            index()
            me.wait()
            one_hot(2)
            dve.sem_inc(S["lo_ok"], split_no[MID])
            for half in range(2):
                dve.wait_ge(S["xth_ok"], half + 1)
                less(XTl, ps[half], XTh, half, S["xtl_ok"], whole_k)
            lo_part(-1, MID)
            dve.wait_ge(S["lo_ok"], split_no[MID] + 1)
            dve.sem_inc(S["lo_ok"], NS - split_no[MID] - 1)
            base2 = me.base + me.count
            n_in = 9
            with dve.Fori(0, n_blocks) as b:
                me.base, me.count = base2 + n_in * b, 0
                lo_part(b, EARLY[0])
                dve.wait_ge(S["xi_ps"], b + 3)
                dve.wait_ge(S["mid_ok"], b + 2)
                index()
                dve.wait_ge(S["w_used"], b * NC + (W1C + 1))
                V.tensor_scalar(sel[:, :], bef[0:96, bass.ds(b, 1)].broadcast_to([96, P]), pmod[0:96, :], None,
                                ALU.is_equal).then_inc(S["sel_ok"], 1)
                for j in range(EARLY[1], MID + 1):
                    lo_part(b, j)
                dve.wait_ge(S["xth_ok"], b * 2 + 3)
                less(XTl, ps[0], XTh, 0, S["xtl_ok"], whole_k)
                for n in range(2):
                    c0 = slice(n * 512, n * 512 + 512)
                    dve.wait_ge(S["lin_ok"], b * 2 + (n + 1))
                    me.link(V.tensor_scalar(act_a[:, c0], lin[:, c0], 1.0 + LIMIT, 1.0 - LIMIT, ALU.min, ALU.max))
                    dve.wait_ge(S["sig_ok"], b * 2 + (n + 1))
                    V.scalar_tensor_tensor(act_a[:, c0], ps[2 + n][:, :], LIMIT, act_a[:, c0], ALU.min,
                                           ALU.mult).then_inc(S["glu_ok"], 1)
                for n in range(2):
                    c0 = slice(n * 512, n * 512 + 512)
                    dve.wait_ge(S["glu_ok"], b * 2 + (n + 1))
                    V.scalar_tensor_tensor(act_a[:, c0], sig[:, c0], SIG_MAX, act_a[:, c0], ALU.min,
                                           ALU.mult).then_inc(S["act_ok"], 1)
                lo_part(b, W1C)
                dve.wait_ge(S["xth_ok"], b * 2 + 4)
                less(XTl, ps[1], XTh, 1, S["xtl_ok"], whole_k)
                for half in range(2):
                    dve.wait_ge(S["ath_ok"], b * 2 + (half + 1))
                    less(aTl, ps[6 + half], aTh, half, S["atl_ok"])
                lo_part(b, W1C + 1)
                lo_part(b, W1C + 2)
                me.wait()
                one_hot(b + 3)
                lo_part(b, W1C + 3)
                assert me.count == n_in, me.count

            me = Steps(dve, S["fin_s"])

            def finish(i):
                dve.wait_ge(S["fin_std"], i + 1)
                me.link(V.reciprocal(rst[:, 12 + i:13 + i], rst[:, 12 + i:13 + i]))
                V.scalar_tensor_tensor(x_sb[:, i, :], x_sb[:, i, :], rst[:, 12 + i:13 + i], fin_row,
                                       ALU.mult, ALU.mult).then_inc(S["fin_ok"], 1)

            dve.wait_ge(S["ld_rows"], 16)
            for i in range(LT):
                dve.wait_ge(gath[i], 16)
                y0 = ygat[:, i, 0, :]
                me.link(V.tensor_scalar(y0, y0, wk[:, i, 0:1], None, ALU.mult))
                for k in range(1, TOPK):
                    me.link(V.scalar_tensor_tensor(y0, ygat[:, i, k, :], wk[:, i, k:k + 1], y0,
                                                   ALU.mult, ALU.add))
                me.link(V.tensor_tensor(y0, y0, g2_row, ALU.mult))
                V.tensor_tensor(x_sb[:, i, :], x_sb[:, i, :], y0, ALU.add).then_inc(S["fin_sq"], 1)
                if i:
                    finish(i - 1)
            finish(LT - 1)

        @block.tensor
        def _(pe):
            mm, tr = nc.tensor.matmul, nc.tensor.transpose
            pe.wait_ge(S["ld_vec"], 16 * 9)
            pe.wait_ge(S["consts"], 4)
            tr(ps[0][:, 0:112], vecs, ident[0:112, 0:112]).then_inc(S["vecs_ps"], 1)
            pe.wait_ge(S["csil_ok"], 1)
            pe.wait_ge(ld_mw, 16 * DK)
            for m in range(16):
                for k in range(DK):
                    last = mm(ps[1][:, 2 * m:2 * m + 2], mwc[:, k, m * P:(m + 1) * P], csil[:, k, :],
                              start=(k == 0), stop=(k == DK - 1))
            last.then_inc(S["modc_ps"], 1)
            pe.wait_ge(S["xn_ok"], TT)
            for j in range(DK):
                for lat in (True, False):
                    if j >= 3:
                        pe.wait_ge(S["aT_lat_ok" if lat else "aT_ctx_ok"], j - 2)
                    bank = ps[(2 if lat else 5) + j % 3]
                    tiles = range(CT, TT) if lat else range(CT)
                    for n, i in enumerate(tiles):
                        last = tr(bank[:, n * P:(n + 1) * P], xv[:, i, j * P:(j + 1) * P], ident[:, :])
                    last.then_inc(S["xT_ps"], 1)
            pe.wait_ge(S["ld_wv"], 16 * DK)
            pe.wait_ge(S["aT_lat_ok"], DK)
            pe.wait_ge(S["aT_ctx_ok"], DK)
            for n in range(2 * TT):
                if n >= 4:
                    pe.wait_ge(S["v_ev_a" if n % 2 == 0 else "v_ev_d"], (n - 4) // 2 + 1)
                i = n // 2
                for k in range(DK):
                    last = mm(ps[n % 4][:, :], aT[:, k, i * P:(i + 1) * P],
                              w_sq[:, k, (n % 2) * 512:(n % 2) * 512 + 512], start=(k == 0), stop=(k == DK - 1))
                last.then_inc(S["v_ps"], 1)
            pe.wait_ge(S["v_ev_a"], TT)
            pe.wait_ge(S["v_ev_d"], TT)

            def section(s, bank, done):
                for k in range(DK):
                    last = mm(bank[:, :], wh[:, s, k, :], aT[:, k, CTX:TOK], start=(k == 0), stop=(k == DK - 1))
                last.then_inc(done, 1)

            def scores(h1):
                pe.wait_ge(S["ew_ok"], h1)
                pe.wait_ge(S["rs_ok"], 2 * h1 - 1)
                for d in range(2):
                    for ch in range(NCH):
                        r = slice((ch % 2) * CH, (ch % 2) * CH + CH)
                        cs = slice(ch * CH, (ch + 1) * CH)
                        col = d * 256 + (ch // 2) * CH
                        mm(ps[4][r, col:col + CH], ke[d][:, cs], qe[d][:, cs], start=True, stop=True)
                for d in range(2):
                    for n in range(LT):
                        tr(ps[5 if d == 0 else 7][:, n * P:(n + 1) * P], ko[d][:, CTX + n * P:CTX + (n + 1) * P],
                           ident[:, :])
                    for n in range(CT):
                        last = tr(ps[6][:, (d * CT + n) * P:(d * CT + n + 1) * P], ko[d][:, n * P:(n + 1) * P],
                                  ident[:, :])
                last.then_inc(S["a_ps"], 1)

            def outer(h1, zc_seen):
                pe.wait_ge(S["koT_ok"], h1)
                pe.wait_ge(S["pm_ok"], h1)
                pe.wait_ge(S["zc_sig"], zc_seen)
                for d in range(2):
                    for i in range(CT):
                        mm(ps[4][:, d * P:(d + 1) * P], koT[d][:, i, :], v_h[:, i, :], start=(i == 0),
                           stop=(i == CT - 1))
                    for ch in range(NCH):
                        if ch == (NCH - 1 if d == 0 else 0):
                            continue
                        r = slice((ch % 2) * CH, (ch % 2) * CH + CH)
                        bank = ps[(5, 6)[ch % 2] if d == 0 else (7, 2)[ch % 2]]
                        last = mm(bank[:, (ch // 2) * P:(ch // 2 + 1) * P], koT[d][r, CT + ch // 2, :],
                                  v_h[r, CT + ch // 2, :], start=True, stop=True)
                last.then_inc(S["b_ps"], 1)

            def outputs(h1):
                pe.wait_ge(S["st_ok"], h1)
                for d in range(2):
                    for n in range(LT):
                        mm(ps[5][:, n * P:(n + 1) * P], v_h[:, CT + n, :], pm[d][:, n, :],
                           start=(d == 0 and n == 0), stop=False, skip_group_check=True)
                for d in range(2):
                    for ch in range(NCH):
                        last = mm(ps[5][:, ch * CH:(ch + 1) * CH], st[d][:, ch, :],
                                  lfq[d][:, CTX + ch * CH:CTX + (ch + 1) * CH], start=False,
                                  stop=(d == 1 and ch == NCH - 1), skip_group_check=True)
                last.then_inc(S["o_ps"], 1)
                pe.wait_ge(S["sq_ok"], h1)
                mm(ps[6][:, :], ones[:, :], sq, start=True, stop=True).then_inc(S["ss_ps"], 1)

            def head(h, prev):
                for s in range(2):
                    pe.wait_ge(ld_wh[s], 16 * h + 16)
                if prev is not None:
                    pe.wait_ge(S["zc_sig"], h)
                for s in range(2):
                    for k in range(DK):
                        last = mm(ps[2][:, s * CTX:(s + 1) * CTX], wh[:, s, k, :], aT[:, k, 0:CTX],
                                  start=(k == 0), stop=(k == DK - 1))
                last.then_inc(S["zc_ps"], 1)
                if prev is not None:
                    pe.wait_ge(S["gs_ok"], h)
                section(0, ps[0], S["zf_ps"])
                if prev is not None:
                    pe.wait_ge(S["zb_sig"], h)
                section(1, ps[1], S["zb_ps"])
                if prev is not None:
                    scores(h)
                pe.wait_ge(ld_wh[2], 16 * h + 16)
                if prev is not None:
                    pe.wait_ge(S["qs_ok"], h)
                section(2, ps[3], S["q_ps"])
                if prev is not None:
                    outer(h, h + 1)
                pe.wait_ge(ld_wh[3], 16 * h + 16)
                pe.wait_ge(S["zf_sig"], h + 1)
                section(3, ps[0], S["g_ps"])
                if prev is not None:
                    outputs(h)

            head(0, None)
            with pe.Fori(1, H) as h:
                head(h, 1)
            scores(H)
            outer(H, H)
            outputs(H)

            pe.wait_ge(S["csb_ok"], 1)
            pe.wait_ge(S["rs_ok"], 2 * H)
            pe.wait_ge(S["gs_ok"], H)
            for k in range(DK):
                pe.wait_ge(ld_mwr[k % 3], 16 * (k // 3 + 1))
                for n in range(8):
                    last = mm(ps[n][:, :], csb[:, k, :], mwr[k % 3][:, n * 512:(n + 1) * 512],
                              start=(k == 0), stop=(k == DK - 1))
                last.then_inc(S["mwr_used"], 1)
            pe.wait_ge(S["rows_ok"], 1)
            pe.wait_ge(S["og_ok"], H)
            pe.wait_ge(S["ld_wout"], 16 * DK)
            for j in range(2 * LT):
                i, n = j // 2, j % 2
                for k in range(DK):
                    last = mm(ps[j][:, :], ogT[:, k, i * P:(i + 1) * P], w_sq[:, k, n * 512:(n + 1) * 512],
                              start=(k == 0), stop=(k == DK - 1))
                last.then_inc(S["yo_ps"], 1)
            pe.wait_ge(S["f_ok"], LT)
            for j in range(DK):
                for i in range(LT):
                    last = tr(ps[j][:, i * P:(i + 1) * P], f_sb[:, i, j * P:(j + 1) * P], ident[:, :])
                last.then_inc(S["fT_ps"], 1)
            pe.wait_ge(S["fT_ok"], DK)
            pe.wait_ge(S["ld_rw"], 32)
            for i in range(LT):
                for k in range(DK):
                    last = mm(ps[0][:, i * E:(i + 1) * E], ogT[:, k, i * P:(i + 1) * P], rw[:, k, :],
                              start=(k == 0), stop=(k == DK - 1))
            last.then_inc(S["lg_ps"], 1)
            pe.wait_ge(S["msk_ok"], 1)
            for i in range(LT):
                for i0 in range(i + 1):
                    mm(ps[1][:, i * E:(i + 1) * E], (tri if i0 == i else ones)[:, :], msk[:, i0, :],
                       start=(i0 == 0), stop=(i0 == i))
            for i in range(LT):
                last = mm(ps[1][:, LT * E:(LT + 1) * E], ones[:, :], msk[:, i, :], start=(i == 0),
                          stop=(i == LT - 1))
            last.then_inc(S["pos_ps"], 1)

            pe.wait_ge(S["tab_ok"], 1)
            n_blocks = pe.value_load(tab_n[0:1, 0:1], min_val=1, max_val=NB_MAX)

            def slots_of(count):
                pe.wait_ge(S["pt_ok"], count)
                for i in range(LT):
                    last = mm(ps[0][:, 0:P], pt[:, i, :], ids[:, i, :], start=(i == 0), stop=(i == LT - 1))
                last.then_inc(S["xi_ps"], 1)

            def transpose_x(count):
                pe.wait_ge(S["idx_ok"], count + 1)
                pe.wait_ge(S["xg_ld"], count * 16)
                for k in range(DK):
                    last = tr(ps[k // 4][:, (k % 4) * P:(k % 4 + 1) * P], xg[:, k * P:(k + 1) * P], ident[:, :])
                last.then_inc(S["xt_ps"], 1)

            def three(bank, th, tl, k, slot, c0, start, stop):
                kc = slice(k * P, (k + 1) * P)
                mm(bank, th[:, kc], w_hi[slot][:, c0], start=start, stop=False)
                mm(bank, th[:, kc], w_lo[slot][:, c0], start=False, stop=False)
                return mm(bank, tl[:, kc], w_hi[slot][:, c0], start=False, stop=stop)

            def z_chunk(b, j, free=False):
                _, ahead, k = order[j]
                if j in WHOLE:
                    pe.wait_ge(ld_w1[k], b * 16 + 16 * (1 + ahead))
                else:
                    pe.wait_ge(S["lo_ok"], b * NS + (NS + split_no[j] + 1))
                for n in (2, 0, 3, 1):
                    c0 = slice(n * 512, n * 512 + 512)
                    if free:
                        pe.wait_ge(S["lin_ok" if n >= 2 else "glu_ok"], b * 2 + (n % 2 + 1))
                    if j in WHOLE:
                        last = mm(ps[2 + n][:, :], XT[:, k * P:(k + 1) * P], w1s[:, k, c0], start=(k == 0),
                                  stop=False)
                    else:
                        last = three(ps[2 + n][:, :], XTh, XTl, k, slot_of[j], c0, start=(k == 0), stop=False)
                last.then_inc(S["w_used"], 1)

            slots_of(1)
            pe.wait_ge(S["idx_ok"], 1)
            slots_of(2)
            transpose_x(1)
            pe.sem_inc(S["w_used"], MID)
            pe.wait_ge(S["xtl_ok"], 1)
            for j in range(MID, MID + AHEAD):
                z_chunk(-1, j)
            pe.wait_ge(S["w_used"], MID + AHEAD)
            pe.sem_inc(S["w_used"], W2C)
            pe.wait_ge(S["xtl_ok"], 2)
            with pe.Fori(0, n_blocks) as b:
                pe.wait_ge(S["xtl_ok"], b * 2 + 2)
                slots_of(b + 3)
                for j in range(MID):
                    if j == MID - 1:
                        transpose_x(b + 2)
                    z_chunk(b, j)
                pe.wait_ge(S["sel_ok"], b + 1)
                for n in range(4):
                    last = mm(ps[2 + n][:, :], sel[:, :], bias3[:, n * 512:(n + 1) * 512], start=False, stop=True)
                last.then_inc(S["z_ps"], 1)
                pe.wait_ge(S["xtl_ok"], b * 2 + 3)
                z_chunk(b, MID, free=True)
                z_chunk(b, MID + 1)
                pe.wait_ge(S["act_ok"], b * 2 + 2)
                pe.wait_ge(S["y_ok"], b + 1)
                for k in range(DK):
                    last = tr(ps[6 + k // 4][:, (k % 4) * P:(k % 4 + 1) * P], act_a[:, k * P:(k + 1) * P],
                              ident[:, :])
                last.then_inc(S["at_ps"], 1)
                z_chunk(b, MID + 2)
                pe.wait_ge(S["atl_ok"], b * 2 + 2)
                for n in range(2):
                    mm(ps[6 + n][:, :], sel[:, :], bias3[:, 2 * FF + n * 512:2 * FF + (n + 1) * 512],
                       start=True, stop=False)
                for m in range(W2C):
                    j = W1C + m
                    pe.wait_ge(S["lo_ok"], b * NS + (NS + split_no[j] + 1))
                    for a in range(2):
                        for n in range(2):
                            last = three(ps[6 + n][:, :], aTh, aTl, 2 * m + a, slot_of[j],
                                         slice(a * 1024 + n * 512, a * 1024 + n * 512 + 512),
                                         start=False, stop=(m == W2C - 1 and a == 1))
                    last.then_inc(S["w_used"], 1)


INPUTS = ["x", "c", "ctx", "c_ctx", "mod_w", "mod_b", "norm1_g", "norm2_g", "hg_w_in", "hg_lb_logits",
          "hg_norm_g", "hg_w_out", "router_w", "router_b", "moe_w1", "moe_b1", "moe_w2", "moe_b2", "final_g"]
SHAPES = {"x": [LAT, D], "c": [1, D], "ctx": [CTX, D], "mod_w": [D, 6 * D], "mod_b": [6 * D],
          "norm1_g": [D], "norm2_g": [D], "hg_w_in": [D, 5 * D], "hg_norm_g": [D], "hg_w_out": [D, D],
          "router_w": [D, E], "router_b": [E], "moe_w1": [E * D, 2 * FF], "moe_b1": [E, 2 * FF],
          "moe_w2": [E * FF, D], "moe_b2": [E, D]}


def kernel(**inputs):
    import concourse.bacc as bacc
    from concourse.bass_utils import run_bass_kernel_spmd

    nc = bacc.Bacc("TRN2", target_bir_lowering=False, num_devices=1, dynamic_dma_scratch_size=4096)
    arrays, args = {}, []
    for name in INPUTS:
        a = np.ascontiguousarray(inputs[name])
        a = a.reshape(SHAPES.get(name, a.shape))
        arrays[f"in_{name}"] = a
        args.append(nc.dram_tensor(f"in_{name}", a.shape, mybir.dt.from_np(a.dtype), kind="ExternalInput").ap())
    args.append(nc.dram_tensor("out", [LAT, D], F32, kind="ExternalOutput").ap())
    build(nc, *args)
    r = run_bass_kernel_spmd(nc, [arrays], core_ids=[0])
    return r.results[0]["out"].reshape(1, LAT, D)
```

```python
import numpy as np
import concourse.bass as bass
from concourse import mybir
from contextlib import ExitStack

F32 = mybir.dt.float32
BF16 = mybir.dt.bfloat16
I32 = mybir.dt.int32
U32 = mybir.dt.uint32
F32R = mybir.dt.float32r
ALU = mybir.AluOpType
ACT = mybir.ActivationFunctionType
AX_X = mybir.AxisListType.X

P = 128
D = 1024
DK = D // P
LAT, CTX = 512, 256
TOK = LAT + CTX
LT, CT, TT = LAT // P, CTX // P, TOK // P
CH = 64
NCH = LAT // CH
E, TOPK = 32, 4
FF = 1024
NB_MAX = LAT * TOPK // P + E
NBT = NB_MAX + 3
EPS = 1e-6
N_CONST = 15
LIMIT = 7.0
ALPHA = 1.702
SIG_MAX = float(1.0 / (1.0 + np.exp(-ALPHA * LIMIT)))
W1C, W2C = DK, DK // 2
NC = W1C + W2C
AHEAD = 3
UN = 2 * NC
SLOTS = 5
WHOLE = (6, 7)
NS = UN - 2 * len(WHOLE)
H = DK


class Steps:

    def __init__(self, engine, sem):
        self.engine, self.sem, self.count, self.base = engine, sem, 0, 0

    def mark(self, ins):
        ins.then_inc(self.sem, 1)
        self.count += 1
        return self.count

    def wait(self, count=None):
        self.engine.wait_ge(self.sem, self.base + (self.count if count is None else count))

    def link(self, ins):
        self.mark(ins)
        self.wait()


def build(nc, x, c, ctx_in, c_ctx, mod_w, mod_b, norm1_g, norm2_g, hg_w_in, hg_lb_logits, hg_norm_g,
          hg_w_out, router_w, router_b, moe_w1, moe_b1, moe_w2, moe_b2, final_g, out):
    frows = nc.dram_tensor("frows", [LAT, D], F32, kind="Internal").ap()
    yrows = nc.dram_tensor("yrows", [TOPK * LAT, D], F32, kind="Internal").ap()
    with ExitStack() as stack:
        place = {}

        def sb(name, shape, dt=F32):
            place[name] = -(-nc.sbuf_base // 32) * 32
            return stack.enter_context(nc.sbuf_tensor(name, shape, dt))

        def sem(name):
            return stack.enter_context(nc.semaphore(name))

        arena = sb("arena", [P, 24576])
        x_sb = sb("x_sb", [P, LT, D])
        aT_t = sb("aT_t", [P, DK * TOK])
        xv_t = sb("xv_t", [P, TT * D])
        ring_t = sb("ring_t", [P, 4096])
        ogT = sb("ogT", [P, DK, LAT])
        rows2 = sb("rows2", [P, 2 * D])
        g2_row, fin_row = rows2[:, 0:D], rows2[:, D:2 * D]

        mwc = arena[:, 0:16384].rearrange("p (k n) -> p k n", k=DK)
        w_sq = arena[:, 16384:24576].rearrange("p (k n) -> p k n", k=DK)
        aT_ctx = rows2[:, :].rearrange("p (k t) -> p k t", k=DK)
        f_sb = aT_t[:, 0:LT * D].rearrange("p (i n) -> p i n", i=LT)
        xv = xv_t[:, :].rearrange("p (i n) -> p i n", i=TT)
        wh = ring_t[:, :].rearrange("p (s k n) -> p s k n", s=4, k=DK)

        at = [0]

        def take(n):
            at[0] += n
            return arena[:, at[0] - n:at[0]]

        sgk = [take(TOK) for _ in range(2)]
        q_in = [take(TOK) for _ in range(2)]
        bc = [take(TOK) for _ in range(2)]
        qe = [take(LAT) for _ in range(2)]
        ke = [take(LAT) for _ in range(2)]
        ko = [take(TOK) for _ in range(2)]
        qs, sgq, sgg, gs = (take(LAT) for _ in range(4))
        pm = [take(LAT).rearrange("p (a t) -> p a t", a=LT) for _ in range(2)]
        st = [take(NCH * P).rearrange("p (c v) -> p c v", c=NCH) for _ in range(2)]
        koT = [take(TOK).rearrange("p (i k) -> p i k", i=TT) for _ in range(2)]
        v_h = take(TOK).rearrange("p (i v) -> p i v", i=TT)
        assert at[0] <= 16384
        osb, sq = rows2[:, 0:LAT], rows2[:, LAT:2 * LAT]

        g1_row, sh2_row, G2_row, n2_row = (arena[:, i * D:(i + 1) * D] for i in range(4))
        mb_rows = arena[:, 4096:8192]
        mwe = [ring_t[:, :].rearrange("p (k n) -> p k n", n=D), aT_t[:, 0:4 * D].rearrange("p (k n) -> p k n", n=D)]
        mwr = [ring_t[:, 0:3 * D], aT_t[:, 3 * D:6 * D], arena[:, 8 * D:11 * D], arena[:, 12 * D:15 * D]]

        cols = sb("cols", [P, 112])
        csil = sb("csil", [P, DK, 2])
        csb = rows2[:, D:2 * D].rearrange("p (k m) -> p k m", k=DK)
        sc16 = sb("sc16", [P, 16])
        modc = sb("modc", [P, 16, 2])
        G1 = sb("G1", [P, DK, 2])
        stat = sb("stat", [P, 16])
        rst = sb("rst", [P, 16])
        eps_t = sb("eps_t", [P, 1])
        junk = sb("junk", [P, 1])
        hcols = sb("hcols", [P, H, 8])
        hc = sb("hc", [P, 8])
        ed = sb("ed", [P, 2, NCH])
        ident = sb("ident", [P, P])
        ones = sb("ones", [P, P])
        tri = sb("tri", [P, P])
        tri16, ones16 = sb("tri16", [P, P], BF16), sb("ones16", [P, P], BF16)
        msk16 = sb("msk16", [P, LT, E], BF16)
        res = sb("res", [P, 2, TOK], BF16)
        mk = sb("mk", [P, 2, LT, CH], mybir.dt.uint8)
        mkf = xv_t[:, 2048:2048 + 512].rearrange("p (d a t) -> p d a t", d=2, a=LT)

        rw = sb("rw", [P, DK, E])
        rb_row = sb("rb_row", [P, E])
        at2 = [0]

        def rtake(n):
            at2[0] += n
            return ring_t[:, at2[0] - n:at2[0]]

        lg = rtake(LT * E).rearrange("p (i e) -> p i e", i=LT)
        v8 = rtake(LT * 8).rearrange("p (i e) -> p i e", i=LT)
        i8 = rtake(LT * 8).rearrange("p (i e) -> p i e", i=LT).bitcast(U32)
        i8f = rtake(LT * 8).rearrange("p (i e) -> p i e", i=LT)
        oh = rtake(LT * TOPK * E).rearrange("p (i k e) -> p i k e", i=LT, k=TOPK)
        ohd = rtake(LT * TOPK * E).rearrange("p (i k e) -> p i k e", i=LT, k=TOPK)
        msk = rtake(LT * E).rearrange("p (i e) -> p i e", i=LT)
        io_e = rtake(E)
        ew4 = rtake(LT * TOPK).rearrange("p (i k) -> p i k", i=LT)
        es = rtake(LT)
        cnt, nblk, nb1, cum, pst, onesE = (rtake(E) for _ in range(6))
        io_b = rtake(NBT * E).rearrange("p (b e) -> p b e", e=E)
        assert at2[0] <= 4096
        kk = sb("kk", [P, LT, E])
        kf = sb("kf", [P, LT * TOPK])
        idx_f = sb("idx_f", [P, 8])
        row_next, row_3, row_2, row_1, tok_next, zero_i, zero_j, zero_k = (
            sb(n, [P, 1], U32) for n in ("row_next", "row_3", "row_2", "row_1", "tok_next", "zero_i", "zero_j", "zero_k"))
        wk = sb("wk", [P, LT, TOPK])
        dm = sb("dm", [P, LT, E])
        bef = sb("bef", [P, NBT])
        tab_e = sb("tab_e", [1, NBT], I32)
        tab_new = sb("tab_new", [1, NBT], I32)
        tab_nf = sb("tab_nf", [1, NBT])
        tab_n = sb("tab_n", [1, 1], I32)
        slot_io = sb("slot_io", [P, P])
        pt = sb("pt", [P, LT, P], BF16)
        ids = sb("ids", [P, LT, P], BF16)
        pmod = sb("pmod", [P, 1])
        sel = sb("sel", [96, P], BF16)
        bias3 = sb("bias3", [96, 3 * FF], BF16)
        b_raw = aT_t[0:96, 0:3 * FF]

        w1s = arena[:, 0:16384].rearrange("p (k n) -> p k n", k=DK)
        w2s = arena[:, 16384:24576].rearrange("p (k n) -> p k n", k=DK)

        def at_place(name, base, offset, n):
            return nc.alloc_sbuf_tensor_at(name, [P, n], F32R, offset=place[base] + 4 * offset)

        aT_hi, aT_lo = at_place("aT_hi", "aT_t", 0, DK * LAT), at_place("aT_lo", "x_sb", 0, DK * LAT)
        a_tmp = ogT
        aTc_hi = at_place("aTc_hi", "aT_t", DK * LAT, DK * CTX)
        aTc_lo = [at_place(f"aTc_lo{k}", "bias3", k * CTX, CTX) for k in range(6)] \
            + [at_place("aTc_lo6", "pt", 0, CTX), at_place("aTc_lo7", "ids", 0, CTX)]
        wv_hi, wv_lo = at_place("wv_hi", "arena", 0, DK * D), at_place("wv_lo", "arena", DK * D, DK * D)
        wh_hi = [at_place(f"wh_hi{s}", "arena", 16384 + s * 2 * D, D) for s in range(4)]
        wh_lo = [at_place(f"wh_lo{s}", "arena", 16384 + s * 2 * D + D, D) for s in range(4)]

        w_hi = [at_place(f"w_hi{i}", "aT_t", i * 1024, 1024) for i in range(5)]
        w_lo = [at_place(f"w_lo{i}", base, offset, 1024) for i, (base, offset) in enumerate(
            (("aT_t", 5120), ("ogT", 0), ("ogT", 1024), ("ogT", 2048), ("ogT", 3072)))]
        XTh, XTl, aTh, aTl = (at_place(n, "xv_t", i * 1024, 1024) for i, n in
                              enumerate(("XTh", "XTl", "aTh", "aTl")))
        XT = xv_t[:, 1024:2048]
        xg, act_a = (xv_t[:, 4096 + i * 1024:5120 + i * 1024] for i in range(2))
        y_sb, lin = (ring_t[:, 2048 + i * 1024:3072 + i * 1024] for i in range(2))
        sig = rows2[:, D:2 * D]
        ygat = arena[:, 0:16384].rearrange("p (i k n) -> p i k n", i=LT, k=TOPK)

        ps = [stack.enter_context(nc.psum_tensor(f"ps{i}", [P, 512], F32)) for i in range(8)]

        MID = W1C - AHEAD
        order = [("w1", 0, k) for k in range(AHEAD, W1C)] + [("w1", 1, k) for k in range(AHEAD)] \
            + [("w2", 0, m) for m in range(W2C)]
        assert all(order[j][0] == "w1" for j in WHOLE)
        whole_k = sorted(order[j][2] for j in WHOLE)
        split_no = {(j, u): n for n, (j, u) in enumerate((j, u) for j in range(NC) if j not in WHOLE
                                                         for u in range(2))}
        assert len(split_no) == NS and NS % SLOTS == 0
        slot_of = {ju: n % SLOTS for ju, n in split_no.items()}
        place_of = {(kind, k): (j, ahead) for j, (kind, ahead, k) in enumerate(order)}
        EARLY = (0, 1)

        def slot_free(j, u):
            n = split_no[j, u] - SLOTS
            j0, u0 = next(ju for ju, m in split_no.items() if m == n % NS)
            return 2 * j0 + u0 + 1 - (UN if n < 0 else 0)

        def half_of(j, u):
            kind, _, k = order[j]
            return w1s[:, k, (1 - u) * 1024:(2 - u) * 1024] if kind == "w1" else w2s[:, 2 * k + u, :]

        names = """lbx_ok lbe_ok dve_gla dve_ew fin_s ld_vec ld_x ld_ctx ld_wv ld_wout ld_rw ld_rows ld_mb consts pool_s dve_s act_s
        vecs_ps cols_ok c_sig csil_ok modr_ps modr_ok modc_ps modc_ok stdev_ok xn_ok xT_ps aT_lat_ok aT_ctx_ok
        v_ps v_ev_a v_ev_d ah_ok al_ok wvh_ok wvl_ok whh_ok whl_ok gm_ok
        zc_ps zf_ps zb_ps q_ps g_ps a_ps b_ps o_ps ss_ps
        zc_sig zf_sig zb_sig q_sig g_sig qs_ok gs_ok koT_ok pm_ok st_ok o_ev sq_ok rs_ok og_ok
        hc_ok lnf_ok b_ok bm_ok bo_ok exp_ok ew_ok
        rows_ok csb_ok mwr_used mwe_ps yo_ps h_ok stdev2_ok f_ok fT_ps fT_a fT_d rows_ev lg_ps
        e_v_ok e_w_ok msk_ok cnt_ps pos_ps tab_ok
        frow_st pt_ok xi_ps idx_ok mid_ok xg_ld xt_ps xth_ok xtl_ok z_ps lin_ok sig_ok glu_ok act_ok at_ps
        ath_ok atl_ok y_ok y_st y_free y0_ok rot hi_ok lo_ok w_used sel_ok ld_br ld_e0 arena_free fin_sq fin_std fin_ok out_st""".split()
        S = {n: sem(n) for n in names}
        ld_mw = [sem(f"ld_mw{k}") for k in range(DK)]
        ld_wh = [sem(f"ld_wh{s}") for s in range(4)]
        sec_done = [S["zf_ps"], S["zb_ps"], S["q_ps"], S["g_ps"]]
        ld_mwe = [sem(f"ld_mwe{s}") for s in range(2)]
        ld_mwr = [sem(f"ld_mwr{s}") for s in range(4)]
        gath = [sem(f"gath{i}") for i in range(LT)]
        ld_w1 = [sem(f"ld_w1_{k}") for k in range(DK)]
        ld_w2 = [sem(f"ld_w2_{k}") for k in range(4)]

        block = stack.enter_context(nc.Block())
        vecs = ring_t[0:112, 0:P]
        mod2 = rows2[0:2, :]
        SEC = [2, 3, 0, 4]

        w_in_s = hg_w_in.rearrange("(k p) n -> p k n", p=P)

        def vrow(v):
            return v.rearrange("(j p) -> j p", p=P)

        @block.sync
        def _(sp):
            row = 0
            for v in (c[0], c_ctx, mod_b, norm1_g, hg_lb_logits[0, 0], hg_lb_logits[0, 1],
                      hg_lb_logits[1, 0], hg_lb_logits[1, 1], hg_norm_g):
                n = v.shape[0] // P
                sp.dma_start(ring_t[row:row + n, 0:P], vrow(v)).then_inc(S["ld_vec"], 16)
                row += n
            assert row == 112
            for k in range(DK):
                if k == 2:
                    sp.dma_start(x_sb[:, :, :], x.rearrange("(i p) n -> p i n", p=P)).then_inc(S["ld_x"], 16)
                if k == 3:
                    sp.dma_start(xv[:, 0:CT, :], ctx_in.rearrange("(i p) n -> p i n", p=P)
                                 ).then_inc(S["ld_ctx"], 16)
                sp.dma_start(mwc[:, k, :], mod_w[k * P:(k + 1) * P, 0:2 * D]).then_inc(ld_mw[k], 16)
            for k in range(DK):
                sp.dma_start(w_sq[:, k, :], hg_w_in[k * P:(k + 1) * P, D:2 * D]).then_inc(S["ld_wv"], 16)
            sp.dma_start(rw[:, :, :], router_w.rearrange("(k p) e -> p k e", p=P)).then_inc(S["ld_rw"], 16)
            sp.dma_start(rb_row[:, :], router_b.partition_broadcast(P)).then_inc(S["ld_rw"], 16)

            sp.wait_ge(S["vecs_ps"], 1)
            for s in range(4):
                sp.dma_start(wh[:, s], w_in_s[:, :, SEC[s] * D:SEC[s] * D + P]).then_inc(ld_wh[s], 16)
            with sp.Fori(1, H) as h:
                for s in range(4):
                    sp.wait_ge(S["whl_ok"], h * 4 + (s - 3))
                    sp.dma_start(wh[:, s], w_in_s[:, :, bass.ds((h - 1) * P + (SEC[s] * D + P), P)]).then_inc(ld_wh[s], 16)
            sp.wait_ge(S["whl_ok"], 4 * H)
            for half in range(2):
                if half:
                    for s in range(4):
                        sp.wait_ge(sec_done[s], H)
                for k in range(4):
                    row = (4 * half + k) * P
                    sp.dma_start(mwe[half][:, k, :], mod_w[row:row + P, 2 * D:3 * D]).then_inc(ld_mwe[half], 16)
            sp.dma_start(x_sb[:, :, :], x.rearrange("(i p) n -> p i n", p=P)).then_inc(S["ld_x"], 16)
            for k in range(DK):
                if k == 0:
                    sp.wait_ge(S["mwe_ps"], 1)
                if k == 2:
                    for kw in range(DK):
                        sp.dma_start(w_sq[:, kw, :], hg_w_out[kw * P:(kw + 1) * P, :]).then_inc(S["ld_wout"], 16)
                    for part in range(3):
                        sp.dma_start(aT_t[part * E:(part + 1) * E, 0:2 * FF], moe_b1).then_inc(S["ld_br"], 16)
                        sp.dma_start(aT_t[part * E:(part + 1) * E, 2 * FF:3 * FF], moe_b2
                                     ).then_inc(S["ld_br"], 16)
                    sp.wait_ge(S["o_ps"], H)
                    sp.wait_ge(S["og_ok"], H)
                if k == 4:
                    sp.dma_start(mb_rows, mod_b[2 * D:6 * D].partition_broadcast(P)).then_inc(S["ld_mb"], 16)
                    sp.dma_start(n2_row, norm2_g.partition_broadcast(P)).then_inc(S["ld_mb"], 16)
                if k >= 4:
                    sp.wait_ge(S["mwr_used"], k - 3)
                sp.dma_start(mwr[k % 4], mod_w[k * P:(k + 1) * P, 3 * D:6 * D]).then_inc(ld_mwr[k % 4], 16)

            def load_w1(e, k, done):
                sp.dma_start(w1s[:, k, :], moe_w1[bass.ds(e * D + k * P, P), :]).then_inc(done, 16)

            def load_w2(e, k, done):
                sp.dma_start(w2s[:, 2 * k:2 * k + 2, :],
                             moe_w2[bass.ds(e * FF + 2 * k * P, 2 * P), :].rearrange("(a p) n -> p a n", p=P)
                             ).then_inc(done, 16)

            sp.wait_ge(S["rows_ev"], 8)
            for k in range(2, W1C):
                load_w1(0, k, S["ld_e0"])
            for i in range(LT):
                sp.wait_ge(S["f_ok"], i + 1)
                sp.dma_start(frows[i * P:(i + 1) * P, :], f_sb[:, i, :]).then_inc(S["frow_st"], 16)
            sp.wait_ge(S["arena_free"], 1)
            for k in range(2):
                load_w1(0, k, S["ld_e0"])
            for k in range(W2C):
                load_w2(0, k, S["ld_e0"])
            sp.wait_ge(S["tab_ok"], 1)
            n_blocks = sp.value_load(tab_n[0:1, 0:1], min_val=1, max_val=NB_MAX)
            e0 = sp.value_load(tab_e[0:1, 0:1], min_val=0, max_val=E - 1)
            sp.wait_ge(S["ld_e0"], 16 * NC)
            with sp.If(e0):
                for k in range(W1C):
                    load_w1(e0, k, ld_w1[k])
                for k in range(W2C):
                    load_w2(e0, k, ld_w2[k])
            with sp.Else():
                for k in range(W1C):
                    sp.sem_inc(ld_w1[k], 16)
                for k in range(W2C):
                    sp.sem_inc(ld_w2[k], 16)

            def chunk_read(b, kind, k):
                j, ahead = place_of[kind, k]
                if j in WHOLE:
                    sp.wait_ge(S["w_used"], b * UN + (2 * j + 2 - ahead * UN))
                else:
                    sp.wait_ge(S["lo_ok"], b * NS + (split_no[j, 1] + 1 - ahead * NS))

            chunks = [("w1", k) for k in range(W1C)] + [("w2", k) for k in range(W2C)]
            with sp.Fori(1, n_blocks) as b:
                e = sp.value_load(tab_e[0:1, bass.ds(b, 1)], min_val=0, max_val=E - 1)
                new = sp.value_load(tab_new[0:1, bass.ds(b, 1)], min_val=0, max_val=1)
                with sp.If(new):
                    for kind, k in chunks:
                        chunk_read(b, kind, k)
                        load_w1(e, k, ld_w1[k]) if kind == "w1" else load_w2(e, k, ld_w2[k])
                with sp.Else():
                    for kind, k in chunks:
                        chunk_read(b, kind, k)
                        sp.sem_inc(ld_w1[k] if kind == "w1" else ld_w2[k], 16)
            sp.wait_ge(S["lo_ok"], n_blocks * NS + (split_no[EARLY[-1], 1] + 1))
            for k in list(range(AHEAD)) + [order[j][2] for j in EARLY]:
                sp.sem_inc(ld_w1[k], 16)
            sp.wait_ge(S["y_st"], n_blocks * 16)
            for i in range(LT):
                if i == 1:
                    sp.dma_start(fin_row, final_g.partition_broadcast(P)).then_inc(S["ld_rows"], 16)
                sp.dma_start(ygat[:, i], yrows.rearrange("(k i p) n -> i p k n", k=TOPK, p=P)[i]
                             ).then_inc(gath[i], 16)
            for i in range(LT):
                sp.wait_ge(S["fin_ok"], i + 1)
                sp.dma_start(out[i * P:(i + 1) * P, :], x_sb[:, i, :]).then_inc(S["out_st"], 16)
            sp.wait_ge(S["out_st"], 16 * LT)

        @block.gpsimd
        def _(pool):
            me = Steps(pool, S["pool_s"])
            me.mark(pool.memset(ones[:, :], 1.0))
            me.mark(pool.memset(ident[:, :], 0.0))
            me.mark(pool.memset(mkf, 1.0))
            me.mark(pool.memset(res[:, :, :], 1.0))
            pool.memset(eps_t[:, :], EPS).then_inc(S["consts"], 1)
            me.wait()
            pool.affine_select(out=ident[:, :], in_=ident[:, :], compare_op=ALU.not_equal, fill=1.0, base=0,
                               pattern=[[-1, P]], channel_multiplier=1).then_inc(S["consts"], 1)
            pool.affine_select(out=tri[:, :], in_=ones[:, :], compare_op=ALU.is_gt, fill=0.0, base=0,
                               pattern=[[1, P]], channel_multiplier=-1).then_inc(S["consts"], 1)
            me.mark(pool.memset(res[:, 0, 0:1], 0.0))
            me.mark(pool.memset(res[:, 0, CTX:TOK:CH], 0.0))
            me.mark(pool.memset(res[:, 1, 0:LAT:CH], 0.0))
            me.mark(pool.memset(res[:, 1, LAT:LAT + 1], 0.0))
            me.wait()
            pool.wait_ge(S["consts"], 3)
            for half in range(2):
                r = slice(half * CH, (half + 1) * CH)
                me.link(pool.affine_select(out=mkf[r, 0], in_=mkf[r, 0], compare_op=ALU.is_ge, fill=0.0, base=0,
                                           pattern=[[0, LT], [1, CH]], channel_multiplier=-1))
                me.link(pool.affine_select(out=mkf[r, 1], in_=mkf[r, 1], compare_op=ALU.is_ge, fill=0.0, base=0,
                                           pattern=[[0, LT], [-1, CH]], channel_multiplier=1))
            me.wait()
            pool.tensor_copy(mk[:, :, :, :], mkf).then_inc(S["consts"], 1)
            pool.wait_ge(S["yo_ps"], 1)
            pool.iota(io_e, pattern=[[1, E]], base=0, channel_multiplier=0,
                      allow_small_or_imprecise_dtypes=True).then_inc(S["consts"], 1)
            pool.iota(io_b, pattern=[[1, NBT], [0, E]], base=0, channel_multiplier=0,
                      allow_small_or_imprecise_dtypes=True).then_inc(S["consts"], 1)
            pool.iota(slot_io[:, :], pattern=[[1, P]], base=0, channel_multiplier=0,
                      allow_small_or_imprecise_dtypes=True).then_inc(S["consts"], 1)
            pool.memset(onesE, 1.0).then_inc(S["consts"], 1)
            pool.iota(kf[:, :].rearrange("p (i k) -> p i k", i=LT), pattern=[[0, LT], [1, TOPK]], base=1,
                      channel_multiplier=0, allow_small_or_imprecise_dtypes=True).then_inc(S["consts"], 1)
            for part in range(3):
                pool.wait_ge(S["consts"], 9 + part)
                pool.iota(pmod[part * E:(part + 1) * E, :], pattern=[[0, 1]], base=0, channel_multiplier=1,
                          allow_small_or_imprecise_dtypes=True).then_inc(S["consts"], 1)
            pool.wait_ge(S["consts"], 12)
            me.mark(pool.memset(ids[:, :, :], 0.0))
            me.wait()
            pool.iota(ids[:, :, 0:1], pattern=[[0, LT], [0, 1]], base=0, channel_multiplier=1,
                      allow_small_or_imprecise_dtypes=True).then_inc(S["consts"], 1)
            pool.iota(ids[:, :, 1:2], pattern=[[1, LT], [0, 1]], base=0, channel_multiplier=0,
                      allow_small_or_imprecise_dtypes=True).then_inc(S["consts"], 1)
            pool.memset(zero_i[:, :], 0).then_inc(S["consts"], 1)
            pool.wait_ge(S["consts"], N_CONST)
            pool.wait_ge(S["tab_ok"], 1)
            n_blocks = pool.value_load(tab_n[0:1, 0:1], min_val=1, max_val=NB_MAX)
            pool.sem_inc(S["y_free"], 1)
            me.link(pool.memset(xg, 0.0))

            def move(out, in_):
                return pool.tensor_tensor(out=out[:, :], in0=in_[:, :], in1=zero_i[:, :], op=ALU.add)

            def gather():
                pool.indirect_dma_start(out=xg, out_offset=None, in_=frows,
                                        in_offset=bass.IndirectOffsetOnAxis(ap=tok_next[:, :], axis=0),
                                        bounds_check=LAT - 1, oob_is_err=False).then_inc(S["xg_ld"], 16)

            pool.wait_ge(S["frow_st"], 16 * LT)
            for n, row in enumerate((row_1, row_2)):
                pool.wait_ge(S["idx_ok"], n + 1)
                if n:
                    pool.wait_ge(S["xt_ps"], 2 * n)
                move(row, row_next)
                gather()
                pool.wait_ge(S["xg_ld"], 16 * n + 16)
                move(zero_j, zero_i).then_inc(S["mid_ok"], 1)
                pool.wait_ge(S["mid_ok"], n + 1)

            def round_(b, first):
                pool.wait_ge(S["idx_ok"], b + 3)
                pool.wait_ge(S["xt_ps"], b * 2 + 4)
                move(zero_j, zero_i)
                gather()
                if not first:
                    pool.wait_ge(S["y_st"], b * 16)
                    move(row_1, row_2).then_inc(S["rot"], 1)
                    pool.wait_ge(S["rot"], b * 2 - 1)
                    move(row_2, row_3).then_inc(S["rot"], 1)
                    pool.wait_ge(S["rot"], b * 2)
                    pool.sem_inc(S["y_free"], 1)
                pool.wait_ge(S["xg_ld"], b * 16 + 48)
                move(row_3, row_next).then_inc(S["mid_ok"], 1)
                pool.wait_ge(S["y_ok"], b + 2)
                pool.wait_ge(S["mid_ok"], b + 3)
                move(zero_k, zero_i)
                pool.indirect_dma_start(out=yrows, out_offset=bass.IndirectOffsetOnAxis(ap=row_1[:, :], axis=0),
                                        in_=y_sb, in_offset=None, bounds_check=TOPK * LAT - 1,
                                        oob_is_err=False).then_inc(S["y_st"], 16)

            round_(0, True)
            with pool.Fori(1, n_blocks) as b:
                round_(b, False)

        @block.scalar
        def _(act):
            me = Steps(act, S["act_s"])
            A = nc.scalar.activation
            act.wait_ge(S["cols_ok"], 1)
            A(sc16[:, :], cols[:, 0:16], ACT.Sigmoid).then_inc(S["c_sig"], 1)
            act.wait_ge(S["lbx_ok"], 1)
            A(hcols[:, :, 2:6], hcols[:, :, 2:6], ACT.Exp).then_inc(S["lbe_ok"], 1)
            act.wait_ge(S["ld_x"], 16)
            act.wait_ge(S["ld_ctx"], 16)
            for i in range(TT):
                src = xv[:, i, :] if i < CT else x_sb[:, i - CT, :]
                if i:
                    me.wait()
                me.mark(A(ogT[:, 0:2, :], src.rearrange("p (a n) -> p a n", a=2), ACT.Square,
                          accum_out=stat[:, i:i + 1]))
            me.wait()
            act.wait_ge(S["consts"], 4)
            A(rst[:, 0:TT], stat[:, 0:TT], ACT.Sqrt, bias=eps_t[:, :], scale=1.0 / D).then_inc(S["stdev_ok"], 1)
            act.wait_ge(S["modr_ps"], 1)
            for n in (0, 2):
                last = A(mod2[:, n * 512:n * 512 + 512], ps[1 + n][0:2, :], ACT.Copy)
            last.then_inc(S["modr_ok"], 1)
            act.wait_ge(S["modc_ok"], 1)
            for j in range(DK):
                act.wait_ge(S["xT_ps"], 2 * j + 2)
                A(aT_ctx[:, j, :], ps[5 + j % 3][:, 0:CTX], ACT.Identity, bias=modc[:, j, 1:2],
                  scale=G1[:, j, 1:2]).then_inc(S["aT_ctx_ok"], 1)
                act.wait_ge(S["aT_lat_ok"], j + 1)
                A(aT_hi[:, j * LAT:(j + 1) * LAT], a_tmp[:, j, :], ACT.Copy).then_inc(S["ah_ok"], 1)
            act.wait_ge(S["aT_ctx_ok"], DK)
            A(aTc_hi[:, :].rearrange("p (k t) -> p k t", k=DK), aT_ctx, ACT.Copy).then_inc(S["ah_ok"], 1)
            act.wait_ge(S["ld_wv"], 16 * DK)
            for k in range(DK):
                A(wv_hi[:, k * D:(k + 1) * D], w_sq[:, k, :], ACT.Copy).then_inc(S["wvh_ok"], 1)
            def split_hi(h, s):
                act.wait_ge(ld_wh[s], 16 * h + 16)
                if not (isinstance(h, int) and h == 0):
                    act.wait_ge(sec_done[s], h)
                A(wh_hi[s][:, :].rearrange("p (k n) -> p k n", k=DK), wh[:, s], ACT.Copy).then_inc(S["whh_ok"], 1)

            for n in range(0, 2 * TT, 2):
                if n == 2 * CT:
                    act.wait_ge(S["v_ps"], 2 * CT)
                    act.wait_ge(S["wvl_ok"], DK)
                    for s in range(4):
                        split_hi(0, s)
                act.wait_ge(S["v_ps"], n + 1)
                A(xv[:, n // 2, 0:512], ps[n % 4][:, :], ACT.Copy).then_inc(S["v_ev_a"], 1)

            base = me.count
            per_head = 8

            def head(h, prev, split):
                me.base, me.count = base + per_head * h, 0
                act.wait_ge(S["zc_ps"], h + 1)
                if prev is not None:
                    act.wait_ge(S["ew_ok"], h)
                A(sgk[0][:, 0:CTX], ps[2][:, 0:CTX], ACT.Sigmoid)
                A(sgk[1][:, 0:CTX], ps[2][:, CTX:2 * CTX], ACT.Sigmoid).then_inc(S["zc_sig"], 1)
                act.wait_ge(S["zf_ps"], h + 1)
                A(sgk[0][:, CTX:TOK], ps[0][:, :], ACT.Sigmoid).then_inc(S["zf_sig"], 1)
                if split:
                    split_hi(h + 1, 0)
                act.wait_ge(S["zb_ps"], h + 1)
                A(sgk[1][:, CTX:TOK], ps[1][:, :], ACT.Sigmoid).then_inc(S["zb_sig"], 1)
                if prev is not None:
                    evac_koT(h)
                if split:
                    split_hi(h + 1, 1)
                act.wait_ge(S["q_ps"], h + 1)
                if prev is not None:
                    act.wait_ge(S["qs_ok"], h)
                A(sgq, ps[3][:, :], ACT.Sigmoid).then_inc(S["q_sig"], 1)
                if split:
                    split_hi(h + 1, 2)
                act.wait_ge(S["g_ps"], h + 1)
                if prev is not None:
                    act.wait_ge(S["gs_ok"], h)
                A(sgg, ps[0][:, :], ACT.Sigmoid).then_inc(S["g_sig"], 1)
                if split:
                    split_hi(h + 1, 3)
                act.wait_ge(S["hc_ok"], h + 1)
                act.wait_ge(S["zb_sig"], h + 1)
                for d in range(2):
                    A(ko[d], sgk[d], ACT.Ln, bias=hc[:, d:d + 1], scale=hc[:, 2 + d:3 + d]).then_inc(S["lnf_ok"], 1)
                if prev is not None:
                    read_o(h)
                if prev is not None:
                    rms(h)
                for d in range(2):
                    act.wait_ge(S["b_ok"], 2 * h + (d + 1))
                    m1 = me.mark(A(q_in[d][:, CTX:TOK], bc[d][:, CTX:TOK], ACT.Exp))
                    last = bc[d][:, CTX + (CH - 1 if d == 0 else 0):TOK:CH]
                    me.mark(A(ed[:, d, :], last, ACT.Exp))
                    act.wait_ge(S["bm_ok"], 2 * h + (d + 1))
                    m2 = me.mark(A(ke[d], qe[d], ACT.Exp, scale=-1.0))
                    me.wait(m2)
                    A(qe[d], qe[d], ACT.Exp)
                    act.wait_ge(S["bo_ok"], 2 * h + (d + 1))
                    me.wait(m1)
                    me.mark(A(ko[d], ko[d], ACT.Exp))
                    me.wait()
                    act.sem_inc(S["exp_ok"], 1)
                assert me.count == per_head

            def evac_koT(h1):
                act.wait_ge(S["a_ps"], h1)
                A(koT[0][:, CT:TT, :], ps[5][:, :].rearrange("p (i k) -> p i k", i=LT), ACT.Copy)
                A(koT[0][:, 0:CT, :], ps[6][:, 0:CTX].rearrange("p (i k) -> p i k", i=CT), ACT.Copy)
                A(koT[1][:, CT:TT, :], ps[7][:, :].rearrange("p (i k) -> p i k", i=LT), ACT.Copy)
                A(koT[1][:, 0:CT, :], ps[6][:, CTX:2 * CTX].rearrange("p (i k) -> p i k", i=CT),
                  ACT.Copy).then_inc(S["koT_ok"], 1)

            def read_o(h1):
                act.wait_ge(S["o_ps"], h1)
                A(osb, ps[5][:, :], ACT.Copy).then_inc(S["o_ev"], 1)
                A(sq, ps[5][:, :], ACT.Square).then_inc(S["sq_ok"], 1)

            def rms(h1):
                act.wait_ge(S["ss_ps"], h1)
                act.wait_ge(S["sq_ok"], h1)
                A(sq, ps[6][:, :], ACT.Ln, bias=eps_t[:, :], scale=1.0 / P).then_inc(S["rs_ok"], 1)
                act.wait_ge(S["rs_ok"], 2 * h1)
                A(sq, sq, ACT.Exp, scale=-0.5).then_inc(S["rs_ok"], 1)

            act.sem_inc(S["rs_ok"], 1)
            head(0, None, True)
            with act.Fori(1, H - 1) as h:
                head(h, 1, True)
            head(H - 1, 1, False)
            evac_koT(H)
            read_o(H)
            rms(H)

            me.base, me.count = base + per_head * H, 0
            def fT_copy(i):
                act.wait_ge(S["fT_ps"], i + 1)
                A(ogT[:, 0:4, i * P:(i + 1) * P], ps[4][:, :].rearrange("p (k t) -> p k t", k=4),
                  ACT.Copy).then_inc(S["fT_a"], 1)

            for i in range(LT):
                act.wait_ge(S["h_ok"], i + 1)
                if i:
                    me.wait()
                me.mark(A(aT_t[:, 5120:6144], x_sb[:, i, :], ACT.Square, accum_out=stat[:, 8 + i:9 + i]))
                me.wait()
                A(rst[:, 8 + i:9 + i], stat[:, 8 + i:9 + i], ACT.Sqrt, bias=eps_t[:, :],
                  scale=1.0 / D).then_inc(S["stdev2_ok"], 1)
                if i:
                    fT_copy(i - 1)
            fT_copy(LT - 1)
            act.wait_ge(S["e_v_ok"], 1)
            A(ew4, ew4, ACT.Exp).then_inc(S["e_w_ok"], 1)

            act.wait_ge(S["tab_ok"], 1)
            n_blocks = act.value_load(tab_n[0:1, 0:1], min_val=1, max_val=NB_MAX)


            def hi_part(b, j):
                kind, ahead, k = order[j]
                act.wait_ge(ld_w1[k] if kind == "w1" else ld_w2[k], b * 16 + 16 * (1 + ahead))
                for u in range(2):
                    act.wait_ge(S["w_used"], b * UN + (UN + slot_free(j, u)))
                    A(w_hi[slot_of[j, u]][:, :], half_of(j, u), ACT.Copy).then_inc(S["hi_ok"], 1)

            def xth(half, bank):
                for k in whole_k:
                    if k // 4 == half:
                        A(XT[:, k * P:(k + 1) * P], bank[:, (k % 4) * P:(k % 4 + 1) * P], ACT.Copy)
                A(XTh[:, half * 512:half * 512 + 512], bank[:, :], ACT.Copy).then_inc(S["xth_ok"], 1)

            act.sem_inc(S["y_ok"], 1)
            act.sem_inc(S["hi_ok"], split_no[MID, 0])
            act.wait_ge(ld_w1[0], 16)
            for u in range(2):
                A(w_hi[slot_of[MID, u]][:, :], half_of(MID, u), ACT.Copy).then_inc(S["hi_ok"], 1)
            act.wait_ge(S["hi_ok"], split_no[MID, 1] + 1)
            act.sem_inc(S["hi_ok"], NS - split_no[MID, 1] - 1)
            act.wait_ge(S["xt_ps"], 2)
            xth(0, ps[0])
            xth(1, ps[1])
            for j in EARLY:
                act.wait_ge(ld_w1[order[j][2]], 16)
                for u in range(2):
                    for u0 in range(2):
                        if slot_of[j, u] == slot_of[MID, u0]:
                            act.wait_ge(S["w_used"], 2 * MID + u0 + 1)
                    A(w_hi[slot_of[j, u]][:, :], half_of(j, u), ACT.Copy).then_inc(S["hi_ok"], 1)
            with act.Fori(0, n_blocks) as b:
                A(junk[:, :], eps_t[:, :], ACT.Sigmoid)
                for j in range(EARLY[-1] + 1, MID + 1):
                    hi_part(b, j)
                act.wait_ge(S["xt_ps"], b * 2 + 3)
                act.wait_ge(S["w_used"], b * UN + (UN + 2))
                xth(0, ps[0])
                hi_part(b, W1C)
                act.wait_ge(S["z_ps"], b + 1)
                for n in range(2):
                    A(lin[:, n * 512:n * 512 + 512], ps[4 + n][:, :], ACT.Identity,
                      bias=ones[:, 0:1]).then_inc(S["lin_ok"], 1)
                    A(sig[:, n * 512:n * 512 + 512], ps[2 + n][:, :], ACT.Sigmoid,
                      scale=ALPHA).then_inc(S["sig_ok"], 1)
                act.wait_ge(S["xt_ps"], b * 2 + 4)
                xth(1, ps[1])
                hi_part(b, W1C + 1)
                act.wait_ge(S["at_ps"], b + 1)
                for n in range(2):
                    A(aTh[:, n * 512:n * 512 + 512], ps[6 + n][:, :], ACT.Copy).then_inc(S["ath_ok"], 1)
                hi_part(b, W1C + 2)
                hi_part(b, W1C + 3)
                for j in EARLY:
                    hi_part(b + 1, j)
                act.wait_ge(S["w_used"], b * UN + 2 * UN)
                act.wait_ge(S["y_free"], b + 1)
                A(y_sb[:, 0:512], ps[6][:, :], ACT.Copy)
                A(y_sb[:, 512:1024], ps[7][:, :], ACT.Copy).then_inc(S["y_ok"], 1)

            me.base, me.count = base + per_head * H + LT, 0

            def first_choice(i):
                act.wait_ge(gath[i], 16)
                A(ygat[:, i, 0, :], ygat[:, i, 0, :], ACT.Copy, scale=wk[:, i, 0:1]).then_inc(S["y0_ok"], 1)

            first_choice(0)
            for i in range(LT):
                if i + 1 < LT:
                    first_choice(i + 1)
                act.wait_ge(S["fin_sq"], i + 1)
                if i:
                    me.wait()
                me.mark(A(aT_t[:, 5120:6144], x_sb[:, i, :], ACT.Square, accum_out=stat[:, 12 + i:13 + i]))
                me.wait()
                A(rst[:, 12 + i:13 + i], stat[:, 12 + i:13 + i], ACT.Sqrt, bias=eps_t[:, :],
                  scale=1.0 / D).then_inc(S["fin_std"], 1)

        @block.vector
        def _(dve):
            V = nc.vector
            me = Steps(dve, S["dve_s"])
            dve.wait_ge(S["vecs_ps"], 1)
            V.tensor_copy(cols[:, :], ps[0][:, 0:112]).then_inc(S["cols_ok"], 1)
            dve.wait_ge(S["c_sig"], 1)
            dve.wait_ge(S["cols_ok"], 1)
            V.tensor_tensor(csil[:, :, :].rearrange("p k j -> p j k"),
                            cols[:, 0:16].rearrange("p (j k) -> p j k", j=2),
                            sc16[:, :].rearrange("p (j k) -> p j k", j=2), ALU.mult).then_inc(S["csil_ok"], 1)
            lb0 = cols[:, 72:88].rearrange("p (d h) -> p d h", d=2)
            lb1 = cols[:, 88:104].rearrange("p (d h) -> p d h", d=2)
            hd = hcols[:, :, :].rearrange("p h j -> p j h")
            me.link(V.tensor_tensor(hd[:, 0:2], lb0, lb1, ALU.max))
            me.mark(V.tensor_tensor(hd[:, 2:4], lb0, hd[:, 0:2], ALU.subtract))
            me.mark(V.tensor_tensor(hd[:, 4:6], lb1, hd[:, 0:2], ALU.subtract))
            me.wait()
            dve.sem_inc(S["lbx_ok"], 1)
            dve.wait_ge(S["stdev_ok"], 1)
            me.link(V.reciprocal(rst[:, 0:TT], rst[:, 0:TT]))
            for i in range(TT):
                src = xv[:, i, :] if i < CT else x_sb[:, i - CT, :]
                V.tensor_scalar(xv[:, i, :], src, rst[:, i:i + 1], None, ALU.mult).then_inc(S["xn_ok"], 1)
            dve.wait_ge(S["modr_ps"], 1)
            for n in (1, 3):
                last = V.tensor_copy(mod2[:, n * 512:n * 512 + 512], ps[1 + n][0:2, :])
            last.then_inc(S["modr_ok"], 1)
            dve.wait_ge(S["modc_ps"], 1)
            me.link(V.tensor_tensor(modc[:, :, :], ps[0][:, 0:32].rearrange("p (m j) -> p m j", j=2),
                                    cols[:, 16:32].unsqueeze(2).broadcast_to([P, 16, 2]), ALU.add))
            V.scalar_tensor_tensor(G1[:, :, :], modc[:, 8:16, :], 1.0,
                                   cols[:, 64:72].unsqueeze(2).broadcast_to([P, DK, 2]),
                                   ALU.add, ALU.mult).then_inc(S["modc_ok"], 1)
            dve.wait_ge(S["modc_ok"], 1)

            def less_a(j):
                cs = slice(j * LAT, (j + 1) * LAT)
                dve.wait_ge(S["ah_ok"], j + 1)
                V.tensor_tensor(aT_lo[:, cs], a_tmp[:, j, :], aT_hi[:, cs].bitcast(F32),
                                ALU.subtract).then_inc(S["al_ok"], 1)

            for j in range(DK):
                dve.wait_ge(S["xT_ps"], 2 * j + 1)
                V.tensor_scalar(a_tmp[:, j, :], ps[2 + j % 3][:, :], G1[:, j, 0:1], modc[:, j, 0:1],
                                ALU.mult, ALU.add).then_inc(S["aT_lat_ok"], 1)
                if j:
                    less_a(j - 1)
            less_a(DK - 1)
            for k in range(DK):
                dve.wait_ge(S["wvh_ok"], k + 1)
                V.tensor_tensor(wv_lo[:, k * D:(k + 1) * D], w_sq[:, k, :],
                                wv_hi[:, k * D:(k + 1) * D].bitcast(F32), ALU.subtract).then_inc(S["wvl_ok"], 1)
            dve.wait_ge(S["ah_ok"], DK + 1)
            for k in range(DK):
                V.tensor_tensor(aTc_lo[k][:, :], aT_ctx[:, k, :], aTc_hi[:, k * CTX:(k + 1) * CTX].bitcast(F32),
                                ALU.subtract).then_inc(S["al_ok"], 1)
            def split_lo(h, s):
                dve.wait_ge(S["whh_ok"], 4 * h + (s + 1))
                V.tensor_tensor(wh_lo[s][:, :].rearrange("p (k n) -> p k n", k=DK), wh[:, s],
                                wh_hi[s][:, :].bitcast(F32).rearrange("p (k n) -> p k n", k=DK),
                                ALU.subtract).then_inc(S["whl_ok"], 1)

            for n in range(1, 2 * TT, 2):
                if n == 2 * CT + 1:
                    for s in range(4):
                        split_lo(0, s)
                dve.wait_ge(S["v_ps"], n + 1)
                V.tensor_copy(xv[:, n // 2, 512:1024], ps[n % 4][:, :]).then_inc(S["v_ev_d"], 1)
            dve.wait_ge(S["lbe_ok"], 1)
            me.link(V.tensor_tensor(hd[:, 6:8], hd[:, 2:4], hd[:, 4:6], ALU.add))
            me.link(V.reciprocal(hd[:, 6:8], hd[:, 6:8]))
            me.link(V.tensor_tensor(hd[:, 0:2], hd[:, 2:4], hd[:, 6:8], ALU.mult))
            me.mark(V.tensor_scalar(hd[:, 2:4], hd[:, 0:2], -1.0, 1.0, ALU.mult, ALU.add))
            me.mark(V.tensor_scalar(hd[:, 4:6], hd[:, 0:2], 1.0, None, ALU.subtract))
            me.mark(V.tensor_copy(hd[:, 6], cols[:, 104:112]))
            for d in range(2):
                me.mark(V.memset(pm[d], 0.0))
            V.tensor_copy(csb, csil[:, :, 0:1].broadcast_to([P, DK, P])).then_inc(S["csb_ok"], 1)
            me.wait()

            gla = Steps(dve, S["dve_gla"])
            ew = Steps(dve, S["dve_ew"])

            def consume_scores(h1):
                dve.wait_ge(S["a_ps"], h1)
                V.memset(stat[:, 15:16], 0.0)
                for d in range(2):
                    sc = ps[4][:, d * 256:d * 256 + 256].rearrange("p (a t) -> p a t", a=LT)
                    V.copy_predicated(pm[d][0:CH, :, 0:CH], mk[0:CH, d], sc[0:CH])
                    last = V.copy_predicated(pm[d][CH:P, :, CH:P], mk[CH:P, d], sc[CH:P])
                last.then_inc(S["pm_ok"], 1)

            def states(h1):
                gla.base, gla.count = 17 * (h1 - 1), 0
                dve.wait_ge(S["b_ps"], h1)
                for d in range(2):
                    first = 0 if d == 0 else NCH - 1
                    gla.mark(V.tensor_copy(st[d][:, first, :], ps[4][:, d * P:(d + 1) * P]))
                for n in range(NCH - 1):
                    gla.wait()
                    for d in range(2):
                        ci = n if d == 0 else NCH - 1 - n
                        co = ci + 1 if d == 0 else ci - 1
                        bank = (5, 6)[ci % 2] if d == 0 else (7, 2)[ci % 2]
                        gla.mark(V.scalar_tensor_tensor(st[d][:, co, :], st[d][:, ci, :], ed[:, d, ci:ci + 1],
                                                       ps[bank][:, (ci // 2) * P:(ci // 2 + 1) * P],
                                                       ALU.mult, ALU.add))
                gla.wait()
                dve.sem_inc(S["st_ok"], 1)

            def gate(h1, ho):
                g_col = hcols[:, ho, 6:7] if isinstance(ho, int) else hcols[:, bass.ds(ho, 1), 6:7].squeeze(1)
                dve.wait_ge(S["o_ev"], h1)
                dve.wait_ge(S["rs_ok"], 2 * h1 + 1)
                gla.link(V.scalar_tensor_tensor(osb, osb, g_col, sq, ALU.mult, ALU.mult))
                V.tensor_tensor(ogT[:, ho, :], osb, gs, ALU.mult).then_inc(S["og_ok"], 1)

            def decays(h, d):
                dve.wait_ge(S["lnf_ok"], 2 * h + (d + 1))
                ew.mark(V.tensor_scalar(sgk[d], sgk[d], hc[:, 4 + d:5 + d], hc[:, 2 + d:3 + d],
                                        ALU.mult, ALU.add))
                rev = slice(None, None, 1 if d == 0 else -1)
                V.tensor_tensor_scan(bc[d][:, rev], res[:, d, :], ko[d][:, rev], 0.0, ALU.mult,
                                     ALU.add).then_inc(S["b_ok"], 1)
                dve.wait_ge(S["b_ok"], 2 * h + (d + 1))
                bl = bc[d][:, CTX:TOK].rearrange("p (c t) -> p c t", c=NCH)
                iref, ilast = (CH // 2 - 1, CH - 1) if d == 0 else (CH // 2, 0)
                V.tensor_tensor(qe[d].rearrange("p (c t) -> p c t", c=NCH), bl,
                                bl[:, :, iref:iref + 1].broadcast_to([P, NCH, CH]),
                                ALU.subtract).then_inc(S["bm_ok"], 1)
                ew.mark(V.tensor_tensor(ko[d][:, CTX:TOK].rearrange("p (c t) -> p c t", c=NCH),
                                        bl[:, :, ilast:ilast + 1].broadcast_to([P, NCH, CH]), bl,
                                        ALU.subtract))
                il = CTX - 1 if d == 0 else 0
                V.tensor_scalar(ko[d][:, 0:CTX], bc[d][:, 0:CTX], -1.0, bc[d][:, il:il + 1],
                                ALU.mult, ALU.add).then_inc(S["bo_ok"], 1)

            def head(h, prev, split):
                ew.base, ew.count = 6 * h, 0
                V.tensor_copy(hc[:, :], hcols[:, bass.ds(h, 1), :].squeeze(1)).then_inc(S["hc_ok"], 1)
                if split:
                    split_lo(h + 1, 0)
                if prev is not None:
                    consume_scores(h)
                if split:
                    split_lo(h + 1, 1)
                dve.wait_ge(S["q_sig"], h + 1)
                V.tensor_tensor(qs, ps[3][:, :], sgq, ALU.mult).then_inc(S["qs_ok"], 1)
                if prev is not None:
                    states(h)
                dve.wait_ge(S["g_sig"], h + 1)
                V.tensor_tensor(sgg, ps[0][:, :], sgg, ALU.mult).then_inc(S["gm_ok"], 1)
                if split:
                    split_lo(h + 1, 2)
                    split_lo(h + 1, 3)
                dve.wait_ge(S["hc_ok"], h + 1)
                decays(h, 0)
                if prev is not None:
                    dve.wait_ge(S["o_ps"], h)
                V.tensor_copy(v_h, xv[:, :, bass.ds(h * P, P)])
                decays(h, 1)
                if prev is not None:
                    gate(h, prev)
                    dve.wait_ge(S["og_ok"], h)
                dve.wait_ge(S["gm_ok"], h + 1)
                V.tensor_copy(gs, sgg).then_inc(S["gs_ok"], 1)
                for d in range(2):
                    dve.wait_ge(S["exp_ok"], 2 * h + (d + 1))
                    ew.wait()
                    V.tensor_tensor(qe[d], qe[d], qs, ALU.mult)
                    V.tensor_tensor(ke[d], ke[d], sgk[d][:, CTX:TOK], ALU.mult)
                    V.tensor_tensor(q_in[d][:, CTX:TOK], q_in[d][:, CTX:TOK], qs, ALU.mult)
                    ew.mark(V.tensor_tensor(ko[d], ko[d], sgk[d], ALU.mult))
                ew.wait()
                dve.sem_inc(S["ew_ok"], 1)
                assert ew.count == 6

            head(0, None, True)
            with dve.Fori(1, H - 1) as h:
                head(h, h - 1, True)
            head(H - 1, H - 2, False)
            consume_scores(H)
            states(H)
            gate(H, H - 1)

            dve.wait_ge(S["o_ps"], H)
            V.tensor_copy(tri16[:, :], tri[:, :])
            V.tensor_copy(ones16[:, :], ones[:, :])
            dve.wait_ge(S["ld_br"], 16 * 6)
            me.link(V.tensor_copy(bias3[:, :], b_raw))
            for part in range(1, 3):
                r = slice(part * E, (part + 1) * E)
                for _ in range(part):
                    me.link(V.tensor_tensor(b_raw[r], b_raw[r], bias3[r, :], ALU.subtract))
                    me.link(V.tensor_copy(bias3[r, :], b_raw[r]))
            dve.wait_ge(S["mwr_used"], DK)
            dve.wait_ge(S["ld_mb"], 32)
            dve.wait_ge(S["og_ok"], H)
            for n in range(8):
                dst = (g1_row, sh2_row, G2_row, g2_row)[n // 2]
                V.tensor_tensor(dst[:, (n % 2) * 512:(n % 2) * 512 + 512], ps[n][:, :],
                                mb_rows[:, n * 512:(n + 1) * 512], ALU.add).then_inc(S["rows_ev"], 1)
            dve.wait_ge(S["rows_ev"], 8)
            V.scalar_tensor_tensor(G2_row, G2_row, 1.0, n2_row, ALU.add, ALU.mult).then_inc(S["rows_ok"], 1)
            dve.wait_ge(S["rows_ok"], 1)

            def fT_copy(i):
                dve.wait_ge(S["fT_ps"], i + 1)
                V.tensor_copy(ogT[:, 4:8, i * P:(i + 1) * P],
                              ps[5][:, :].rearrange("p (k t) -> p k t", k=4)).then_inc(S["fT_d"], 1)

            dve.wait_ge(S["ld_x"], 32)
            for i in range(LT):
                for n in range(2):
                    j = 2 * i + n
                    dve.wait_ge(S["yo_ps"], j + 1)
                    c0 = slice(n * 512, n * 512 + 512)
                    tmp = xv_t[:, 1024 + j * 512:1536 + j * 512]
                    me.link(V.tensor_tensor(tmp, ps[j % 4][:, :], g1_row[:, c0], ALU.mult))
                    ins = V.tensor_tensor(x_sb[:, i, c0], x_sb[:, i, c0], tmp, ALU.add)
                    if n:
                        ins.then_inc(S["h_ok"], 1)
                    else:
                        me.mark(ins)
                if i:
                    fT_copy(i - 1)
                dve.wait_ge(S["h_ok"], i + 1)
                dve.wait_ge(S["stdev2_ok"], i + 1)
                me.link(V.reciprocal(rst[:, 8 + i:9 + i], rst[:, 8 + i:9 + i]))
                me.link(V.scalar_tensor_tensor(f_sb[:, i, :], x_sb[:, i, :], rst[:, 8 + i:9 + i], G2_row,
                                               ALU.mult, ALU.mult))
                V.tensor_tensor(f_sb[:, i, :], f_sb[:, i, :], sh2_row, ALU.add).then_inc(S["f_ok"], 1)
            dve.wait_ge(S["f_ok"], LT)
            dve.sem_inc(S["arena_free"], 1)
            fT_copy(LT - 1)

            dve.wait_ge(S["lg_ps"], LT)
            dve.wait_ge(S["ld_rw"], 32)
            dve.wait_ge(S["consts"], N_CONST)
            me.link(V.tensor_tensor(lg, ps[6][:, 0:LT * E].rearrange("p (i e) -> p i e", i=LT),
                                    rb_row[:, :].unsqueeze(1).broadcast_to([P, LT, E]), ALU.add))
            for i in range(LT):
                me.mark(V.max(v8[:, i, :], lg[:, i, :]))
            me.wait()
            for i in range(LT):
                me.mark(V.max_index(i8[:, i, :], v8[:, i, :], lg[:, i, :]))
            me.wait()
            me.mark(V.tensor_copy(i8f, i8))
            V.tensor_tensor(ew4, v8[:, :, 0:TOPK], v8[:, :, 0:1].broadcast_to([P, LT, TOPK]),
                            ALU.subtract).then_inc(S["e_v_ok"], 1)
            me.wait()
            for k in range(TOPK):
                me.mark(V.tensor_tensor(oh[:, :, k, :], io_e.unsqueeze(1).broadcast_to([P, LT, E]),
                                        i8f[:, :, k:k + 1].broadcast_to([P, LT, E]), ALU.is_equal))
            me.wait()
            me.link(V.tensor_reduce(msk, oh.rearrange("p i k e -> p i e k"), AX_X, ALU.add))
            V.tensor_copy(msk16[:, :, :], msk).then_inc(S["msk_ok"], 1)
            for k in range(TOPK):
                me.mark(V.tensor_tensor(ohd[:, :, k, :], oh[:, :, k, :],
                                        kf[:, :].rearrange("p (i k) -> p i k", i=LT)[:, :, k:k + 1]
                                        .broadcast_to([P, LT, E]), ALU.mult))
            dve.wait_ge(S["cnt_ps"], 1)
            me.link(V.tensor_copy(cnt, ps[1][:, 0:E]))
            me.link(V.tensor_scalar(nblk, cnt, 0.5, None, ALU.is_gt))
            for n in range(1, LT):
                me.link(V.scalar_tensor_tensor(nblk, cnt, n * P + 0.5, nblk, ALU.is_gt, ALU.add))
            me.link(V.tensor_tensor_scan(cum, onesE, nblk, 0.0, ALU.mult, ALU.add))
            me.link(V.tensor_tensor(io_b, io_b, cum.unsqueeze(1).broadcast_to([P, NBT, E]), ALU.is_ge))
            me.link(V.tensor_reduce(bef[:, :], io_b, AX_X, ALU.add))
            me.link(V.tensor_scalar(bef[:, :], bef[:, :], float(E - 1), None, ALU.min))
            me.mark(V.tensor_copy(tab_e[:, :], bef[0:1, :]))
            me.mark(V.memset(tab_nf[:, :], 1.0))
            me.wait()
            me.mark(V.tensor_tensor(tab_nf[:, 1:NBT], bef[0:1, 1:NBT], bef[0:1, 0:NBT - 1], ALU.not_equal))
            me.mark(V.tensor_copy(tab_n[:, :], cum[0:1, E - 1:E]))
            me.wait()
            me.link(V.tensor_copy(tab_new[:, :], tab_nf[:, :]))
            dve.sem_inc(S["tab_ok"], 1)
            me.mark(V.tensor_reduce(kk[:, :, :], ohd.rearrange("p i k e -> p i e k"), AX_X, ALU.add))
            me.link(V.tensor_tensor(pst, cum, nblk, ALU.subtract))
            me.link(V.tensor_scalar(pst, pst, float(P), None, ALU.mult))
            dve.wait_ge(S["pos_ps"], 1)
            me.link(V.tensor_tensor(dm[:, :, :], ps[2][:, 0:LT * E].rearrange("p (i e) -> p i e", i=LT),
                                    pst.unsqueeze(1).broadcast_to([P, LT, E]), ALU.add))
            me.link(V.scalar_tensor_tensor(dm[:, :, :], dm[:, :, :], 1.0, msk, ALU.add, ALU.mult))
            me.link(V.tensor_scalar(dm[:, :, :], dm[:, :, :], -1.0, None, ALU.add))
            dve.wait_ge(S["e_w_ok"], 1)
            me.link(V.tensor_reduce(es, ew4, AX_X, ALU.add))
            me.link(V.reciprocal(es, es))
            me.link(V.tensor_tensor(wk[:, :, :], ew4, es.unsqueeze(2).broadcast_to([P, LT, TOPK]), ALU.mult))
            n_blocks = dve.value_load(tab_n[0:1, 0:1], min_val=1, max_val=NB_MAX)

            def one_hot(b):
                e = dve.value_load(tab_e[0:1, bass.ds(b, 1)] if not isinstance(b, int) else tab_e[0:1, b:b + 1],
                                   min_val=0, max_val=E - 1)
                for i in range(LT):
                    V.tensor_scalar(pt[:, i, :], slot_io[:, :], dm[:, i, bass.ds(e, 1)], None, ALU.is_equal)
                V.tensor_copy(ids[:, :, 2:3], kk[:, :, bass.ds(e, 1)]).then_inc(S["pt_ok"], 1)
                me.mark(V.tensor_scalar(slot_io[:, :], slot_io[:, :], float(P), None, ALU.add))

            def index():
                col = lambda n: idx_f[:, n:n + 1]
                me.link(V.tensor_copy(idx_f[:, 0:3], ps[0][:, 0:3]))
                me.mark(V.scalar_tensor_tensor(col(3), col(1), float(P), col(0), ALU.mult, ALU.add))
                me.link(V.tensor_scalar(col(4), col(2), 0.0, 8192.0, ALU.is_equal, ALU.mult))
                me.link(V.tensor_tensor(col(3), col(3), col(4), ALU.add))
                me.mark(V.tensor_copy(tok_next[:, :], col(3)))
                me.link(V.tensor_scalar(col(5), col(2), float(LAT), float(-LAT), ALU.mult, ALU.add))
                V.tensor_tensor(row_next[:, :], col(5), col(3), ALU.add).then_inc(S["idx_ok"], 1)

            def lo_part(b, j):
                for u in range(2):
                    dve.wait_ge(S["hi_ok"], b * NS + (NS + split_no[j, u] + 1))
                    V.tensor_tensor(w_lo[slot_of[j, u]][:, :], half_of(j, u),
                                    w_hi[slot_of[j, u]][:, :].bitcast(F32), ALU.subtract).then_inc(S["lo_ok"], 1)

            def less(out, bank, hi, half, done, skip=()):
                ks = [k for k in range(4 * half, 4 * half + 4) if k not in skip]
                step = ks[1] - ks[0]
                assert ks == list(range(ks[0], ks[-1] + 1, step))

                def cols_of(t, k0):
                    return t.rearrange("p (k n) -> p k n", n=P)[:, ks[0] - k0:ks[-1] - k0 + 1:step, :]

                V.tensor_tensor(cols_of(out[:, :], 0), cols_of(bank[:, :], 4 * half),
                                cols_of(hi[:, :].bitcast(F32), 0), ALU.subtract).then_inc(done, 1)

            one_hot(0)
            dve.wait_ge(S["xi_ps"], 1)
            index()
            me.wait()
            one_hot(1)
            dve.wait_ge(S["xi_ps"], 2)
            dve.wait_ge(S["mid_ok"], 1)
            index()
            me.wait()
            one_hot(2)
            dve.sem_inc(S["lo_ok"], split_no[MID, 0])
            lo_part(-1, MID)
            dve.wait_ge(S["lo_ok"], split_no[MID, 1] + 1)
            dve.sem_inc(S["lo_ok"], NS - split_no[MID, 1] - 1)
            for half in range(2):
                dve.wait_ge(S["xth_ok"], half + 1)
                less(XTl, ps[half], XTh, half, S["xtl_ok"], whole_k)
            base2 = me.base + me.count
            n_in = 9
            with dve.Fori(0, n_blocks) as b:
                me.base, me.count = base2 + n_in * b, 0
                lo_part(b, EARLY[0])
                dve.wait_ge(S["w_used"], b * UN + (2 * W1C + 1))
                V.tensor_scalar(sel[:, :], bef[0:96, bass.ds(b, 1)].broadcast_to([96, P]), pmod[0:96, :], None,
                                ALU.is_equal).then_inc(S["sel_ok"], 1)
                for j in range(EARLY[1], MID + 1):
                    lo_part(b, j)
                dve.wait_ge(S["xth_ok"], b * 2 + 3)
                less(XTl, ps[0], XTh, 0, S["xtl_ok"], whole_k)
                for n in range(2):
                    c0 = slice(n * 512, n * 512 + 512)
                    dve.wait_ge(S["lin_ok"], b * 2 + (n + 1))
                    me.link(V.tensor_scalar(act_a[:, c0], lin[:, c0], 1.0 + LIMIT, 1.0 - LIMIT, ALU.min, ALU.max))
                    dve.wait_ge(S["sig_ok"], b * 2 + (n + 1))
                    V.scalar_tensor_tensor(act_a[:, c0], ps[2 + n][:, :], LIMIT, act_a[:, c0], ALU.min,
                                           ALU.mult).then_inc(S["glu_ok"], 1)
                for n in range(2):
                    c0 = slice(n * 512, n * 512 + 512)
                    dve.wait_ge(S["glu_ok"], b * 2 + (n + 1))
                    V.scalar_tensor_tensor(act_a[:, c0], sig[:, c0], SIG_MAX, act_a[:, c0], ALU.min,
                                           ALU.mult).then_inc(S["act_ok"], 1)
                lo_part(b, W1C)
                dve.wait_ge(S["xth_ok"], b * 2 + 4)
                less(XTl, ps[1], XTh, 1, S["xtl_ok"], whole_k)
                lo_part(b, W1C + 1)
                for half in range(2):
                    dve.wait_ge(S["ath_ok"], b * 2 + (half + 1))
                    less(aTl, ps[6 + half], aTh, half, S["atl_ok"])
                dve.wait_ge(S["xi_ps"], b + 3)
                dve.wait_ge(S["mid_ok"], b + 2)
                index()
                lo_part(b, W1C + 2)
                me.wait()
                one_hot(b + 3)
                lo_part(b, W1C + 3)
                assert me.count == n_in, me.count

            me = Steps(dve, S["fin_s"])

            def finish(i):
                dve.wait_ge(S["fin_std"], i + 1)
                me.link(V.reciprocal(rst[:, 12 + i:13 + i], rst[:, 12 + i:13 + i]))
                V.scalar_tensor_tensor(x_sb[:, i, :], x_sb[:, i, :], rst[:, 12 + i:13 + i], fin_row,
                                       ALU.mult, ALU.mult).then_inc(S["fin_ok"], 1)

            for i in range(LT):
                dve.wait_ge(gath[i], 16)
                y0 = ygat[:, i, 0, :]
                dve.wait_ge(S["y0_ok"], i + 1)
                for k in range(1, TOPK):
                    me.link(V.scalar_tensor_tensor(y0, ygat[:, i, k, :], wk[:, i, k:k + 1], y0,
                                                   ALU.mult, ALU.add))
                me.link(V.tensor_tensor(y0, y0, g2_row, ALU.mult))
                V.tensor_tensor(x_sb[:, i, :], x_sb[:, i, :], y0, ALU.add).then_inc(S["fin_sq"], 1)
                if i == 1:
                    dve.wait_ge(S["ld_rows"], 16)
                if i:
                    finish(i - 1)
            finish(LT - 1)

        @block.tensor
        def _(pe):
            mm, tr = nc.tensor.matmul, nc.tensor.transpose
            pe.wait_ge(S["ld_vec"], 16 * 9)
            pe.wait_ge(S["consts"], 4)
            tr(ps[0][:, 0:112], vecs, ident[0:112, 0:112]).then_inc(S["vecs_ps"], 1)
            pe.wait_ge(S["csil_ok"], 1)
            for k in range(DK):
                pe.wait_ge(ld_mw[k], 16)
                for n in range(4):
                    last = mm(ps[1 + n][0:2, :], csil[:, k, :], mwc[:, k, n * 512:(n + 1) * 512],
                              start=(k == 0), stop=(k == DK - 1))
            last.then_inc(S["modr_ps"], 1)
            pe.wait_ge(S["modr_ok"], 2)
            for m in range(16):
                last = tr(ps[0][:, 2 * m:2 * m + 2], mod2[:, m * P:(m + 1) * P], ident[0:2, 0:2])
            last.then_inc(S["modc_ps"], 1)
            pe.wait_ge(S["xn_ok"], TT)
            for j in range(DK):
                for lat in (True, False):
                    if j >= 3:
                        pe.wait_ge(S["aT_lat_ok" if lat else "aT_ctx_ok"], j - 2)
                    bank = ps[(2 if lat else 5) + j % 3]
                    tiles = range(CT, TT) if lat else range(CT)
                    for n, i in enumerate(tiles):
                        last = tr(bank[:, n * P:(n + 1) * P], xv[:, i, j * P:(j + 1) * P], ident[:, :])
                    last.then_inc(S["xT_ps"], 1)
            pe.wait_ge(S["ld_wv"], 16 * DK)
            pe.wait_ge(S["aT_ctx_ok"], DK)

            def two_parts(bank, th, tl, mh, ml, start, stop):
                mm(bank, th, mh, start=start, stop=False)
                mm(bank, th, ml, start=False, stop=False)
                return mm(bank, tl, mh, start=False, stop=stop)

            for n in range(2 * TT):
                if n == 2:
                    pe.wait_ge(S["aT_lat_ok"], DK)
                if n == 2 * CT:
                    pe.wait_ge(S["al_ok"], DK)
                if n >= 4:
                    pe.wait_ge(S["v_ev_a" if n % 2 == 0 else "v_ev_d"], (n - 4) // 2 + 1)
                i = n // 2
                for k in range(DK):
                    if i < CT:
                        last = mm(ps[n % 4][:, :], aT_ctx[:, k, i * P:(i + 1) * P],
                                  w_sq[:, k, (n % 2) * 512:(n % 2) * 512 + 512], start=(k == 0), stop=(k == DK - 1))
                        continue
                    if n == 2 * CT:
                        pe.wait_ge(S["wvl_ok"], k + 1)
                    tc = slice(k * LAT + (i - CT) * P, k * LAT + (i - CT + 1) * P)
                    wc = slice(k * D + (n % 2) * 512, k * D + (n % 2) * 512 + 512)
                    last = two_parts(ps[n % 4][:, :], aT_hi[:, tc], aT_lo[:, tc], wv_hi[:, wc], wv_lo[:, wc],
                                     k == 0, k == DK - 1)
                last.then_inc(S["v_ps"], 1)
            pe.wait_ge(S["v_ev_a"], TT)
            pe.wait_ge(S["v_ev_d"], TT)

            def section(h, s, bank, done):
                pe.wait_ge(S["whl_ok"], 4 * h + (s + 1))
                for k in range(DK):
                    kc, tc = slice(k * P, (k + 1) * P), slice(k * LAT, (k + 1) * LAT)
                    last = two_parts(bank[:, :], wh_hi[s][:, kc], wh_lo[s][:, kc], aT_hi[:, tc], aT_lo[:, tc],
                                     k == 0, k == DK - 1)
                last.then_inc(done, 1)

            def scores(h1):
                pe.wait_ge(S["ew_ok"], h1)
                pe.wait_ge(S["rs_ok"], 2 * h1 - 1)
                for d in range(2):
                    for ch in range(NCH):
                        r = slice((ch % 2) * CH, (ch % 2) * CH + CH)
                        cs = slice(ch * CH, (ch + 1) * CH)
                        col = d * 256 + (ch // 2) * CH
                        mm(ps[4][r, col:col + CH], ke[d][:, cs], qe[d][:, cs], start=True, stop=True)
                for d in range(2):
                    for n in range(LT):
                        tr(ps[5 if d == 0 else 7][:, n * P:(n + 1) * P], ko[d][:, CTX + n * P:CTX + (n + 1) * P],
                           ident[:, :])
                    for n in range(CT):
                        last = tr(ps[6][:, (d * CT + n) * P:(d * CT + n + 1) * P], ko[d][:, n * P:(n + 1) * P],
                                  ident[:, :])
                last.then_inc(S["a_ps"], 1)

            def outer(h1, zc_seen):
                pe.wait_ge(S["koT_ok"], h1)
                pe.wait_ge(S["pm_ok"], h1)
                pe.wait_ge(S["zc_sig"], zc_seen)
                for d in range(2):
                    for i in range(CT):
                        mm(ps[4][:, d * P:(d + 1) * P], koT[d][:, i, :], v_h[:, i, :], start=(i == 0),
                           stop=(i == CT - 1))
                    for ch in range(NCH):
                        if ch == (NCH - 1 if d == 0 else 0):
                            continue
                        r = slice((ch % 2) * CH, (ch % 2) * CH + CH)
                        bank = ps[(5, 6)[ch % 2] if d == 0 else (7, 2)[ch % 2]]
                        last = mm(bank[:, (ch // 2) * P:(ch // 2 + 1) * P], koT[d][r, CT + ch // 2, :],
                                  v_h[r, CT + ch // 2, :], start=True, stop=True)
                last.then_inc(S["b_ps"], 1)

            def outputs(h1):
                pe.wait_ge(S["st_ok"], h1)
                for d in range(2):
                    for n in range(LT):
                        mm(ps[5][:, n * P:(n + 1) * P], v_h[:, CT + n, :], pm[d][:, n, :],
                           start=(d == 0 and n == 0), stop=False, skip_group_check=True)
                for d in range(2):
                    for ch in range(NCH):
                        last = mm(ps[5][:, ch * CH:(ch + 1) * CH], st[d][:, ch, :],
                                  q_in[d][:, CTX + ch * CH:CTX + (ch + 1) * CH], start=False,
                                  stop=(d == 1 and ch == NCH - 1), skip_group_check=True)
                last.then_inc(S["o_ps"], 1)

            def sum_squares(h1):
                pe.wait_ge(S["sq_ok"], h1)
                mm(ps[6][:, :], ones[:, :], sq, start=True, stop=True).then_inc(S["ss_ps"], 1)

            def head(h, prev, pending=False):
                if prev is not None:
                    pe.wait_ge(S["zc_sig"], h)
                for s in range(2):
                    pe.wait_ge(S["whl_ok"], 4 * h + (s + 1))
                    for k in range(DK):
                        kc = slice(k * P, (k + 1) * P)
                        last = two_parts(ps[2][:, s * CTX:(s + 1) * CTX], wh_hi[s][:, kc], wh_lo[s][:, kc],
                                         aTc_hi[:, k * CTX:(k + 1) * CTX], aTc_lo[k][:, :], k == 0, k == DK - 1)
                    if s == 0 and pending:
                        sum_squares(h - 1)
                last.then_inc(S["zc_ps"], 1)
                if prev is not None:
                    pe.wait_ge(S["gm_ok"], h)
                section(h, 0, ps[0], S["zf_ps"])
                if prev is not None:
                    pe.wait_ge(S["zb_sig"], h)
                section(h, 1, ps[1], S["zb_ps"])
                if prev is not None:
                    scores(h)
                if prev is not None:
                    pe.wait_ge(S["qs_ok"], h)
                section(h, 2, ps[3], S["q_ps"])
                if prev is not None:
                    outer(h, h + 1)
                pe.wait_ge(S["zf_sig"], h + 1)
                section(h, 3, ps[0], S["g_ps"])
                if prev is not None:
                    outputs(h)

            pe.wait_ge(S["al_ok"], 2 * DK)
            head(0, None)
            head(1, 1)
            with pe.Fori(2, H) as h:
                head(h, 1, True)
            sum_squares(H - 1)
            pe.wait_ge(S["csb_ok"], 1)
            pe.wait_ge(S["gm_ok"], H)
            pe.wait_ge(S["zb_sig"], H)
            for k in range(DK):
                if k % 4 == 0:
                    pe.wait_ge(ld_mwe[k // 4], 64)
                for n in range(2):
                    last = mm(ps[n][:, :], csb[:, k, :], mwe[k // 4][:, k % 4, n * 512:(n + 1) * 512],
                              start=(k == 0), stop=(k == DK - 1))
            last.then_inc(S["mwe_ps"], 1)
            scores(H)
            outer(H, H)
            outputs(H)
            sum_squares(H)

            pe.wait_ge(S["rs_ok"], 2 * H)
            for k in range(DK):
                pe.wait_ge(ld_mwr[k % 4], 16 * (k // 4 + 1))
                for n in range(2, 8):
                    last = mm(ps[n][:, :], csb[:, k, :], mwr[k % 4][:, (n - 2) * 512:(n - 1) * 512],
                              start=(k == 0), stop=(k == DK - 1))
                last.then_inc(S["mwr_used"], 1)
            def f_transposed(i):
                pe.wait_ge(S["f_ok"], i + 1)
                pe.wait_ge(S["rows_ev"], 8)
                if i:
                    pe.wait_ge(S["fT_a"], i)
                    pe.wait_ge(S["fT_d"], i)
                for k in range(DK):
                    last = tr(ps[4 + k // 4][:, (k % 4) * P:(k % 4 + 1) * P], f_sb[:, i, k * P:(k + 1) * P],
                              ident[:, :])
                last.then_inc(S["fT_ps"], 1)

            def logits(i):
                pe.wait_ge(S["fT_a"], i + 1)
                pe.wait_ge(S["fT_d"], i + 1)
                pe.wait_ge(S["ld_rw"], 32)
                for k in range(DK):
                    last = mm(ps[6][:, i * E:(i + 1) * E], ogT[:, k, i * P:(i + 1) * P], rw[:, k, :],
                              start=(k == 0), stop=(k == DK - 1))
                last.then_inc(S["lg_ps"], 1)

            pe.wait_ge(S["og_ok"], H)
            pe.wait_ge(S["ld_wout"], 16 * DK)
            for i in range(LT):
                for n in range(2):
                    j = 2 * i + n
                    if j < 4:
                        pe.wait_ge(S["rows_ev"], j + 1)
                    else:
                        pe.wait_ge(S["h_ok"], i - 1)
                    for k in range(DK):
                        last = mm(ps[j % 4][:, :], ogT[:, k, i * P:(i + 1) * P], w_sq[:, k, n * 512:(n + 1) * 512],
                                  start=(k == 0), stop=(k == DK - 1))
                    last.then_inc(S["yo_ps"], 1)
                if i >= 2:
                    logits(i - 2)
                if i >= 1:
                    f_transposed(i - 1)
            logits(LT - 2)
            f_transposed(LT - 1)
            logits(LT - 1)
            pe.wait_ge(S["msk_ok"], 1)
            for i in range(LT):
                last = mm(ps[1][:, 0:E], ones16[:, :], msk16[:, i, :], start=(i == 0), stop=(i == LT - 1))
            last.then_inc(S["cnt_ps"], 1)
            for i in range(LT):
                for i0 in range(i + 1):
                    last = mm(ps[2][:, i * E:(i + 1) * E], (tri16 if i0 == i else ones16)[:, :], msk16[:, i0, :],
                              start=(i0 == 0), stop=(i0 == i))
            last.then_inc(S["pos_ps"], 1)

            pe.wait_ge(S["tab_ok"], 1)
            n_blocks = pe.value_load(tab_n[0:1, 0:1], min_val=1, max_val=NB_MAX)

            def slots_of(count):
                pe.wait_ge(S["pt_ok"], count)
                for i in range(LT):
                    last = mm(ps[0][:, 0:P], pt[:, i, :], ids[:, i, :], start=(i == 0), stop=(i == LT - 1))
                last.then_inc(S["xi_ps"], 1)

            def transpose_x(half, count):
                pe.wait_ge(S["xg_ld"], count * 16)
                for k in range(4 * half, 4 * half + 4):
                    last = tr(ps[half][:, (k % 4) * P:(k % 4 + 1) * P], xg[:, k * P:(k + 1) * P], ident[:, :])
                last.then_inc(S["xt_ps"], 1)

            def three(bank, th, tl, k, slot, c0, start, stop):
                kc = slice(k * P, (k + 1) * P)
                return two_parts(bank, th[:, kc], tl[:, kc], w_hi[slot][:, c0], w_lo[slot][:, c0], start, stop)

            def z_chunk(b, j, free=False):
                _, ahead, k = order[j]
                if j in WHOLE:
                    pe.wait_ge(ld_w1[k], b * 16 + 16 * (1 + ahead))
                for u in range(2):
                    if j not in WHOLE:
                        pe.wait_ge(S["lo_ok"], b * NS + (NS + split_no[j, u] + 1))
                    for n in range(2):
                        bank, c0 = ps[4 - 2 * u + n], slice(n * 512, n * 512 + 512)
                        if free:
                            pe.wait_ge(S["glu_ok" if u else "lin_ok"], b * 2 + (n + 1))
                        if j in WHOLE:
                            last = mm(bank[:, :], XT[:, k * P:(k + 1) * P], half_of(j, u)[:, c0], start=(k == 0),
                                      stop=False)
                        else:
                            last = three(bank[:, :], XTh, XTl, k, slot_of[j, u], c0, start=(k == 0), stop=False)
                    last.then_inc(S["w_used"], 1)

            slots_of(1)
            pe.wait_ge(S["idx_ok"], 1)
            slots_of(2)
            pe.wait_ge(S["idx_ok"], 2)
            transpose_x(0, 1)
            transpose_x(1, 1)
            pe.sem_inc(S["w_used"], 2 * MID)
            pe.wait_ge(S["xtl_ok"], 1)
            for j in range(MID, MID + AHEAD):
                z_chunk(-1, j)
            pe.wait_ge(S["w_used"], 2 * (MID + AHEAD))
            pe.sem_inc(S["w_used"], 2 * W2C)
            pe.wait_ge(S["xtl_ok"], 2)
            with pe.Fori(0, n_blocks) as b:
                pe.wait_ge(S["xtl_ok"], b * 2 + 2)
                for j in range(MID):
                    if j == MID - 1:
                        pe.wait_ge(S["idx_ok"], b + 2)
                        transpose_x(0, b + 2)
                    z_chunk(b, j)
                pe.wait_ge(S["sel_ok"], b + 1)
                for n in range(4):
                    last = mm(ps[2 + n][:, :], sel[:, :], bias3[:, n * 512:(n + 1) * 512], start=False, stop=True)
                last.then_inc(S["z_ps"], 1)
                transpose_x(1, b + 2)
                pe.wait_ge(S["xtl_ok"], b * 2 + 3)
                slots_of(b + 3)
                z_chunk(b, MID, free=True)
                z_chunk(b, MID + 1)
                pe.wait_ge(S["act_ok"], b * 2 + 2)
                pe.wait_ge(S["y_ok"], b + 1)
                for k in range(DK):
                    last = tr(ps[6 + k // 4][:, (k % 4) * P:(k % 4 + 1) * P], act_a[:, k * P:(k + 1) * P],
                              ident[:, :])
                last.then_inc(S["at_ps"], 1)
                z_chunk(b, MID + 2)
                pe.wait_ge(S["atl_ok"], b * 2 + 2)
                for n in range(2):
                    mm(ps[6 + n][:, :], sel[:, :], bias3[:, 2 * FF + n * 512:2 * FF + (n + 1) * 512],
                       start=True, stop=False)
                for m in range(W2C):
                    j = W1C + m
                    for a in range(2):
                        pe.wait_ge(S["lo_ok"], b * NS + (NS + split_no[j, a] + 1))
                        for n in range(2):
                            last = three(ps[6 + n][:, :], aTh, aTl, 2 * m + a, slot_of[j, a],
                                         slice(n * 512, n * 512 + 512), start=False,
                                         stop=(m == W2C - 1 and a == 1))
                        last.then_inc(S["w_used"], 1)


INPUTS = ["x", "c", "ctx", "c_ctx", "mod_w", "mod_b", "norm1_g", "norm2_g", "hg_w_in", "hg_lb_logits",
          "hg_norm_g", "hg_w_out", "router_w", "router_b", "moe_w1", "moe_b1", "moe_w2", "moe_b2", "final_g"]
SHAPES = {"x": [LAT, D], "c": [1, D], "ctx": [CTX, D], "mod_w": [D, 6 * D], "mod_b": [6 * D],
          "norm1_g": [D], "norm2_g": [D], "hg_w_in": [D, 5 * D], "hg_norm_g": [D], "hg_w_out": [D, D],
          "router_w": [D, E], "router_b": [E], "moe_w1": [E * D, 2 * FF], "moe_b1": [E, 2 * FF],
          "moe_w2": [E * FF, D], "moe_b2": [E, D]}


def kernel(**inputs):
    import concourse.bacc as bacc
    from concourse.bass_utils import run_bass_kernel_spmd

    nc = bacc.Bacc("TRN2", target_bir_lowering=False, num_devices=1, dynamic_dma_scratch_size=4096)
    arrays, args = {}, []
    for name in INPUTS:
        a = np.ascontiguousarray(inputs[name])
        a = a.reshape(SHAPES.get(name, a.shape))
        arrays[f"in_{name}"] = a
        args.append(nc.dram_tensor(f"in_{name}", a.shape, mybir.dt.from_np(a.dtype), kind="ExternalInput").ap())
    args.append(nc.dram_tensor("out", [LAT, D], F32, kind="ExternalOutput").ap())
    build(nc, *args)
    r = run_bass_kernel_spmd(nc, [arrays], core_ids=[0])
    return r.results[0]["out"].reshape(1, LAT, D)
```
